# Optimizing a Trainium2 kernel written in Bass

```python
import math
import jax, jax.numpy as jnp
from jax import lax
import numpy as np

D_MODEL = 1024
BATCH = 1
SEQ = 512
DEPTH = 2

N_EVEN = (DEPTH + 1) // 2
N_ODD = DEPTH // 2

MEM_LEN = 256
XA_HEADS = 4
XA_HEAD_DIM = D_MODEL // XA_HEADS

POOL_W = D_MODEL // 2
POOL_WINDOWS = (2, 4, 8, 16)
N_POOL_GROUPS = len(POOL_WINDOWS)
POOL_GROUP = POOL_W // N_POOL_GROUPS
CONV_W = D_MODEL // 2
CONV_K = 31

MLA_HEADS = 16
QK_NOPE = 64
QK_ROPE = 32
V_HEAD = 64
Q_LORA = 384
KV_LORA = 256
ROPE_THETA = 10000.0
Q_BLOCK = 128
MLA_SCALE = 1.0 / math.sqrt(QK_NOPE + QK_ROPE)

D_FF = 2816
FFN_CONV_K = 3

EPS = 1e-6
NEG = -1e30


def rmsnorm(x, g):
    xf = x.astype(jnp.float32)
    y = xf * lax.rsqrt(jnp.mean(xf * xf, axis=-1, keepdims=True) + EPS)
    return (y * g.astype(jnp.float32)).astype(x.dtype)

def layernorm(x, g, b):
    xf = x.astype(jnp.float32)
    mu = jnp.mean(xf, axis=-1, keepdims=True)
    xc = xf - mu
    y = xc * lax.rsqrt(jnp.mean(xc * xc, axis=-1, keepdims=True) + EPS)
    return (y * g.astype(jnp.float32) + b.astype(jnp.float32)).astype(x.dtype)

def causal_dwconv(u, w):
    k = w.shape[0]
    return lax.conv_general_dilated(
        u, w[:, None, :], window_strides=(1,), padding=[(k - 1, 0)],
        dimension_numbers=("NWC", "WIO", "NWC"), feature_group_count=u.shape[-1])

def window_mean_minus_self(u, w):
    t = u.shape[1]
    uf = u.astype(jnp.float32)
    cs = jnp.cumsum(uf, axis=1)
    cs_lag = jnp.pad(cs, ((0, 0), (w, 0), (0, 0)))[:, :t]
    cnt = jnp.minimum(jnp.arange(t) + 1, w).astype(jnp.float32)
    return ((cs - cs_lag) / cnt[None, :, None] - uf).astype(u.dtype)

def rope_tables(positions):
    inv = 1.0 / (ROPE_THETA ** (jnp.arange(0, QK_ROPE, 2, dtype=jnp.float32) / QK_ROPE))
    ang = positions.astype(jnp.float32)[..., None] * inv
    return jnp.cos(ang), jnp.sin(ang)

def apply_rope(x, cos, sin):
    half = x.shape[-1] // 2
    c = cos.astype(x.dtype)
    s = sin.astype(x.dtype)
    x1, x2 = x[..., :half], x[..., half:]
    return jnp.concatenate([x1 * c - x2 * s, x1 * s + x2 * c], axis=-1)

def pool_conv_mixer(h, w_in, pool_w, pool_scale, dw_w, dw_b, ln_g, ln_b, w_out):
    b, t, _ = h.shape
    z = h @ w_in
    u, glu_a, glu_b = jnp.split(z, [POOL_W, POOL_W + CONV_W], axis=-1)
    ug = u.reshape(b, t, N_POOL_GROUPS, POOL_GROUP)
    pooled = jnp.stack([window_mean_minus_self(ug[:, :, i], w)
                        for i, w in enumerate(POOL_WINDOWS)], axis=2)
    ya = jnp.einsum("btgc,gcd->btgd", pooled, pool_w).reshape(b, t, POOL_W) * pool_scale
    gl = glu_a * jax.nn.sigmoid(glu_b)
    cv = causal_dwconv(gl, dw_w) + dw_b
    yb = jax.nn.silu(layernorm(cv, ln_g, ln_b))
    return jnp.concatenate([ya, yb], axis=-1) @ w_out

def mla_attention(h, cos, sin, w_dq_dkv, q_norm_g, w_uq, kv_norm_g, w_ukv, w_o):
    b, t, _ = h.shape
    c = h @ w_dq_dkv
    cq, ckv, k_pe = jnp.split(c, [Q_LORA, Q_LORA + KV_LORA], axis=-1)
    q = (rmsnorm(cq, q_norm_g) @ w_uq).reshape(b, t, MLA_HEADS, QK_NOPE + QK_ROPE)
    q_nope = q[..., :QK_NOPE]
    q_pe = apply_rope(q[..., QK_NOPE:], cos[:, :, None, :], sin[:, :, None, :])
    kv = (rmsnorm(ckv, kv_norm_g) @ w_ukv).reshape(b, t, MLA_HEADS, QK_NOPE + V_HEAD)
    k_nope, v = kv[..., :QK_NOPE], kv[..., QK_NOPE:]
    k_pe = apply_rope(k_pe, cos, sin)
    nb = t // Q_BLOCK
    kpos = jnp.arange(t)

    def block(args):
        qn, qp, i = args
        s = (jnp.einsum("bqhd,bkhd->bhqk", qn, k_nope)
             + jnp.einsum("bqhr,bkr->bhqk", qp, k_pe)).astype(jnp.float32) * MLA_SCALE
        qpos = i * Q_BLOCK + jnp.arange(Q_BLOCK)
        s = jnp.where(kpos[None, :] <= qpos[:, None], s, NEG)
        p = jax.nn.softmax(s, axis=-1).astype(v.dtype)
        return jnp.einsum("bhqk,bkhd->bqhd", p, v)

    qn_b = q_nope.reshape(b, nb, Q_BLOCK, MLA_HEADS, QK_NOPE).transpose(1, 0, 2, 3, 4)
    qp_b = q_pe.reshape(b, nb, Q_BLOCK, MLA_HEADS, QK_ROPE).transpose(1, 0, 2, 3, 4)
    o = lax.map(block, (qn_b, qp_b, jnp.arange(nb)))
    o = o.transpose(1, 0, 2, 3, 4).reshape(b, t, MLA_HEADS * V_HEAD)
    return o @ w_o

def memory_cross_attention(h, m, wq, wkv, wo):
    b, t, _ = h.shape
    q = (h @ wq).reshape(b, t, XA_HEADS, XA_HEAD_DIM)
    k, v = jnp.split(m @ wkv, 2, axis=-1)
    k = k.reshape(b, MEM_LEN, XA_HEADS, XA_HEAD_DIM)
    v = v.reshape(b, MEM_LEN, XA_HEADS, XA_HEAD_DIM)
    s = jnp.einsum("bthd,bmhd->bhtm", q, k).astype(jnp.float32) * (XA_HEAD_DIM ** -0.5)
    p = jax.nn.softmax(s, axis=-1).astype(v.dtype)
    o = jnp.einsum("bhtm,bmhd->bthd", p, v).reshape(b, t, D_MODEL)
    return o @ wo

def conv_ffn(h, w_up, conv_w, conv_b, w_down):
    a, g = jnp.split(h @ w_up, 2, axis=-1)
    g = causal_dwconv(g, conv_w) + conv_b
    return (jax.nn.silu(g) * a) @ w_down

def first_inputs(seed: int = 0) -> dict:
    key = jax.random.key(seed)
    ks = iter(jax.random.split(key, 40))
    f32 = jnp.float32

    def dense(shape, fan_in, scale=1.0):
        return jax.random.normal(next(ks), shape, f32) * (scale * fan_in ** -0.5)

    def gain(shape):
        return 1.0 + 0.02 * jax.random.normal(next(ks), shape, f32)

    def bias(shape):
        return 0.01 * jax.random.normal(next(ks), shape, f32)

    out_scale = 0.5
    x = jax.random.normal(next(ks), (BATCH, SEQ, D_MODEL), f32)
    mem = jax.random.normal(next(ks), (BATCH, MEM_LEN, D_MODEL), f32)
    offsets = jax.random.randint(next(ks), (BATCH, 1), 0, 4096, dtype=jnp.int32)
    positions = offsets + jnp.arange(SEQ, dtype=jnp.int32)[None, :]
    return {
        "x": x,
        "mem": mem,
        "positions": positions,
        "norm_mix_g": gain((DEPTH, D_MODEL)),
        "norm_xa_g": gain((DEPTH, D_MODEL)),
        "norm_mem_g": gain((DEPTH, D_MODEL)),
        "xa_wq": dense((DEPTH, D_MODEL, D_MODEL), D_MODEL),
        "xa_wkv": dense((DEPTH, D_MODEL, 2 * D_MODEL), D_MODEL),
        "xa_wo": dense((DEPTH, D_MODEL, D_MODEL), D_MODEL, out_scale),
        "norm_ffn_g": gain((DEPTH, D_MODEL)),
        "ffn_w_up": dense((DEPTH, D_MODEL, 2 * D_FF), D_MODEL),
        "ffn_conv_w": dense((DEPTH, FFN_CONV_K, D_FF), FFN_CONV_K),
        "ffn_conv_b": bias((DEPTH, D_FF)),
        "ffn_w_down": dense((DEPTH, D_FF, D_MODEL), D_FF, out_scale),
        "pc_w_in": dense((N_EVEN, D_MODEL, POOL_W + 2 * CONV_W), D_MODEL),
        "pool_w": dense((N_EVEN, N_POOL_GROUPS, POOL_GROUP, POOL_GROUP), POOL_GROUP),
        "pool_scale": gain((N_EVEN, POOL_W)),
        "conv_dw_w": dense((N_EVEN, CONV_K, CONV_W), CONV_K),
        "conv_dw_b": bias((N_EVEN, CONV_W)),
        "conv_ln_g": gain((N_EVEN, CONV_W)),
        "conv_ln_b": bias((N_EVEN, CONV_W)),
        "pc_w_out": dense((N_EVEN, POOL_W + CONV_W, D_MODEL), POOL_W + CONV_W, out_scale),
        "mla_w_dq_dkv": dense((N_ODD, D_MODEL, Q_LORA + KV_LORA + QK_ROPE), D_MODEL),
        "mla_q_norm_g": gain((N_ODD, Q_LORA)),
        "mla_w_uq": dense((N_ODD, Q_LORA, MLA_HEADS * (QK_NOPE + QK_ROPE)), Q_LORA),
        "mla_kv_norm_g": gain((N_ODD, KV_LORA)),
        "mla_w_ukv": dense((N_ODD, KV_LORA, MLA_HEADS * (QK_NOPE + V_HEAD)), KV_LORA),
        "mla_w_o": dense((N_ODD, MLA_HEADS * V_HEAD, D_MODEL), MLA_HEADS * V_HEAD, out_scale),
        "final_norm_g": gain((D_MODEL,)),
    }

def first_block(x, mem, positions, norm_mix_g, norm_xa_g, norm_mem_g, xa_wq, xa_wkv, xa_wo,
              norm_ffn_g, ffn_w_up, ffn_conv_w, ffn_conv_b, ffn_w_down,
              pc_w_in, pool_w, pool_scale, conv_dw_w, conv_dw_b, conv_ln_g, conv_ln_b, pc_w_out,
              mla_w_dq_dkv, mla_q_norm_g, mla_w_uq, mla_kv_norm_g, mla_w_ukv, mla_w_o,
              final_norm_g):
    cos, sin = rope_tables(positions)
    for l in range(DEPTH):
        h = rmsnorm(x, norm_mix_g[l])
        if l % 2 == 0:
            e = l // 2
            x = x + pool_conv_mixer(h, pc_w_in[e], pool_w[e], pool_scale[e], conv_dw_w[e],
                                    conv_dw_b[e], conv_ln_g[e], conv_ln_b[e], pc_w_out[e])
        else:
            o = l // 2
            x = x + mla_attention(h, cos, sin, mla_w_dq_dkv[o], mla_q_norm_g[o], mla_w_uq[o],
                                  mla_kv_norm_g[o], mla_w_ukv[o], mla_w_o[o])
        x = x + memory_cross_attention(rmsnorm(x, norm_xa_g[l]), rmsnorm(mem, norm_mem_g[l]),
                                       xa_wq[l], xa_wkv[l], xa_wo[l])
        x = x + conv_ffn(rmsnorm(x, norm_ffn_g[l]), ffn_w_up[l], ffn_conv_w[l], ffn_conv_b[l],
                         ffn_w_down[l])
    return rmsnorm(x, final_norm_g)


DEPTH_2 = 1

HEAD_DIM = 64
SB_HEADS = 8
SW_HEADS = 8
SW_KV_HEADS = 2
SB_WIDTH = SB_HEADS * HEAD_DIM
SW_WIDTH = SW_HEADS * HEAD_DIM
SW_KV_WIDTH = SW_KV_HEADS * HEAD_DIM
MIX_WIDTH = SB_WIDTH + SW_WIDTH
WINDOW = 128
BLOCK = 128
RMS_EPS = 1e-6
NEG_INF = -1e30
IN_SPLIT_SIZES = (SB_WIDTH, SB_WIDTH, SB_WIDTH, SB_WIDTH, SW_WIDTH, SW_KV_WIDTH, SW_KV_WIDTH, SW_WIDTH)
IN_WIDTH = 4 * SB_WIDTH + 2 * SW_WIDTH + 2 * SW_KV_WIDTH


def rmsnorm_2(x, g):
    xf = x.astype(jnp.float32)
    y = xf * lax.rsqrt(jnp.mean(xf * xf, axis=-1, keepdims=True) + RMS_EPS)
    return (y * g.astype(jnp.float32)).astype(x.dtype)

def alibi_slopes(n):
    return jnp.asarray([2.0 ** (-8.0 * (h + 1) / n) for h in range(n)], dtype=jnp.float32)

def stick_breaking_attention(q, k, v):
    S, Dh = q.shape[1], q.shape[3]
    scale = Dh ** -0.5
    outs = []
    for start in range(0, S, BLOCK):
        end = start + BLOCK
        qb = q[:, start:end]
        kb = k[:, :end]
        vb = v[:, :end]
        z = jnp.einsum('bqhd,bkhd->bhqk', qb, kb).astype(jnp.float32) * scale
        qpos = start + jnp.arange(BLOCK)[:, None]
        kpos = jnp.arange(end)[None, :]
        causal = kpos < qpos
        log_beta = jax.nn.log_sigmoid(z)
        log_1mb = jnp.where(causal, jax.nn.log_sigmoid(-z), 0.0)
        later = lax.cumsum(log_1mb, axis=3, reverse=True) - log_1mb
        w = jnp.where(causal, jnp.exp(log_beta + later), 0.0)
        outs.append(jnp.einsum('bhqk,bkhd->bqhd', w.astype(v.dtype), vb))
    return jnp.concatenate(outs, axis=1)

def sliding_window_sink_attention(q, k, v, sinks, slopes):
    B, S, H, Dh = q.shape
    Hkv = k.shape[2]
    G = H // Hkv
    nb = S // BLOCK
    qb = q.reshape(B, nb, BLOCK, Hkv, G, Dh)

    def band(t):
        tb = t.reshape(B, nb, BLOCK, Hkv, Dh)
        prev = jnp.pad(tb[:, :-1], ((0, 0), (1, 0), (0, 0), (0, 0), (0, 0)))
        return jnp.concatenate([prev, tb], axis=2)

    kb, vb = band(k), band(v)
    s = jnp.einsum('bnqhgd,bnshd->bhgnqs', qb, kb).astype(jnp.float32) * (Dh ** -0.5)
    r = jnp.arange(BLOCK)[:, None]
    j = jnp.arange(2 * BLOCK)[None, :]
    rel = (BLOCK + r - j)
    kpos = (jnp.arange(nb)[:, None, None] - 1) * BLOCK + j[None]
    valid = (rel >= 0)[None] & (rel < WINDOW)[None] & (kpos >= 0)
    m = slopes.reshape(Hkv, G)[:, :, None, None, None]
    logits = s - m * rel.astype(jnp.float32)
    logits = jnp.where(valid, logits, NEG_INF)
    sink = jnp.broadcast_to(sinks.astype(jnp.float32).reshape(1, Hkv, G, 1, 1, 1),
                            logits.shape[:-1] + (1,))
    p = jax.nn.softmax(jnp.concatenate([logits, sink], axis=-1), axis=-1)[..., :-1]
    o = jnp.einsum('bhgnqs,bnshd->bnqhgd', p.astype(v.dtype), vb)
    return o.reshape(B, S, H, Dh)

def second_inputs(seed: int = 0) -> dict:
    key = jax.random.key(seed)
    ks = jax.random.split(key, 11)
    D = D_MODEL
    x = jax.random.normal(ks[0], (BATCH, SEQ, D), jnp.float32)
    c = jax.random.normal(ks[1], (BATCH, D), jnp.float32)
    w_ada = jax.random.normal(ks[2], (DEPTH_2, D, 3 * D), jnp.float32) * (0.5 * D ** -0.5)
    b_ada = jax.random.normal(ks[3], (DEPTH_2, 3 * D), jnp.float32) * 0.01
    norm_g = 1.0 + 0.01 * jax.random.normal(ks[4], (DEPTH_2, D), jnp.float32)
    w_in = jax.random.normal(ks[5], (DEPTH_2, D, IN_WIDTH), jnp.float32) * (D ** -0.5)
    sinks = jax.random.normal(ks[6], (DEPTH_2, SW_HEADS), jnp.float32) * 0.5
    w_out = jax.random.normal(ks[7], (DEPTH_2, MIX_WIDTH, D), jnp.float32) * (MIX_WIDTH ** -0.5)
    final_g = 1.0 + 0.01 * jax.random.normal(ks[8], (D,), jnp.float32)
    return {"x": x, "c": c, "w_ada": w_ada, "b_ada": b_ada, "norm_g": norm_g,
            "w_in": w_in, "sinks": sinks, "w_out": w_out, "final_g": final_g}

def second_block(x, c, w_ada, b_ada, norm_g, w_in, sinks, w_out, final_g):
    B, S, _ = x.shape
    slopes = alibi_slopes(SW_HEADS)
    offsets = np.cumsum(IN_SPLIT_SIZES)[:-1].tolist()
    cond = jax.nn.silu(c)
    for l in range(DEPTH_2):
        mod = cond @ w_ada[l] + b_ada[l]
        shift, scale, gate = jnp.split(mod, 3, axis=-1)
        h = rmsnorm_2(x, norm_g[l]) * (1.0 + scale[:, None, :]) + shift[:, None, :]
        proj = h @ w_in[l]
        sb_q, sb_k, sb_v, sb_g, sw_q, sw_k, sw_v, sw_g = jnp.split(proj, offsets, axis=-1)
        y_sb = stick_breaking_attention(
            sb_q.reshape(B, S, SB_HEADS, HEAD_DIM),
            sb_k.reshape(B, S, SB_HEADS, HEAD_DIM),
            sb_v.reshape(B, S, SB_HEADS, HEAD_DIM)).reshape(B, S, SB_WIDTH)
        y_sb = y_sb * jax.nn.silu(sb_g)
        y_sw = sliding_window_sink_attention(
            sw_q.reshape(B, S, SW_HEADS, HEAD_DIM),
            sw_k.reshape(B, S, SW_KV_HEADS, HEAD_DIM),
            sw_v.reshape(B, S, SW_KV_HEADS, HEAD_DIM),
            sinks[l], slopes).reshape(B, S, SW_WIDTH)
        y_sw = y_sw * jax.nn.silu(sw_g)
        y = jnp.concatenate([y_sb, y_sw], axis=-1) @ w_out[l]
        x = x + gate[:, None, :] * y
    return rmsnorm_2(x, final_g)


def setup_inputs(seed=0):
    out = dict(first_inputs(seed))
    for name, value in second_inputs(seed + 1).items():
        if name != "x":
            out[name + "_2"] = value
    return out


def reference(
    x, mem, positions, norm_mix_g, norm_xa_g, norm_mem_g, xa_wq, xa_wkv, xa_wo, norm_ffn_g,
    ffn_w_up, ffn_conv_w, ffn_conv_b, ffn_w_down, pc_w_in, pool_w, pool_scale, conv_dw_w,
    conv_dw_b, conv_ln_g, conv_ln_b, pc_w_out, mla_w_dq_dkv, mla_q_norm_g, mla_w_uq,
    mla_kv_norm_g, mla_w_ukv, mla_w_o, final_norm_g, c_2, w_ada_2, b_ada_2, norm_g_2, w_in_2,
    sinks_2, w_out_2, final_g_2,
):
    x = first_block(
        x, mem, positions, norm_mix_g, norm_xa_g, norm_mem_g, xa_wq, xa_wkv, xa_wo, norm_ffn_g,
        ffn_w_up, ffn_conv_w, ffn_conv_b, ffn_w_down, pc_w_in, pool_w, pool_scale, conv_dw_w,
        conv_dw_b, conv_ln_g, conv_ln_b, pc_w_out, mla_w_dq_dkv, mla_q_norm_g, mla_w_uq,
        mla_kv_norm_g, mla_w_ukv, mla_w_o, final_norm_g,
    )
    return second_block(
        x, c_2, w_ada_2, b_ada_2, norm_g_2, w_in_2, sinks_2, w_out_2, final_g_2,
    )


_drawn_inputs = setup_inputs


def setup_inputs(seed=0):
    import zlib

    import numpy as np

    out = dict(_drawn_inputs(seed))
    spreads = {}
    factors = {'norm_mix_g': 7.031,
     'norm_xa_g': 8.0,
     'norm_mem_g': 8.0,
     'norm_ffn_g': 4.887,
     'ffn_conv_b': 8.0,
     'pool_scale': 8.0,
     'conv_dw_b': 8.0,
     'conv_ln_g': 8.0,
     'conv_ln_b': 8.0,
     'mla_q_norm_g': 8.0,
     'mla_kv_norm_g': 8.0,
     'final_norm_g': 2.717,
     'b_ada_2': 8.0,
     'norm_g_2': 8.0,
     'sinks_2': 64.0,
     'final_g_2': 27.961}
    for name, (base, spread) in spreads.items():
        noise = np.random.default_rng([zlib.crc32(name.encode()), seed]).standard_normal(out[name].shape)
        drawn = base * np.exp(spread * noise) if base else spread * noise
        out[name] = __import__('jax').numpy.asarray(drawn.astype(out[name].dtype))
    for name, factor in factors.items():
        out[name] = (out[name] * factor).astype(out[name].dtype)
    return out
```

```python
import concourse.bass as bass
from concourse import mybir
from contextlib import ExitStack

P = 128
D = 1024
T = 512
DT = D // P
MEM = 256
XH = 4
XHD = D // XH
FF = 2816
FT = FF // P
CK = 31
MH = 16
NOPE, ROPE, VD = 64, 32, 64
QL, KVL = 384, 256
QKD = NOPE + ROPE
MLA_SCALE = QKD ** -0.5
SBH = SWH = 8
HD = 64
HSCALE = HD ** -0.5
WINDOWS = (2, 4, 8, 16)
EPS = 1e-6
NEG = -1e30
NB = T // P
SLAB = 2048

STAGES = [("ada", 12), ("pc_in", 6), ("kv0", 8), ("pc_out", 4), ("wq0", 4), ("wo0", 4), ("up0", 22),
          ("down0", 12), ("dq", 3), ("ukv", 2), ("uq", 8), ("mla_o", 4), ("kv1", 8), ("wq1", 4), ("wo1", 4),
          ("up1", 22), ("down1", 12), ("w_in", 13), ("w_out", 4)]
FIRST, COUNT = {}, {}
NSLAB = 0
for _name, _count in STAGES:
    FIRST[_name], COUNT[_name] = NSLAB, _count
    NSLAB += _count

TILES = {"down0": 8, "down1": 8, "ukv": 24}
TILE0 = {}
_t = 0
for _name, _count in STAGES:
    TILE0[_name] = _t
    _t += TILES.get(_name, 2 * _count)

NORMS = [("mem", 8), ("mix0", 8), ("xa0", 8), ("ffn0", 8), ("mix1", 8), ("ckv", 2), ("cq", 3), ("xa1", 8),
         ("ffn1", 8), ("final1", 8), ("second", 8), ("final2", 8)]
NORM0, NORMI, NORMT = {}, {}, {}
_t = 0
for _i, (_name, _count) in enumerate(NORMS):
    NORM0[_name], NORMI[_name], NORMT[_name] = _t, _i, _count
    _t += _count

PROW = {"norm_mix_g": (0, 0), "norm_xa_g": (0, 16), "norm_mem_g": (0, 32), "norm_ffn_g": (0, 48),
        "final_norm_g": (0, 64), "norm_g_2": (0, 72), "final_g_2": (0, 80), "pool_scale": (0, 88),
        "conv_dw_b": (0, 92), "conv_ln_g": (0, 96), "conv_ln_b": (0, 100), "mla_q_norm_g": (0, 104),
        "mla_kv_norm_g": (0, 107), "c_2": (0, 109), "b_ada_2": (1, 0), "ffn_conv_w1": (1, 24),
        "conv_dw_w": (2, 0), "ffn_conv_w0": (3, 0), "ffn_conv_b": (3, 66)}
PROWS = (117, 90, 124, 110)

TWO_PI = 6.283185307179586
PI2_A = 6.28125
PI2_B = 0.0019350051879882812
PI2_C = TWO_PI - PI2_A - PI2_B
ROUNDER = 12582912.0

SPLITS = ["mix0", "xa0", "ffn0", "mix1", "ckv", "cq", "xa1", "ffn1", "second"]
SPLIT0 = {}
_t = 0
for _name in SPLITS:
    SPLIT0[_name] = _t
    _t += NORMT[_name]


def build(nc, ins, out, stop=None):
    f32 = mybir.dt.float32
    f32r = mybir.dt.float32r
    i32 = mybir.dt.int32
    ALU = mybir.AluOpType
    ACT = mybir.ActivationFunctionType
    AX = mybir.AxisListType
    MUL, ADD, SUB, MAX = ALU.mult, ALU.add, ALU.subtract, ALU.max

    ctx = ExitStack()
    with ctx:
        top = [(nc.sbuf_base + 31) // 32 * 32]

        def at(name, shape, offset, dt=f32):
            return nc.alloc_sbuf_tensor_at(name, shape, dt, offset=offset)

        def size(shape):
            n = 4
            for s in shape[1:]:
                n *= s
            return (n + 31) // 32 * 32

        def sb(name, shape, dt=f32):
            here = top[0]
            top[0] += size(shape)
            return at(name, shape, here, dt)

        x = sb("x", [P, DT, T])
        h_hi = sb("h_hi", [P, DT, T], f32r)
        h_lo = sb("h_lo", [P, DT, T], f32r)
        raw = [sb(f"w_raw{i}", [P, SLAB]) for i in range(2)]
        w_hi = [sb(f"w_hi{i}", [P, SLAB], f32r) for i in range(2)]
        w_lo = [sb(f"w_lo{i}", [P, SLAB], f32r) for i in range(2)]
        memn = sb("memn", [P, DT, MEM])
        fb = [sb(f"fb{i}", [P, T]) for i in range(2)]
        sq = [sb(f"sq{i}", [P, T]) for i in range(2)]
        rstd = sb("rstd", [P, T])
        prm = sb("prm", [P, 4, P])
        ident = sb("ident", [P, P])
        ones = sb("ones", [P, P])
        later = sb("later", [P, P])
        relm = sb("relm", [P, 2 * P])
        c_silu = sb("c_silu", [P, DT])
        c_pair = sb("c_pair", [P, DT, 2], f32r)
        mod = sb("mod", [P, 24])
        gs2 = sb("gs2", [P, DT])
        eps = sb("eps", [P, 1])
        inv16 = sb("inv16", [P, 16])
        sinks = sb("sinks", [P, SWH])
        rope_c = sb("rope_const", [P, 2])
        nmax = sb("nmax", [P, 2, NB])
        rsum = sb("rsum", [P, 2, NB])
        rinv = sb("rinv", [P, 2, NB])
        esink = sb("esink", [P, 2, NB])
        arena = top[0]

        def area():
            here = [arena]

            def put(name, shape, dt=f32):
                o = here[0]
                here[0] += size(shape)
                return at(name, shape, o, dt)
            return put, here

        put, _ = area()
        x_nat = put("x_nat", [P, NB, D])
        mem_nat = put("mem_nat", [P, 2, D])
        prow = put("prow", [P, 4, P])
        iota_i = put("iota_i", [P, 2 * P], i32)
        put, here = area()
        glu = put("glu", [P, 4, CK - 1 + T])
        cv = put("cv", [P, 4, T])
        u_pad = put("u_pad", [P, 4, 16 + T])
        pool_a = put("pool_a", [P, 16 + T])
        pool_b = put("pool_b", [P, 16 + T])
        pooled = put("pooled", [P, T])
        pooled_hi = put("pooled_hi", [P, 4, T], f32r)
        pooled_lo = put("pooled_lo", [P, 4, T], f32r)
        pw_raw = put("pw_raw", [P, 4, P])
        pw_hi = put("pw_hi", [P, 4, P], f32r)
        pw_lo = put("pw_lo", [P, 4, P], f32r)
        xa_at = here[0]
        m_hi = put("m_hi", [P, DT, MEM], f32r)
        m_lo = put("m_lo", [P, DT, MEM], f32r)
        kT = put("xa_kT", [P, DT, MEM])
        vN = put("xa_v", [P, 2, D])
        ends = [here[0]]
        put, here = area()
        qT = put("xa_qT", [P, DT, T])
        xp = put("xa_p", [P, 2, NB, MEM])
        xpT = put("xa_pT", [P, 2, 2, T])
        assert here[0] <= xa_at
        put, here = area()
        g_hi = put("g_hi", [P, FT, T], f32r)
        g_lo = put("g_lo", [P, FT, T], f32r)
        ends.append(here[0])
        put, here = area()
        lk = put("mla_k", [P, MH, T])
        lv = put("mla_v", [P, NB, MH * VD])
        lq = put("mla_q", [P, 4, T])
        cq_hi = put("cq_hi", [P, 3, T], f32r)
        cq_lo = put("cq_lo", [P, 3, T], f32r)
        lp_at = here[0]
        lp = put("mla_p", [P, 2, 10 * P])
        lpT = put("mla_pT", [P, 10 * P])
        r_cos = put("rope_cos", [P, T])
        r_sin = put("rope_sin", [P, T])
        ends.append(here[0])
        here[0] = lp_at
        cq_raw = put("cq_raw", [P, 3, T])
        ckv_raw = put("ckv_raw", [P, 2, T])
        kpe_raw = put("kpe_raw", [P, T])
        pos_i = put("pos_i", [P, T], i32)
        assert here[0] <= lp_at + 15 * P * 2 * 4
        here[0] = arena + size([P, MH, T]) + size([P, NB, MH * VD])
        ckv_hi = put("ckv_hi", [P, 2, T], f32r)
        ckv_lo = put("ckv_lo", [P, 2, T], f32r)
        lsh = sq
        put, here = area()
        sq_T = put("sb_q", [P, 4, T])
        sk_T = put("sb_k", [P, 4, T])
        sv_N = put("sb_v", [P, NB, 512])
        sg_T = put("sb_gate", [P, 4, T])
        wq_T = put("sw_q", [P, 4, T])
        wk_T = put("sw_k", [P, 2, T])
        wv_N = put("sw_v", [P, NB, P])
        wg_T = put("sw_gate", [P, 4, T])
        sp_T = put("softplus", [P, NB, T])
        sw_T = put("sb_w", [P, NB, T])
        wp = put("sw_p", [P, 2, NB, 2 * P])
        wpT = put("sw_pT", [P, NB, 2 * P])
        minus = put("minus", [P, P])
        before = put("before", [P, P])
        not_before = put("not_before", [P, P])
        from_here = put("from_here", [P, P])
        ends.append(here[0])
        assert max(ends) <= nc.sbuf_usable_end, (max(ends) - nc.sbuf_usable_end)

        bank = [ctx.enter_context(nc.psum_tensor(f"bank{i}", [P, T], f32)) for i in range(8)]
        stat = bank[7]

        def sem(name):
            return ctx.enter_context(nc.semaphore(name))

        masks_ready = sem("masks_ready")
        iota_ready = sem("iota_ready")
        x_loaded = sem("x_loaded")
        mem_loaded = sem("mem_loaded")
        rows_loaded = sem("rows_loaded")
        small_loaded = sem("small_loaded")
        poolw_loaded = sem("poolw_loaded")
        pre_ready = sem("pre_ready")
        pre_done = sem("pre_done")
        csilu_done = sem("csilu_done")
        chi_done = sem("chi_done")
        cpair_ready = sem("cpair_ready")
        consts_done = sem("consts_done")
        raw_loaded = [sem(f"raw_loaded{i}") for i in range(2)]
        hi_done = sem("hi_done")
        lo_done = sem("lo_done")
        slab_half = sem("slab_half")
        tile_free = sem("tile_free")
        sq_done = sem("sq_done")
        sum_done = sem("sum_done")
        sqrt_done = sem("sqrt_done")
        scaled = sem("scaled")
        split_hi = sem("split_hi")
        split_lo = sem("split_lo")
        memn_done = sem("memn_done")
        mem_scaled = sem("mem_scaled")
        mem_hi = sem("mem_hi")
        mem_lo = sem("mem_lo")
        fin_done = sem("fin_done")
        dve_step = sem("dve_step")
        sig_done = sem("sig_done")
        pads_ready = sem("pads_ready")
        pool_step = sem("pool_step")
        pooled_ready = sem("pooled_ready")
        poolhi_done = sem("poolhi_done")
        poollo_done = sem("poollo_done")
        pwhi_done = sem("pwhi_done")
        pwlo_done = sem("pwlo_done")
        pool_out = sem("pool_out")
        ya_scaled = sem("ya_scaled")
        ya_hi = sem("ya_hi")
        y_lo = sem("y_lo")
        cv_ready = sem("cv_ready")
        conv_step = sem("conv_step")
        cv_summed = sem("cv_summed")
        xc_ready = sem("xc_ready")
        xc_sq = sem("xc_sq")
        xc_summed = sem("xc_summed")
        ln_sqrt = sem("ln_sqrt")
        ln_norm = sem("ln_norm")
        ln_silu = sem("ln_silu")
        yb_hi = sem("yb_hi")
        xs_ready = sem("xs_ready")
        xmax_done = sem("xmax_done")
        xexp_done = sem("xexp_done")
        xp_ready = sem("xp_ready")
        xt_ready = sem("xt_ready")
        xt_done = sem("xt_done")
        xo_ready = sem("xo_ready")
        xo_hi = sem("xo_hi")
        xo_lo = sem("xo_lo")
        tap2 = sem("tap2")
        tap1 = sem("tap1")
        gate_silu = sem("gate_silu")
        g_hi_done = sem("g_hi_done")
        g_lo_done = sem("g_lo_done")
        sin_done = sem("sin_done")
        pos_loaded = sem("pos_loaded")
        angle_ready = sem("angle_ready")
        rope_ready = sem("rope_ready")
        kv_tile = sem("kv_tile")
        q_base = sem("q_base")
        q_ready = sem("q_ready")
        ls_ready = sem("ls_ready")
        lmax_done = sem("lmax_done")
        lexp_done = sem("lexp_done")
        lp_ready = sem("lp_ready")
        lt_ready = sem("lt_ready")
        lt_done = sem("lt_done")
        lo_ready = sem("lo_ready")
        lo_hi = sem("lo_hi")
        lo_lo = sem("lo_lo")
        gate_act = sem("gate_act")
        k_shift = sem("k_shift")
        sb_masks = sem("sb_masks")
        z_ready = sem("z_ready")
        abs_done = sem("abs_done")
        exp_done = sem("exp_done")
        ln_done = sem("ln_done")
        sp_ready = sem("sp_ready")
        c_ready = sem("c_ready")
        w_ready = sem("w_ready")
        so_ready = sem("so_ready")
        so_scaled = sem("so_scaled")
        so_hi = sem("so_hi")
        so_lo = sem("so_lo")
        ws_ready = sem("ws_ready")
        wl_done = sem("wl_done")
        wmax_done = sem("wmax_done")
        wexp_done = sem("wexp_done")
        wp_ready = sem("wp_ready")
        wt_ready = sem("wt_ready")
        wt_done = sem("wt_done")
        wo_ready = sem("wo_ready")
        wo_scaled = sem("wo_scaled")
        wo_hi = sem("wo_hi")
        wo_lo = sem("wo_lo")
        out_tr = sem("out_tr")
        out_copied = sem("out_copied")
        out_copied_a = sem("out_copied_a")
        out_stored = sem("out_stored")

        def wait(eng, s, value):
            if value > 0:
                eng.wait_ge(s, value)

        def hold(eng, s, value):
            if isinstance(value, int):
                wait(eng, s, value)
            else:
                eng.wait_ge(s, value)
                eng.nop(nofuse=True)

        def param(name, i=0):
            j, r = PROW[name]
            return prm[:, j, r + i:r + i + 1]

        def free_before(stage, tile):
            return TILE0[stage] + tile - 3

        LAST = FIRST[stop] + COUNT[stop] if stop else NSLAB

        def tap(layer, k, tile, moved):
            j, r = PROW[f"ffn_conv_w{layer}"]
            return prm[:, j, bass.ds(moved + (r + FT * k + tile), 1)]

        def conv_bias(layer, tile, moved):
            j, r = PROW["ffn_conv_b"]
            return prm[:, j, bass.ds(moved + (r + FT * layer + tile), 1)]

        def finish_early(dve, stage):
            dve.wait_ge(tile_free, TILE0[stage] + 8)
            for t in range(4):
                nc.vector.tensor_copy(x_nat[:, t, :], x[:, 2 * t:2 * t + 2, :].rearrange("p a t -> p (a t)")).then_inc(out_copied, 1)

        LQ_SEQ = [("S", 0, i) for i in range(NB)]
        for _h in range(1, MH + 1):
            if _h < MH:
                LQ_SEQ += [("S", _h, i) for i in range(NB)]
            LQ_SEQ += [("T", _h - 1, j) for j in range(NB)]
        LQ_AT = {u: n for n, u in enumerate(LQ_SEQ)}
        QOFF = [0, P, 3 * P, 6 * P]
        KOFF = [0, 4 * P, 7 * P, 9 * P]
        XA_SEQ, SW_SEQ = [], []
        for _h in range(XH + 1):
            if _h < XH:
                XA_SEQ += [("S", _h, 0), ("S", _h, 1)]
            if _h:
                XA_SEQ += [("T", _h - 1, 0), ("T", _h - 1, 1), ("O", _h - 1, 0), ("O", _h - 1, 1)]
        for _h in range(SWH + 1):
            if _h < SWH:
                SW_SEQ += [("S", _h, 0), ("S", _h, 1)]
            if _h:
                SW_SEQ += [("T", _h - 1, 0), ("T", _h - 1, 1), ("O", _h - 1, 0)]
        XA_AT = {u: n for n, u in enumerate(XA_SEQ)}
        SW_AT = {u: n for n, u in enumerate(SW_SEQ)}

        def norm_source(name, i):
            after = {"xa0": "pc_out", "ffn0": "wo0", "mix1": "down0", "xa1": "mla_o", "ffn1": "wo1",
                     "final1": "down1", "final2": "w_out"}
            if name in after:
                return tile_free, TILE0[after[name]] + i + 1
            if name == "mem":
                return pre_done, 13 + i
            if name == "mix0":
                return pre_done, 5 + i
            if name == "second":
                return fin_done, i + 1
            return tile_free, TILE0["dq"] + i + 1 + (3 if name == "ckv" else 0)

        NORM_SRC = {"mem": (lambda i: memn[:, i, :], MEM, D), "cq": (lambda i: cq_raw[:, i, :], T, QL),
                    "ckv": (lambda i: ckv_raw[:, i, :], T, KVL)}
        for _n in NORM0:
            NORM_SRC.setdefault(_n, (lambda i: x[:, i, :], T, D))
        NORM_DST = {"cq": (cq_hi, cq_lo), "ckv": (ckv_hi, ckv_lo)}
        NORM_GAIN = {"mix0": ("norm_mix_g", 0), "mix1": ("norm_mix_g", 8), "xa0": ("norm_xa_g", 0),
                     "xa1": ("norm_xa_g", 8), "ffn0": ("norm_ffn_g", 0), "ffn1": ("norm_ffn_g", 8),
                     "cq": ("mla_q_norm_g", 0), "ckv": ("mla_kv_norm_g", 0), "final1": ("final_norm_g", 0),
                     "final2": ("final_g_2", 0)}

        def slab_source(n):
            for stage, _ in STAGES:
                if FIRST[stage] <= n < FIRST[stage] + COUNT[stage]:
                    break
            s = n - FIRST[stage]

            def cols(w, start, width, rows=None):
                return w.rearrange("(k p) n -> p k n", p=P)[:, :, start:start + width], w.shape[0] // P, width
            if stage == "ada":
                return cols(ins["w_ada_2"][0], 256 * s, 256)
            if stage == "pc_in":
                return cols(ins["pc_w_in"][0], [1024, 512, 1280, 768, 0, 256][s], 256)
            if stage[:2] == "kv":
                return cols(ins["xa_wkv"][int(stage[2])], 256 * s, 256)
            if stage == "pc_out":
                return cols(ins["pc_w_out"][0], 256 * s, 256)
            if stage[:2] == "wq":
                return cols(ins["xa_wq"][int(stage[2])], 256 * s, 256)
            if stage[:2] == "wo":
                return cols(ins["xa_wo"][int(stage[2])], 256 * s, 256)
            if stage[:2] == "up":
                return cols(ins["ffn_w_up"][int(stage[2])], (s // 2) * 256 + (0 if s % 2 else FF), 256)
            if stage[:4] == "down":
                part = s % 3
                k0, k1 = 8 * part, min(8 * part + 8, FT)
                return cols(ins["ffn_w_down"][int(stage[4])][k0 * P:k1 * P, :], (s // 3) * 256, 256)
            if stage == "dq":
                return cols(ins["mla_w_dq_dkv"][0], 256 * s, 256 if s < 2 else 160)
            if stage == "ukv":
                return cols(ins["mla_w_ukv"][0], 1024 * s, 1024)
            if stage == "uq":
                return cols(ins["mla_w_uq"][0], 192 * s, 192)
            if stage == "mla_o":
                return cols(ins["mla_w_o"][0], 256 * s, 256)
            if stage == "w_in":
                return cols(ins["w_in_2"][0], 256 * s, 256)
            return cols(ins["w_out_2"][0], 256 * s, 256)

        def view(buf, nk, width):
            return buf[:, 0:nk * width].rearrange("p (k n) -> p k n", k=nk)

        block = ctx.enter_context(nc.Block())

        @block.sync
        def _(sp):
            sp.dma_start(x_nat[:, :, :], ins["x"][0].rearrange("(t p) d -> p t d", p=P)).then_inc(x_loaded, 16)
            sp.dma_start(mem_nat[:, :, :], ins["mem"][0].rearrange("(t p) d -> p t d", p=P)).then_inc(mem_loaded, 16)

            def load(n):
                src, nk, width = slab_source(n)
                if n >= 2:
                    sp.wait_ge(lo_done, n - 1)
                sp.dma_start(view(raw[n % 2], nk, width), src).then_inc(raw_loaded[n % 2], 16)

            def load_up(layer):
                n0 = FIRST[f"up{layer}"]
                w = ins["ffn_w_up"][layer].rearrange("(k p) (a s n) -> p a s k n", p=P, a=2, n=256)
                with sp.Fori(0, COUNT[f"up{layer}"] // 2) as it:
                    for u in range(2):
                        hold(sp, lo_done, 2 * it + (n0 + u - 1))
                        src = w[:, 1 - u, bass.ds(it, 1)].rearrange("p s k n -> p (s k) n")
                        sp.dma_start(view(raw[(n0 + u) % 2], 8, 256), src).then_inc(raw_loaded[(n0 + u) % 2], 16)

            n = 0
            while n < NSLAB:
                layer = {FIRST["up0"]: 0, FIRST["up1"]: 1}.get(n)
                if layer is None:
                    load(n)
                    n += 1
                else:
                    load_up(layer)
                    n += COUNT["up0"]
                    if stop == f"up{layer}":
                        break
                if stop and n == FIRST[stop] + COUNT[stop] + (stop[:4] == "down"):
                    break
            for t in range(NB):
                sp.wait_ge(out_copied, t + 1)
                if not stop:
                    sp.wait_ge(out_copied_a, t + 1)
                sp.dma_start(out[0, t * P:(t + 1) * P, :], x_nat[:, t, :]).then_inc(out_stored, 16)
            sp.wait_ge(out_stored, 16 * NB)

        @block.gpsimd
        def _(pool):
            def rows(name, src):
                j, r = PROW[name]
                v = src.rearrange("(r p) -> r p", p=P)
                pool.dma_start(prow[r:r + v.shape[0], j, :], v).then_inc(rows_loaded, 16)

            for name in ("norm_mix_g", "norm_xa_g", "norm_mem_g", "norm_ffn_g"):
                rows(name, ins[name].rearrange("l d -> (l d)"))
            for name in ("final_norm_g", "final_g_2"):
                rows(name, ins[name])
            for name in ("norm_g_2", "pool_scale", "conv_dw_b", "conv_ln_g", "conv_ln_b", "mla_q_norm_g",
                         "mla_kv_norm_g", "c_2", "b_ada_2"):
                rows(name, ins[name].rearrange("l d -> (l d)"))
            rows("ffn_conv_b", ins["ffn_conv_b"].rearrange("l d -> (l d)"))
            rows("conv_dw_w", ins["conv_dw_w"][0].rearrange("k d -> (k d)"))
            rows("ffn_conv_w0", ins["ffn_conv_w"][0].rearrange("k d -> (k d)"))
            rows("ffn_conv_w1", ins["ffn_conv_w"][1].rearrange("k d -> (k d)"))
            pool.dma_start(sinks[:, :], ins["sinks_2"].broadcast_to([P, SWH])).then_inc(small_loaded, 16)
            pool.dma_start(rope_c[64:96, :], ins["rope_const"]).then_inc(small_loaded, 16)
            pool.dma_start(pw_raw[:, :, :], ins["pool_w"][0].rearrange("g c d -> c g d")).then_inc(poolw_loaded, 16)

            nc.gpsimd.memset(ident[:, :], 0.0).then_inc(iota_ready, 1)
            nc.gpsimd.memset(ones[:, :], 1.0).then_inc(masks_ready, 1)
            nc.gpsimd.memset(later[:, :], 0.0).then_inc(iota_ready, 1)
            nc.gpsimd.iota(iota_i[:, :], pattern=[[-1, 2 * P]], base=P, channel_multiplier=1).then_inc(iota_ready, 1)
            pool.wait_ge(iota_ready, 3)
            nc.gpsimd.affine_select(out=ident[:, :], in_=ident[:, :], compare_op=ALU.not_equal, fill=1.0, base=0,
                                    pattern=[[-1, P]], channel_multiplier=1).then_inc(masks_ready, 1)
            nc.gpsimd.affine_select(out=later[:, :], in_=later[:, :], compare_op=ALU.is_ge, fill=NEG, base=0,
                                    pattern=[[-1, P]], channel_multiplier=1).then_inc(masks_ready, 1)
            nc.gpsimd.tensor_copy(relm[:, :], iota_i[:, :]).then_inc(iota_ready, 1)
            pool.wait_ge(iota_ready, 4)
            nc.gpsimd.affine_select(out=relm[:, :], in_=relm[:, :], compare_op=ALU.is_ge, fill=-NEG, base=P,
                                    pattern=[[-1, 2 * P]], channel_multiplier=1).then_inc(iota_ready, 1)
            pool.wait_ge(iota_ready, 5)
            nc.gpsimd.affine_select(out=relm[:, :], in_=relm[:, :], compare_op=ALU.is_gt, fill=-NEG, base=0,
                                    pattern=[[1, 2 * P]], channel_multiplier=-1).then_inc(masks_ready, 1)
            pool.wait_ge(iota_ready, 5)
            nc.gpsimd.iota(iota_i[:, 0:16], pattern=[[1, 16]], base=1, channel_multiplier=0).then_inc(iota_ready, 1)
            pool.wait_ge(iota_ready, 6)
            nc.gpsimd.tensor_copy(inv16[:, :], iota_i[:, 0:16]).then_inc(masks_ready, 1)
            nc.gpsimd.memset(eps[:, :], EPS).then_inc(masks_ready, 1)

            pool.wait_ge(pre_ready, 20)
            nc.gpsimd.memset(glu[:, :, 0:CK - 1], 0.0).then_inc(pads_ready, 1)
            nc.gpsimd.memset(u_pad[:, :, 0:16], 0.0).then_inc(pads_ready, 1)
            pool.wait_ge(pads_ready, 2)
            step = [0]

            def link(ins_):
                step[0] += 1
                ins_.then_inc(pool_step, 1)
                pool.wait_ge(pool_step, step[0])

            pool.wait_ge(consts_done, 1)
            for g, w in enumerate(WINDOWS):
                pool.wait_ge(tile_free, TILE0["pc_in"] + 8 + g + 1)
                wait(pool, pooled_ready, g)
                src, n = u_pad[:, g, :], 1
                bufs = [pool_a, pool_b]
                while n < w:
                    dst = bufs[0]
                    link(nc.gpsimd.tensor_tensor(dst[:, 2 * n - 1:], src[:, 2 * n - 1:], src[:, n - 1:16 + T - n], ADD))
                    src, n = dst, 2 * n
                    bufs.reverse()
                dst = bufs[0]
                link(nc.gpsimd.tensor_scalar(dst[:, 16:], src[:, 16:], 1.0 / w, 1.0, MUL, MUL))
                link(nc.gpsimd.tensor_tensor(dst[:, 16:16 + w], src[:, 16:16 + w], inv16[:, 0:w], MUL))
                wait(pool, poollo_done, g)
                nc.gpsimd.tensor_tensor(pooled[:, :], dst[:, 16:], u_pad[:, g, 16:], SUB).then_inc(pooled_ready, 1)
            if stop and FIRST[stop] < FIRST["mla_o"]:
                return

            pool.wait_ge(tile_free, TILE0["down0"] + 8)
            pool.dma_start(pos_i[64:96, :], ins["positions"].broadcast_to([32, T])).then_inc(pos_loaded, 16)

            for h in range(MH):
                pool.wait_ge(q_base, h + 1)
                q = lq[64:96, h % 4, :]
                link(nc.gpsimd.tensor_tensor(lsh[h % 2][64:96, :], lsh[h % 2][64:96, :], r_sin[64:96, :], MUL))
                link(nc.gpsimd.tensor_tensor(q, q, r_cos[64:96, :], MUL))
                nc.gpsimd.tensor_tensor(q, q, lsh[h % 2][64:96, :], ADD).then_inc(q_ready, 1)
            if stop:
                return

            pool.wait_ge(tile_free, TILE0["down1"] + 8)
            nc.gpsimd.memset(minus[:, :], -1.0).then_inc(sb_masks, 1)
            nc.gpsimd.memset(not_before[:, :], NEG).then_inc(sb_masks, 1)
            pool.wait_ge(sb_masks, 2)
            nc.gpsimd.affine_select(out=before[:, :], in_=ones[:, :], compare_op=ALU.is_gt, fill=0.0, base=0,
                                    pattern=[[1, P]], channel_multiplier=-1).then_inc(sb_masks, 1)
            nc.gpsimd.affine_select(out=from_here[:, :], in_=minus[:, :], compare_op=ALU.is_ge, fill=0.0, base=0,
                                    pattern=[[-1, P]], channel_multiplier=1).then_inc(sb_masks, 1)
            nc.gpsimd.affine_select(out=not_before[:, :], in_=not_before[:, :], compare_op=ALU.is_ge, fill=0.0, base=0,
                                    pattern=[[1, P]], channel_multiplier=-1).then_inc(sb_masks, 1)
            pool.wait_ge(tile_free, TILE0["w_in"] + 21)
            pool.dma_start(wk_T[HD:, 0, :], wk_T[0:HD, 0, :]).then_inc(k_shift, 16)
            pool.dma_start(wk_T[0:HD, 1, :], wk_T[HD:, 1, :]).then_inc(k_shift, 16)

        @block.tensor
        def _(pe):
            def mm(o, w, v, start, stop_, **kw):
                return nc.tensor.matmul(o, w, v, start=start, stop=stop_, **kw)

            def slab_tile(stage, n, tile, o, nk, weights, operand, ready=None, first=True, last=True, k0=0, inc=1,
                          inc_sem=None, shift=0, free=True):
                if free:
                    value = free_before(stage, tile) + shift
                    if not isinstance(shift, int) or value > 0:
                        pe.wait_ge(tile_free, value)
                for k in range(nk):
                    if ready is not None:
                        pe.wait_ge(ready[0], ready[1] + k + 1)
                    wh, wl = weights(k)
                    vh, vl = operand(k0 + k)
                    mm(o, wh, vh, first and k == 0, False)
                    mm(o, wh, vl, False, False)
                    m = mm(o, wl, vh, False, last and k == nk - 1)
                m.then_inc(inc_sem or slab_half, inc)

            def slab(stage, n, tiles, nk, width, operand, N=T, ready=None, part=(0, 2), rows=None, shift=0, step=0):
                pe.wait_ge(lo_done, n + 1 + step)
                wh, wl = view(w_hi[n % 2], nk, width), view(w_lo[n % 2], nk, width)
                for i, (tile, c0, cn) in enumerate(tiles):
                    o = bank[(TILE0[stage] + tile) % 4][0:cn, 0:N]
                    slab_tile(stage, n, tile, o, nk, lambda k: (wh[:, k, c0:c0 + cn], wl[:, k, c0:c0 + cn]), operand,
                              ready=ready if i == 0 else None, shift=shift)

            def h_operand(k):
                return h_hi[:, k, :], h_lo[:, k, :]

            def linear(stage, ready):
                for s in range(COUNT[stage]):
                    slab(stage, FIRST[stage] + s, [(2 * s, 0, P), (2 * s + 1, P, P)], DT, 256, h_operand,
                         ready=ready if s == 0 else None)

            def norm_sums(name):
                _, N, _ = NORM_SRC[name]
                n0, nt = NORM0[name], NORMT[name]
                wait(pe, sqrt_done, NORMI[name])
                for i in range(nt):
                    pe.wait_ge(sq_done, n0 + i + 1)
                    mm(stat[:, 0:N], ones[:, :], sq[(n0 + i) % 2][:, 0:N], i == 0, i == nt - 1).then_inc(sum_done, 1)

            pe.wait_ge(masks_ready, 2)
            pe.wait_ge(rows_loaded, 16 * 19)
            for j, r in enumerate(PROWS):
                nc.tensor.transpose(bank[4 + j][:, 0:r], prow[0:r, j, :], ident[0:r, 0:r]).then_inc(pre_ready, 1)
            for r in range(4, 20):
                src, d, nt = (x_nat, r - 4, NB) if r < 12 else (mem_nat, r - 12, 2)
                if r == 4:
                    pe.wait_ge(x_loaded, 16)
                if r == 12:
                    pe.wait_ge(mem_loaded, 16)
                pe.wait_ge(pre_done, r - 3)
                for t in range(nt):
                    m = nc.tensor.transpose(bank[4 + r % 4][:, t * P:(t + 1) * P], src[:, t, d * P:(d + 1) * P],
                                            ident[:, :])
                m.then_inc(pre_ready, 1)
            pe.wait_ge(pre_done, 20)
            norm_sums("mem")
            norm_sums("mix0")

            pe.wait_ge(cpair_ready, 1)

            def ada(n, step):
                pe.wait_ge(lo_done, n + 1 + step)
                wh, wl = view(w_hi[n % 2], DT, 256), view(w_lo[n % 2], DT, 256)
                for j in range(2):
                    o = bank[(2 * n + j) % 4][:, 0:2]
                    value = 2 * n + j - 3 + 2 * step
                    if not isinstance(step, int) or value > 0:
                        pe.wait_ge(tile_free, value)
                    for k in range(DT):
                        mm(o, wh[:, k, j * P:(j + 1) * P], c_pair[:, k, :], k == 0, False)
                        m = mm(o, wl[:, k, j * P:(j + 1) * P], c_pair[:, k, :], False, k == DT - 1)
                    m.then_inc(slab_half, 1)

            for n in range(4):
                ada(n, 0)
            with pe.Fori(1, 3) as it:
                for u in range(4):
                    ada(u, 4 * it)

            linear("pc_in", (split_lo, SPLIT0["mix0"]))

            def memory(layer):
                stage = f"kv{layer}"

                def m_operand(k):
                    return m_hi[:, k, :], m_lo[:, k, :]
                for s in range(4):
                    slab(stage, FIRST[stage] + s, [(2 * s, 0, P), (2 * s + 1, P, P)], DT, 256, m_operand, N=MEM,
                         ready=(mem_lo, 8 * layer) if s == 0 else None)
                for s in range(4, 8):
                    n = FIRST[stage] + s
                    pe.wait_ge(lo_done, n + 1)
                    wh, wl = view(w_hi[n % 2], DT, 256), view(w_lo[n % 2], DT, 256)
                    for j in range(2):
                        o = bank[(TILE0[stage] + 2 * s + j) % 4][:, 0:256]
                        slab_tile(stage, n, 2 * s + j, o, DT,
                                  lambda k: (m_hi[:, k, j * P:(j + 1) * P], m_lo[:, k, j * P:(j + 1) * P]),
                                  lambda k: (wh[:, k, :], wl[:, k, :]))

            memory(0)
            pe.wait_ge(pwlo_done, 1)
            for g in range(4):
                pe.wait_ge(poollo_done, g + 1)
                wait(pe, ya_scaled, g - 1)
                o = bank[4 + g % 2][:, :]
                mm(o, pw_hi[:, g, :], pooled_hi[:, g, :], True, False)
                mm(o, pw_hi[:, g, :], pooled_lo[:, g, :], False, False)
                mm(o, pw_lo[:, g, :], pooled_hi[:, g, :], False, True).then_inc(pool_out, 1)
            for i in range(4):
                pe.wait_ge(cv_ready, i + 1)
                mm(bank[6][:, :], ones[:, :], cv[:, i, :], i == 0, i == 3).then_inc(cv_summed, 1)
            for i in range(4):
                pe.wait_ge(xc_sq, i + 1)
                mm(stat[:, :], ones[:, :], sq[i % 2][:, :], i == 0, i == 3).then_inc(xc_summed, 1)
            linear("pc_out", (y_lo, 0))

            def cross_attention(layer):
                base = layer

                def place(kind, h, j):
                    r = XA_AT[(kind, h, j)]
                    if r >= 4:
                        k, g, i = XA_SEQ[r - 4]
                        if k == "S":
                            pe.wait_ge(xexp_done, 16 * base + 4 * g + 2 * i + 2)
                        elif k == "T":
                            pe.wait_ge(xt_done, 8 * base + 2 * g + i + 1)
                        else:
                            pe.wait_ge(xo_lo, 8 * base + 2 * g + i + 1)
                    return bank[4 + r % 4]

                for h in range(XH + 1):
                    if h < XH:
                        for i in range(2):
                            o = place("S", h, i)
                            for b in range(2):
                                q0 = (2 * i + b) * P
                                for k in range(2):
                                    m = mm(o[:, b * MEM:(b + 1) * MEM], qT[:, 2 * h + k, q0:q0 + P],
                                           kT[:, 2 * h + k, :], k == 0, k == 1)
                            m.then_inc(xs_ready, 1)
                    if h:
                        g = h - 1
                        for j in range(2):
                            o = place("T", g, j)
                            for t in range(NB):
                                if j == 0:
                                    pe.wait_ge(xp_ready, 16 * base + 4 * g + t + 1)
                                m = nc.tensor.transpose(o[:, t * P:(t + 1) * P], xp[:, g % 2, t, j * P:(j + 1) * P],
                                                        ident[:, :])
                            m.then_inc(xt_ready, 1)
                        for d in range(2):
                            o = place("O", g, d)
                            for j in range(2):
                                pe.wait_ge(xt_done, 8 * base + 2 * g + j + 1)
                                c0 = g * XHD + d * P
                                m = mm(o[:, :], vN[:, j, c0:c0 + P], xpT[:, g % 2, j, :], j == 0, j == 1)
                            m.then_inc(xo_ready, 1)

            def ffn(layer):
                up, down = f"up{layer}", f"down{layer}"
                with pe.Fori(0, COUNT[up] // 2) as it:
                    for u in range(2):
                        slab(up, FIRST[up] + u, [(2 * u, 0, P), (2 * u + 1, P, P)], DT, 256, h_operand,
                             ready=(split_lo, SPLIT0[f"ffn{layer}"]) if u == 0 else None, shift=4 * it, step=2 * it)
                with pe.Fori(0, 2) as it:
                    for s in range(6):
                        n = FIRST[down] + s
                        part, nk = s % 3, (8, 8, 6)[s % 3]
                        pe.wait_ge(lo_done, n + 1 + 6 * it)
                        wh, wl = view(w_hi[n % 2], nk, 256), view(w_lo[n % 2], nk, 256)
                        for j in range(2):
                            tile = 2 * (s // 3) + j
                            slab_tile(down, n, tile, bank[(TILE0[down] + tile) % 4][:, :], nk,
                                      lambda k: (wh[:, k, j * P:(j + 1) * P], wl[:, k, j * P:(j + 1) * P]),
                                      lambda k: (g_hi[:, k, :], g_lo[:, k, :]), k0=8 * part, first=part == 0,
                                      last=part == 2, free=part == 0, shift=4 * it,
                                      ready=(g_lo_done, FT * layer + 8 * part + 2) if j == 0 else None)

            def cross(layer):
                norm_sums(f"xa{layer}")
                if layer:
                    memory(1)
                linear(f"wq{layer}", (split_lo, SPLIT0[f"xa{layer}"]))
                pe.wait_ge(tile_free, TILE0[f"wo{layer}"])
                cross_attention(layer)
                linear(f"wo{layer}", (xo_lo, 8 * layer))
                norm_sums(f"ffn{layer}")
                ffn(layer)

            if stop == "pc_out":
                return
            cross(0)
            if stop in ("wo0", "down0"):
                return

            norm_sums("mix1")
            for s, tiles in enumerate(([(0, 0, P), (1, P, P)], [(2, 0, P), (3, P, P)], [(4, 0, P), (5, 64, 96)])):
                slab("dq", FIRST["dq"] + s, tiles, DT, 256 if s < 2 else 160, h_operand,
                     ready=(split_lo, SPLIT0["mix1"]) if s == 0 else None)
            norm_sums("ckv")
            norm_sums("cq")
            for s in range(2):
                n = FIRST["ukv"] + s
                pe.wait_ge(lo_done, n + 1)
                wh, wl = view(w_hi[n % 2], 2, 1024), view(w_lo[n % 2], 2, 1024)
                for i in range(12):
                    tile = 12 * s + i
                    ready = (split_lo, SPLIT0["ckv"]) if tile == 0 else None
                    last = dict(inc=2) if i == 11 else dict(inc_sem=kv_tile)
                    b = bank[(TILE0["ukv"] + tile) % 4]
                    if i < 8:
                        c0 = i * P
                        slab_tile("ukv", n, tile, b[0:NOPE, :], 2,
                                  lambda k: (wh[:, k, c0:c0 + NOPE], wl[:, k, c0:c0 + NOPE]),
                                  lambda k: (ckv_hi[:, k, :], ckv_lo[:, k, :]), ready=ready, **last)
                    else:
                        t = i - 8
                        vh, vl = (v.rearrange("p k (h c) -> p k h c", c=P)[:, :, :, NOPE:] for v in (wh, wl))
                        slab_tile("ukv", n, tile, b[:, :].rearrange("p (h c) -> p h c", c=VD), 2,
                                  lambda k: (ckv_hi[:, k, t * P:(t + 1) * P], ckv_lo[:, k, t * P:(t + 1) * P]),
                                  lambda k: (vh[:, k], vl[:, k]), **last)

            def queries(pair):
                n = FIRST["uq"] + pair
                pe.wait_ge(lo_done, n + 1)
                wh, wl = view(w_hi[n % 2], 3, 192), view(w_lo[n % 2], 3, 192)
                for j in range(2):
                    slab_tile("uq", n, 2 * pair + j, bank[(TILE0["uq"] + 2 * pair + j) % 4][0:QKD, :], 3,
                              lambda k: (wh[:, k, j * QKD:(j + 1) * QKD], wl[:, k, j * QKD:(j + 1) * QKD]),
                              lambda k: (cq_hi[:, k, :], cq_lo[:, k, :]),
                              ready=(split_lo, SPLIT0["cq"]) if pair + j == 0 else None)

            def lq_place(kind, h, j):
                r = LQ_AT[(kind, h, j)]
                if r >= 3:
                    k, g, i = LQ_SEQ[r - 3]
                    pe.wait_ge(lexp_done if k == "S" else lt_done, 4 * g + i + 1)
                return bank[4 + r % 3]

            def scores(h):
                pe.wait_ge(q_ready, h + 1)
                for i in range(NB):
                    o = lq_place("S", h, i)
                    n = (i + 1) * P
                    mm(o[:, 0:n], lq[0:QKD, h % 4, i * P:(i + 1) * P], lk[0:QKD, h, 0:n], True, False)
                    mm(o[:, i * P:n], ident[:, :], later[:, :], False, True).then_inc(ls_ready, 1)

            def turn(h):
                for j in range(NB):
                    o = lq_place("T", h, j)
                    for i in range(j, NB):
                        if j == 0:
                            pe.wait_ge(lp_ready, 4 * h + i + 1)
                        c0 = QOFF[i] + j * P
                        m = nc.tensor.transpose(o[:, (i - j) * P:(i - j + 1) * P], lp[:, h % 2, c0:c0 + P], ident[:, :])
                    m.then_inc(lt_ready, 1)

            def values(h):
                if h % 2 == 0:
                    wait(pe, lo_lo, h // 2)
                r0 = (h % 2) * VD
                for j in range(NB):
                    pe.wait_ge(lt_done, 4 * h + j + 1)
                    m = mm(stat[r0:r0 + VD, j * P:], lv[:, j, h * VD:(h + 1) * VD], lpT[:, KOFF[j]:KOFF[j] + (NB - j) * P],
                           j == 0, j == NB - 1, skip_group_check=True)
                m.then_inc(lo_ready, 1)

            queries(0)
            pe.wait_ge(tile_free, TILE0["uq"])
            pe.wait_ge(rope_ready, 1)
            for h in range(MH + 1):
                if h < MH:
                    scores(h)
                    if h % 2 == 0 and h // 2 + 1 < MH // 2:
                        queries(h // 2 + 1)
                if h:
                    turn(h - 1)
                    values(h - 1)
            linear("mla_o", (lo_lo, 0))
            if stop == "mla_o":
                return
            cross(1)
            if stop in ("wo1", "down1"):
                return
            norm_sums("final1")
            norm_sums("second")

            for s in range(13):
                n = FIRST["w_in"] + s
                if s in (4, 5):
                    pe.wait_ge(lo_done, n + 1)
                    wh, wl = view(w_hi[n % 2], DT, 256), view(w_lo[n % 2], DT, 256)
                    for j in range(2):
                        tile = 2 * s + j
                        b = bank[(TILE0["w_in"] + tile) % 4]
                        wait(pe, tile_free, free_before("w_in", tile))
                        for half in range(2):
                            t = 2 * j + half
                            for k in range(DT):
                                o, hh, hl = b[:, half * 256:(half + 1) * 256], h_hi[:, k, t * P:(t + 1) * P], h_lo[:, k, t * P:(t + 1) * P]
                                mm(o, hh, wh[:, k, :], k == 0, False)
                                mm(o, hh, wl[:, k, :], False, False)
                                m = mm(o, hl, wh[:, k, :], False, k == DT - 1)
                        m.then_inc(slab_half, 1)
                elif s == 10:
                    pe.wait_ge(lo_done, n + 1)
                    wh, wl = view(w_hi[n % 2], DT, 256), view(w_lo[n % 2], DT, 256)
                    slab_tile("w_in", n, 20, bank[(TILE0["w_in"] + 20) % 4][:, :], DT,
                              lambda k: (wh[:, k, 0:P], wl[:, k, 0:P]), h_operand)
                    b = bank[(TILE0["w_in"] + 21) % 4]
                    wait(pe, tile_free, free_before("w_in", 21))
                    for t in range(NB):
                        for k in range(DT):
                            o, hh, hl = b[:, t * P:(t + 1) * P], h_hi[:, k, t * P:(t + 1) * P], h_lo[:, k, t * P:(t + 1) * P]
                            mm(o, hh, wh[:, k, P:], k == 0, False)
                            mm(o, hh, wl[:, k, P:], False, False)
                            m = mm(o, hl, wh[:, k, P:], False, k == DT - 1)
                    m.then_inc(slab_half, 1)
                else:
                    slab("w_in", n, [(2 * s, 0, P), (2 * s + 1, P, P)], DT, 256, h_operand,
                         ready=(split_lo, SPLIT0["second"]) if s == 0 else None)

            pe.wait_ge(tile_free, TILE0["w_out"])

            pe.wait_ge(sb_masks, 5)

            def logits(h):
                wait(pe, so_scaled, h - 1)
                r0, p = (h % 2) * HD, h // 2
                for j in range(NB - 1, -1, -1):
                    mm(bank[4 * (h % 2) + j][:, 0:(NB - j) * P], sk_T[r0:r0 + HD, p, j * P:(j + 1) * P],
                       sq_T[r0:r0 + HD, p, j * P:], True, True).then_inc(z_ready, 1)

            def sticks(h):
                for j in range(NB - 1, -1, -1):
                    pe.wait_ge(sp_ready, 4 * h + NB - j)
                    o = bank[4 * (h % 2) + j]
                    mm(o[:, 0:P], not_before[:, :], ident[:, :], False, False, skip_group_check=True)
                    for i in range(NB - 1, j, -1):
                        mm(o[:, (i - j) * P:(NB - j) * P], minus[:, :], sp_T[:, i, i * P:], False, False,
                           skip_group_check=True)
                    mm(o[:, 0:(NB - j) * P], from_here[:, :], sp_T[:, j, j * P:], False, True,
                       skip_group_check=True).then_inc(c_ready, 1)

            def stick_values(h):
                r0 = (h % 2) * HD
                o = bank[4 * (h % 2) + 3][r0:r0 + HD, :]
                pe.wait_ge(w_ready, 4 * h + NB)
                for j in range(NB):
                    m = mm(o[:, j * P:], sv_N[:, j, h * HD:(h + 1) * HD], sw_T[:, j, j * P:], j == 0, j == NB - 1)
                m.then_inc(so_ready, 1)

            logits(0)
            for h in range(SBH):
                if h + 1 < SBH:
                    logits(h + 1)
                sticks(h)
                stick_values(h)

            def w_place(kind, h, j):
                r = SW_AT[(kind, h, j)]
                if r >= 4:
                    k, g, i = SW_SEQ[r - 4]
                    if k == "O":
                        pe.wait_ge(wo_scaled, g + 1)
                    else:
                        pe.wait_ge(wl_done if k == "S" else wt_done, (4 if k == "S" else 2) * g + (2 * i + 2 if k == "S" else i + 1))
                return bank[4 + r % 4]

            pe.wait_ge(so_scaled, SBH)
            pe.wait_ge(k_shift, 32)
            for h in range(SWH + 1):
                if h < SWH:
                    r0, p, g = (h % 2) * HD, h // 2, h // 4
                    for i in range(2):
                        o = w_place("S", h, i)
                        for b in range(2):
                            q = 2 * i + b
                            c0 = P if q == 0 else 0
                            m = mm(o[:, b * 2 * P + c0:(b + 1) * 2 * P], wq_T[r0:r0 + HD, p, q * P:(q + 1) * P],
                                   wk_T[r0:r0 + HD, g, (q - 1) * P + c0:(q + 1) * P], True, True)
                        m.then_inc(ws_ready, 1)
                if h:
                    e = h - 1
                    r0, g = (e % 2) * HD, e // 4
                    for b in range(2):
                        o = w_place("T", e, b)
                        pe.wait_ge(wp_ready, 4 * e + 4)
                        for j in (2 * b, 2 * b + 1):
                            for q in (j, j + 1):
                                if q < NB:
                                    c0 = P if q == j else 0
                                    o0 = (j % 2) * 2 * P + (q - j) * P
                                    m = nc.tensor.transpose(o[:, o0:o0 + P], wp[:, e % 2, q, c0:c0 + P], ident[:, :])
                        m.then_inc(wt_ready, 1)
                    o = w_place("O", e, 0)
                    pe.wait_ge(wt_done, 2 * e + 2)
                    for q in range(NB):
                        v = slice(g * HD, (g + 1) * HD)
                        m = mm(o[r0:r0 + HD, q * P:(q + 1) * P], wv_N[:, q, v], wpT[:, q, 0:P], True, q == 0)
                        if q:
                            m = mm(o[r0:r0 + HD, q * P:(q + 1) * P], wv_N[:, q - 1, v], wpT[:, q - 1, P:], False, True)
                    m.then_inc(wo_ready, 1)
            pe.wait_ge(so_lo, SBH)
            pe.wait_ge(wo_lo, SWH)
            for s in range(4):
                slab("w_out", FIRST["w_out"] + s, [(2 * s, 0, P), (2 * s + 1, P, P)], DT, 256, h_operand)
            norm_sums("final2")
            pe.wait_ge(sqrt_done, len(NORMS))
            pe.wait_ge(tile_free, TILE0["w_out"] + 8)
            pe.wait_ge(wo_scaled, SWH)
            for t in range(NB):
                for half in range(2):
                    for d in range(4):
                        if t == 0:
                            pe.wait_ge(fin_done, 9 + 4 * half + d)
                        m = nc.tensor.transpose(bank[2 * t + half][:, d * P:(d + 1) * P],
                                                x[:, 4 * half + d, t * P:(t + 1) * P], ident[:, :])
                    m.then_inc(out_tr, 1)

        @block.scalar
        def _(act):
            def a(o, i, f, **kw):
                return nc.scalar.activation(o, i, f, **kw)

            def split(n, step=0):
                if isinstance(step, int) and n + step >= LAST:
                    return
                hold(act, raw_loaded[n % 2], 16 * (n // 2 + 1) + 8 * step)
                hold(act, slab_half, 2 * (n - 1) + 2 * step)
                a(w_hi[n % 2][:, :], raw[n % 2][:, :], ACT.Copy).then_inc(hi_done, 1)

            def norm_squares(name):
                src, N, width = NORM_SRC[name]
                n0, nt = NORM0[name], NORMT[name]
                for i in range(nt):
                    act.wait_ge(*norm_source(name, i))
                    wait(act, sum_done, n0 + i - 1)
                    a(sq[(n0 + i) % 2][:, 0:N], src(i), ACT.Square).then_inc(sq_done, 1)
                act.wait_ge(sum_done, n0 + nt)
                if name in SPLIT0:
                    wait(act, scaled, SPLIT0[name])
                if name == "mix0":
                    act.wait_ge(memn_done, 8)
                a(rstd[:, 0:N], stat[:, 0:N], ACT.Sqrt, scale=1.0 / width, bias=eps[:, :]).then_inc(sqrt_done, 1)

            def norm_hi(name):
                dst = NORM_DST.get(name, (h_hi, h_lo))[0]
                n0 = SPLIT0[name]
                for i in range(NORMT[name]):
                    act.wait_ge(scaled, n0 + i + 1)
                    a(dst[:, i, :], fb[i % 2][:, :], ACT.Copy).then_inc(split_hi, 1)

            def memory_hi(layer):
                for i in range(8):
                    act.wait_ge(mem_scaled, 8 * layer + i + 1)
                    a(m_hi[:, i, :], fb[i % 2][:, 0:MEM], ACT.Copy).then_inc(mem_hi, 1)

            def splits(stage):
                for s in range(COUNT[stage]):
                    split(FIRST[stage] + s + 1)

            act.wait_ge(pre_done, 1)
            c0 = PROW["c_2"][1]
            a(c_silu[:, :], prm[:, 0, c0:c0 + DT], ACT.Silu).then_inc(csilu_done, 1)
            act.wait_ge(csilu_done, 1)
            a(c_pair[:, :, 0], c_silu[:, :], ACT.Copy).then_inc(chi_done, 1)
            act.wait_ge(masks_ready, 6)
            norm_squares("mem")
            norm_squares("mix0")
            norm_hi("mix0")
            memory_hi(0)
            act.wait_ge(poolw_loaded, 16)
            a(pw_hi[:, :, :], pw_raw[:, :, :], ACT.Copy).then_inc(pwhi_done, 1)
            split(0)
            for n in range(4):
                split(n + 1)
            with act.Fori(1, 3) as it:
                for u in range(4):
                    split(u + 1, 4 * it)

            for s in range(6):
                n = FIRST["pc_in"] + s
                split(n + 1)
                if s in (0, 2):
                    for j in range(2):
                        act.wait_ge(slab_half, 2 * n + 1 + j)
                        if s:
                            act.wait_ge(tile_free, TILE0["pc_in"] + 4)
                        b = bank[(TILE0["pc_in"] + 2 * s + j) % 4]
                        a(sq[j][:, :], b[:, :], ACT.Sigmoid).then_inc(sig_done, 1)
            for s in range(8):
                split(FIRST["kv0"] + s + 1)
                if s % 2:
                    act.wait_ge(pooled_ready, s // 2 + 1)
                    a(pooled_hi[:, s // 2, :], pooled[:, :], ACT.Copy).then_inc(poolhi_done, 1)
            for g in range(4):
                act.wait_ge(ya_scaled, g + 1)
                a(h_hi[:, g, :], fb[g % 2][:, :], ACT.Copy).then_inc(ya_hi, 1)
            for i in range(4):
                act.wait_ge(xc_ready, i + 1)
                wait(act, xc_summed, i - 1)
                a(sq[i % 2][:, :], cv[:, i, :], ACT.Square).then_inc(xc_sq, 1)
            act.wait_ge(xc_summed, 4)
            a(rstd[:, :], stat[:, :], ACT.Sqrt, scale=1.0 / (4 * P), bias=eps[:, :]).then_inc(ln_sqrt, 1)
            for i in range(4):
                act.wait_ge(ln_norm, i + 1)
                a(cv[:, i, :], cv[:, i, :], ACT.Silu, scale=param("conv_ln_g", i),
                  bias=param("conv_ln_b", i)).then_inc(ln_silu, 1)
                act.wait_ge(ln_silu, i + 1)
                a(h_hi[:, 4 + i, :], cv[:, i, :], ACT.Copy).then_inc(yb_hi, 1)
            splits("pc_out")

            def cross(layer):
                norm_squares(f"xa{layer}")
                norm_hi(f"xa{layer}")
                if layer:
                    memory_hi(1)
                    splits("kv1")
                splits(f"wq{layer}")
                for h in range(XH + 1):
                    if h < XH:
                        for t in range(NB):
                            act.wait_ge(xmax_done, 2 * XH * layer + 2 * h + t // 2 + 1)
                            if h >= 2:
                                act.wait_ge(xt_ready, 8 * layer + 2 * (h - 1))
                            b = bank[4 + XA_AT[("S", h, t // 2)] % 4]
                            a(xp[:, h % 2, t, :], b[:, (t % 2) * MEM:(t % 2 + 1) * MEM], ACT.Exp,
                              bias=nmax[:, h % 2, t:t + 1], accum_out=rsum[:, h % 2, t:t + 1]).then_inc(xexp_done, 1)
                    if h:
                        for d in range(2):
                            act.wait_ge(xo_ready, 8 * layer + 2 * (h - 1) + d + 1)
                            b = bank[4 + XA_AT[("O", h - 1, d)] % 4]
                            a(h_hi[:, 2 * (h - 1) + d, :], b[:, :], ACT.Copy).then_inc(xo_hi, 1)
                splits(f"wo{layer}")
                norm_squares(f"ffn{layer}")
                norm_hi(f"ffn{layer}")
                up, down = f"up{layer}", f"down{layer}"
                if stop == f"wo{layer}":
                    return
                n, tile = FIRST[up], TILE0[up]
                with act.Fori(0, COUNT[up] // 2) as it:
                    split(n + 1, 2 * it)
                    for j in range(2):
                        hold(act, slab_half, 4 * it + (2 * n + 1 + j))
                        hold(act, g_lo_done, 2 * it + (FT * layer + j + 1))
                        a(fb[j][:, :], bank[(tile + j) % 4][:, :], ACT.Identity, scale=tap(layer, 2, j, 2 * it),
                          bias=conv_bias(layer, j, 2 * it)).then_inc(tap2, 1)
                    for j in range(2):
                        hold(act, tile_free, 4 * it + (tile + j + 1))
                        a(fb[j][:, :], fb[j][:, :], ACT.Silu).then_inc(gate_silu, 1)
                    split(n + 2, 2 * it)
                    for j in range(2):
                        hold(act, tile_free, 4 * it + (tile + 2 + j + 1))
                        a(g_hi[:, bass.ds(2 * it + j, 1), :].rearrange("p a t -> p (a t)"), fb[j][:, :],
                          ACT.Copy).then_inc(g_hi_done, 1)
                n = FIRST[down]
                with act.Fori(0, 2) as it:
                    for s in range(6):
                        split(n + s + 1, 6 * it)

            if stop == "pc_out":
                return
            cross(0)
            if stop in ("wo0", "down0"):
                return
            norm_squares("mix1")
            norm_hi("mix1")
            splits("dq")
            for i, (o, v) in enumerate(((r_sin, r_sin), (r_cos, r_cos))):
                act.wait_ge(angle_ready, i + 1)
                a(o[64:96, :], v[64:96, :], ACT.Sin).then_inc(sin_done, 1)
            norm_squares("ckv")
            norm_hi("ckv")
            norm_squares("cq")
            norm_hi("cq")
            splits("ukv")
            split(FIRST["uq"] + 1)
            for h in range(MH + 1):
                if h < MH:
                    for i in range(NB):
                        act.wait_ge(lmax_done, 4 * h + i + 1)
                        if h >= 2:
                            act.wait_ge(lt_ready, 4 * (h - 1))
                        b = bank[4 + LQ_AT[("S", h, i)] % 3]
                        n = (i + 1) * P
                        a(lp[:, h % 2, QOFF[i]:QOFF[i] + n], b[:, 0:n], ACT.Exp, bias=nmax[:, h % 2, i:i + 1],
                          accum_out=rsum[:, h % 2, i:i + 1]).then_inc(lexp_done, 1)
                    if h % 2 == 0 and h // 2 + 2 <= MH // 2:
                        split(FIRST["uq"] + h // 2 + 2)
                if h and h % 2 == 0:
                    act.wait_ge(lo_ready, h)
                    a(h_hi[:, h // 2 - 1, :], stat[:, :], ACT.Copy).then_inc(lo_hi, 1)
            splits("mla_o")
            if stop == "mla_o":
                return
            cross(1)
            if stop in ("wo1", "down1"):
                return
            norm_squares("final1")
            norm_squares("second")
            norm_hi("second")
            for s in range(13):
                n = FIRST["w_in"] + s
                split(n + 1)
                if s in (6, 7, 11, 12):
                    for j in range(2):
                        act.wait_ge(tile_free, TILE0["w_in"] + 2 * s + j + 1)
                        g = (sg_T if s < 8 else wg_T)[:, 2 * ((s - 6) if s < 8 else (s - 11)) + j, :]
                        a(g, g, ACT.Silu).then_inc(gate_act, 1)
            chain = [0]
            for h in range(SBH):
                for j in range(NB - 1, -1, -1):
                    act.wait_ge(z_ready, 4 * h + NB - j)
                    wait(act, c_ready, 4 * h)
                    a(sp_T[:, j, j * P:], bank[4 * (h % 2) + j][:, 0:(NB - j) * P], ACT.Abs).then_inc(abs_done, 1)
                for j in range(NB - 1, -1, -1):
                    act.wait_ge(abs_done, 4 * h + NB - j)
                    v = sp_T[:, j, j * P:]
                    a(v, v, ACT.Exp, scale=-1.0).then_inc(exp_done, 1)
                for j in range(NB - 1, -1, -1):
                    act.wait_ge(exp_done, 4 * h + NB - j)
                    v = sp_T[:, j, j * P:]
                    a(v, v, ACT.Ln, bias=ones[:, 0:1]).then_inc(ln_done, 1)
                for j in range(NB - 1, -1, -1):
                    act.wait_ge(c_ready, 4 * h + NB - j)
                    wait(act, so_ready, h)
                    a(sw_T[:, j, j * P:], bank[4 * (h % 2) + j][:, 0:(NB - j) * P], ACT.Exp).then_inc(w_ready, 1)
                act.wait_ge(so_scaled, h + 1)
                r0 = (h % 2) * HD
                a(h_hi[r0:r0 + HD, h // 2, :], fb[h % 2][r0:r0 + HD, :], ACT.Copy).then_inc(so_hi, 1)
            for h in range(SWH + 1):
                if h < SWH:
                    act.wait_ge(wmax_done, h + 1)
                    for q in range(NB):
                        c0 = P if q == 0 else 0
                        v = wp[:, h % 2, q, c0:]
                        a(v, v, ACT.Exp, bias=nmax[:, h % 2, q:q + 1],
                          accum_out=rsum[:, h % 2, q:q + 1]).then_inc(wexp_done, 1)
                    a(esink[:, h % 2, :], nmax[:, h % 2, :], ACT.Exp, bias=sinks[:, h:h + 1]).then_inc(wexp_done, 1)
                if h:
                    e = h - 1
                    r0 = (e % 2) * HD
                    act.wait_ge(wo_scaled, e + 1)
                    a(h_hi[r0:r0 + HD, 4 + e // 2, :], fb[e % 2][r0:r0 + HD, :], ACT.Copy).then_inc(wo_hi, 1)
            splits("w_out")
            norm_squares("final2")
            for t in range(NB):
                act.wait_ge(out_tr, 2 * t + 1)
                a(x_nat[:, t, 0:512], bank[2 * t][:, :], ACT.Copy).then_inc(out_copied_a, 1)

        @block.vector
        def _(dve):
            tt, ts, stt, cp = nc.vector.tensor_tensor, nc.vector.tensor_scalar, nc.vector.scalar_tensor_tensor, \
                nc.vector.tensor_copy
            step = [0]

            def link(ins_):
                step[0] += 1
                ins_.then_inc(dve_step, 1)
                dve.wait_ge(dve_step, step[0])

            def low(lo_, v, hi):
                return tt(lo_, v, hi.bitcast(f32), SUB)

            def split(n, step_=0):
                if isinstance(step_, int) and n + step_ >= LAST:
                    return
                dve.wait_ge(hi_done, n + 1 + step_)
                low(w_lo[n % 2][:, :], raw[n % 2][:, :], w_hi[n % 2][:, :]).then_inc(lo_done, 1)

            def splits(stage):
                for s in range(COUNT[stage]):
                    split(FIRST[stage] + s + 1)

            def root(name):
                dve.wait_ge(sqrt_done, NORMI[name] + 1)
                N = NORM_SRC[name][1]
                link(nc.vector.reciprocal(rstd[:, 0:N], rstd[:, 0:N]))

            def norm_apply(name):
                root(name)
                src, N, _ = NORM_SRC[name]
                n0, nt = SPLIT0[name], NORMT[name]
                hi, lo_ = NORM_DST.get(name, (h_hi, h_lo))
                for i in range(nt + 1):
                    if i < nt:
                        wait(dve, split_lo, n0 + max(i - 1, 0))
                        if name == "second":
                            link(stt(fb[i % 2][:, :], src(i), gs2[:, i:i + 1], rstd[:, :], MUL, MUL))
                            ts(fb[i % 2][:, :], fb[i % 2][:, :], mod[:, i:i + 1], None, ADD).then_inc(scaled, 1)
                        else:
                            g, o = NORM_GAIN[name]
                            stt(fb[i % 2][:, :], src(i), param(g, o + i), rstd[:, :], MUL, MUL).then_inc(scaled, 1)
                    if i:
                        dve.wait_ge(split_hi, n0 + i)
                        low(lo_[:, i - 1, :], fb[(i - 1) % 2][:, :], hi[:, i - 1, :]).then_inc(split_lo, 1)

            def norm_in_place(name):
                root(name)
                g, o = NORM_GAIN[name]
                for i in range(8):
                    stt(x[:, i, :], x[:, i, :], param(g, o + i), rstd[:, :], MUL, MUL).then_inc(fin_done, 1)

            def memory_apply(layer):
                for i in range(9):
                    if i < 8:
                        wait(dve, mem_lo, 8 * layer + max(i - 1, 0))
                        if i < 2:
                            dve.wait_ge(split_lo, SPLIT0["xa1"] + 8 if layer else 8)
                        ts(fb[i % 2][:, 0:MEM], memn[:, i, :], param("norm_mem_g", 8 * layer + i), None, MUL)\
                            .then_inc(mem_scaled, 1)
                    if i:
                        dve.wait_ge(mem_hi, 8 * layer + i)
                        low(m_lo[:, i - 1, :], fb[(i - 1) % 2][:, 0:MEM], m_hi[:, i - 1, :]).then_inc(mem_lo, 1)

            for r in range(20):
                dve.wait_ge(pre_ready, r + 1)
                b = bank[4 + r % 4]
                if r < 4:
                    cp(prm[:, r, 0:PROWS[r]], b[:, 0:PROWS[r]]).then_inc(pre_done, 1)
                elif r < 12:
                    cp(x[:, r - 4, :], b[:, :]).then_inc(pre_done, 1)
                else:
                    cp(memn[:, r - 12, :], b[:, 0:MEM]).then_inc(pre_done, 1)
            dve.wait_ge(masks_ready, 5)
            nc.vector.reciprocal(inv16[:, :], inv16[:, :]).then_inc(consts_done, 1)
            dve.wait_ge(chi_done, 1)
            low(c_pair[:, :, 1], c_silu[:, :], c_pair[:, :, 0]).then_inc(cpair_ready, 1)
            root("mem")
            for i in range(8):
                tt(memn[:, i, :], memn[:, i, :], rstd[:, 0:MEM], MUL).then_inc(memn_done, 1)
            norm_apply("mix0")
            dve.wait_ge(memn_done, 8)
            memory_apply(0)
            dve.wait_ge(pwhi_done, 1)
            low(pw_lo[:, :, :], pw_raw[:, :, :], pw_hi[:, :, :]).then_inc(pwlo_done, 1)

            split(0)

            def ada(n, step_):
                split(n + 1, step_)
                for j in range(2):
                    hold(dve, slab_half, 2 * n + j + 1 + 2 * step_)
                    o = mod[:, 2 * n + j:2 * n + j + 1] if isinstance(step_, int) else \
                        mod[:, bass.ds(2 * step_ + (2 * n + j), 1)]
                    nc.vector.tensor_reduce(o, bank[(2 * n + j) % 4][:, 0:2], AX.X, ADD).then_inc(tile_free, 1)

            for n in range(4):
                ada(n, 0)
            with dve.Fori(1, 3) as it:
                for u in range(4):
                    ada(u, 4 * it)
            dve.wait_ge(tile_free, 24)
            link(tt(mod[:, :], mod[:, :], prm[:, 1, 0:24], ADD))
            g0 = PROW["norm_g_2"][1]
            link(ts(gs2[:, :], mod[:, 8:16], 1.0, None, ADD))
            link(tt(gs2[:, :], gs2[:, :], prm[:, 0, g0:g0 + DT], MUL))

            CONV = [(k, i) for pair in ((0, 1), (2, 3)) for k in range(CK) for i in pair]
            conv_at, n_conv = {}, 0
            for k, i in CONV:
                if k < CK - 1:
                    n_conv += 1
                    conv_at[(k, i)] = n_conv
            todo = list(CONV)

            def conv(count):
                for _ in range(min(count, len(todo))):
                    k, i = todo.pop(0)
                    src, o, w = glu[:, i, k:k + T], cv[:, i, :], param("conv_dw_w", 4 * k + i)
                    if k == 0:
                        m = ts(o, src, w, param("conv_dw_b", i), MUL, ADD)
                    else:
                        dve.wait_ge(conv_step, conv_at[(k - 1, i)])
                        m = stt(o, src, w, o, MUL, ADD)
                    m.then_inc(cv_ready if k == CK - 1 else conv_step, 1)

            T0 = TILE0["pc_in"]
            for s in range(6):
                n = FIRST["pc_in"] + s
                split(n + 1)
                for j in range(2):
                    tile = 2 * s + j
                    b = bank[(T0 + tile) % 4]
                    if s in (1, 3):
                        dve.wait_ge(slab_half, 2 * n + 1 + j)
                        dve.wait_ge(sig_done, s + j)
                        if s == 1 and j == 0:
                            dve.wait_ge(pads_ready, 2)
                        tt(glu[:, s - 1 + j, CK - 1:], sq[j][:, :], b[:, :], MUL).then_inc(tile_free, 3 if j else 1)
                    elif s >= 4:
                        dve.wait_ge(slab_half, 2 * n + 1 + j)
                        cp(u_pad[:, 2 * (s - 4) + j, 16:], b[:, :]).then_inc(tile_free, 1)
                if s == 1:
                    dve.wait_ge(tile_free, T0 + 4)
                if s == 3:
                    dve.wait_ge(tile_free, T0 + 8)
                conv([0, 0, 12, 10, 14, 14][s])

            def memory_out(layer, after=lambda s: None):
                stage = f"kv{layer}"
                for s in range(8):
                    n = FIRST[stage] + s
                    split(n + 1)
                    for j in range(2):
                        dve.wait_ge(slab_half, 2 * n + 1 + j)
                        b = bank[(TILE0[stage] + 2 * s + j) % 4][:, 0:256]
                        o = kT[:, 2 * s + j, :] if s < 4 else vN[:, j, (s - 4) * 256:(s - 3) * 256]
                        cp(o, b).then_inc(tile_free, 1)
                    after(s)

            def mixer_meanwhile(s):
                if s % 2:
                    g = s // 2
                    dve.wait_ge(poolhi_done, g + 1)
                    low(pooled_lo[:, g, :], pooled[:, :], pooled_hi[:, g, :]).then_inc(poollo_done, 1)
                conv(5)

            memory_out(0, mixer_meanwhile)
            for g in range(5):
                if g < 4:
                    dve.wait_ge(pool_out, g + 1)
                    dve.wait_ge(*((mem_lo, 8) if g < 2 else (y_lo, g - 1)))
                    ts(fb[g % 2][:, :], bank[4 + g % 2][:, :], param("pool_scale", g), None, MUL).then_inc(ya_scaled, 1)
                if g:
                    dve.wait_ge(ya_hi, g)
                    low(h_lo[:, g - 1, :], fb[(g - 1) % 2][:, :], h_hi[:, g - 1, :]).then_inc(y_lo, 1)
            conv(len(todo))
            dve.wait_ge(cv_summed, 4)
            for i in range(4):
                dve.wait_ge(cv_ready, i + 1)
                stt(cv[:, i, :], bank[6][:, :], -1.0 / (4 * P), cv[:, i, :], MUL, ADD).then_inc(xc_ready, 1)
            dve.wait_ge(ln_sqrt, 1)
            link(nc.vector.reciprocal(rstd[:, :], rstd[:, :]))
            for i in range(4):
                tt(cv[:, i, :], cv[:, i, :], rstd[:, :], MUL).then_inc(ln_norm, 1)
            for i in range(4):
                dve.wait_ge(yb_hi, i + 1)
                low(h_lo[:, 4 + i, :], cv[:, i, :], h_hi[:, 4 + i, :]).then_inc(y_lo, 1)

            def add_to_x(stage):
                for s in range(4):
                    n = FIRST[stage] + s
                    split(n + 1)
                    for j in range(2):
                        i = 2 * s + j
                        dve.wait_ge(slab_half, 2 * n + 1 + j)
                        tt(x[:, i, :], x[:, i, :], bank[(TILE0[stage] + i) % 4][:, :], ADD).then_inc(tile_free, 1)

            add_to_x("pc_out")

            def cross(layer):
                norm_apply(f"xa{layer}")
                if layer:
                    memory_apply(1)
                    memory_out(1)
                stage = f"wq{layer}"
                for s in range(4):
                    n = FIRST[stage] + s
                    split(n + 1)
                    for j in range(2):
                        i = 2 * s + j
                        dve.wait_ge(slab_half, 2 * n + 1 + j)
                        ts(qT[:, i, :], bank[(TILE0[stage] + i) % 4][:, :], XHD ** -0.5, None, MUL).then_inc(tile_free, 1)
                for h in range(XH + 1):
                    e = h - 1
                    if h < XH:
                        for i in range(2):
                            dve.wait_ge(xs_ready, 8 * layer + 2 * h + i + 1)
                            b = bank[4 + XA_AT[("S", h, i)] % 4]
                            nc.vector.tensor_reduce(nmax[:, h % 2, 2 * i:2 * i + 2],
                                                    b[:, :].rearrange("p (a m) -> p a m", a=2), AX.X, MAX,
                                                    negate=True).then_inc(xmax_done, 1)
                    if h:
                        for j in range(2):
                            dve.wait_ge(xt_ready, 8 * layer + 2 * e + j + 1)
                            wait(dve, xo_ready, 8 * layer + 2 * (e - 1) if e >= 2 else 0)
                            cp(xpT[:, e % 2, j, :], bank[4 + XA_AT[("T", e, j)] % 4][:, :]).then_inc(xt_done, 1)
                        for d in range(2):
                            i = 2 * e + d
                            dve.wait_ge(xo_hi, 8 * layer + i + 1)
                            low(h_lo[:, i, :], bank[4 + XA_AT[("O", e, d)] % 4][:, :], h_hi[:, i, :]).then_inc(xo_lo, 1)
                    if h < XH:
                        dve.wait_ge(xexp_done, 16 * layer + 4 * h + 4)
                        link(nc.vector.reciprocal(rinv[:, h % 2, :], rsum[:, h % 2, :]))
                        for t in range(NB):
                            v = xp[:, h % 2, t, :]
                            ts(v, v, rinv[:, h % 2, t:t + 1], None, MUL).then_inc(xp_ready, 1)
                add_to_x(f"wo{layer}")
                norm_apply(f"ffn{layer}")
                up, down = f"up{layer}", f"down{layer}"
                if stop == f"wo{layer}":
                    return
                if layer == 0:
                    dve.wait_ge(split_lo, SPLIT0["ffn0"] + 8)
                    for j in range(2):
                        nc.vector.memset(fb[j][:, 0:1], 0.0).then_inc(g_lo_done, 1)
                n, tile = FIRST[up], TILE0[up]
                with dve.Fori(0, COUNT[up] // 2) as it:
                    split(n + 1, 2 * it)
                    for j in range(2):
                        b = bank[(tile + j) % 4]
                        dve.wait_ge(tap2, 2 * it + (FT * layer + j + 1))
                        stt(fb[j][:, 1:], b[:, :T - 1], tap(layer, 1, j, 2 * it), fb[j][:, 1:], MUL, ADD).then_inc(tap1, 1)
                        dve.wait_ge(tap1, 2 * it + (FT * layer + j + 1))
                        stt(fb[j][:, 2:], b[:, :T - 2], tap(layer, 0, j, 2 * it), fb[j][:, 2:], MUL, ADD)\
                            .then_inc(tile_free, 1)
                    split(n + 2, 2 * it)
                    for j in range(2):
                        dve.wait_ge(slab_half, 4 * it + (2 * n + 3 + j))
                        dve.wait_ge(gate_silu, 2 * it + (FT * layer + j + 1))
                        tt(fb[j][:, :], fb[j][:, :], bank[(tile + 2 + j) % 4][:, :], MUL).then_inc(tile_free, 1)
                    for j in range(2):
                        dve.wait_ge(g_hi_done, 2 * it + (FT * layer + j + 1))
                        i = bass.ds(2 * it + j, 1)
                        low(g_lo[:, i, :].rearrange("p a t -> p (a t)"), fb[j][:, :],
                            g_hi[:, i, :].rearrange("p a t -> p (a t)")).then_inc(g_lo_done, 1)
                n, tile = FIRST[down], TILE0[down]
                with dve.Fori(0, 2) as it:
                    for s in range(6):
                        split(n + s + 1, 6 * it)
                        if s % 3 == 2:
                            for j in range(2):
                                i = 2 * (s // 3) + j
                                dve.wait_ge(slab_half, 12 * it + (2 * (n + s) + 1 + j))
                                v = x[:, bass.ds(4 * it + i, 1), :].rearrange("p a t -> p (a t)")
                                tt(v, v, bank[(tile + i) % 4][:, :], ADD).then_inc(tile_free, 1)

            if stop == "pc_out":
                return finish_early(dve, "pc_out")
            cross(0)
            if stop in ("wo0", "down0"):
                return finish_early(dve, stop)

            norm_apply("mix1")
            dve.wait_ge(pos_loaded, 16)
            dve.wait_ge(small_loaded, 32)
            rr = slice(64, 96)
            s_, c_, t_ = r_sin[rr, :], r_cos[rr, :], sq[0][rr, :]
            link(cp(s_, pos_i[rr, :]))
            link(ts(c_, s_, rope_c[rr, 0:1], None, MUL))
            for o, shift in ((s_, 0.0), (c_, 0.25)):
                link(ts(t_, c_, 1.0 / TWO_PI, shift, MUL, ADD))
                link(ts(t_, t_, ROUNDER, None, ADD))
                link(ts(t_, t_, -ROUNDER, None, ADD))
                link(stt(o, t_, -PI2_A, c_, MUL, ADD))
                link(stt(o, t_, -PI2_B, o, MUL, ADD))
                link(stt(o, t_, -PI2_C, o, MUL, ADD))
                link(ts(o, o, shift * TWO_PI, 3.1415925, ADD, ALU.min))
                ts(o, o, -3.1415925, None, MAX).then_inc(angle_ready, 1)
                dve.wait_ge(angle_ready, 1 if shift == 0.0 else 2)
            T0 = TILE0["dq"]
            for s in range(3):
                n = FIRST["dq"] + s
                split(n + 1)
                for j in range(2):
                    i = 2 * s + j
                    dve.wait_ge(slab_half, 2 * n + 1 + j)
                    b = bank[(T0 + i) % 4]
                    if i < 3:
                        cp(cq_raw[:, i, :], b[:, :]).then_inc(tile_free, 1)
                    elif i < 5:
                        cp(ckv_raw[:, i - 3, :], b[:, :]).then_inc(tile_free, 1)
                    else:
                        cp(kpe_raw[rr, :], b[rr, :]).then_inc(tile_free, 1)
            norm_apply("ckv")
            norm_apply("cq")
            swap = list(range(16, 32)) + list(range(16))
            dve.wait_ge(sin_done, 2)
            dve.wait_ge(tile_free, T0 + 6)
            k_ = kpe_raw[rr, :]
            link(ts(s_, s_, rope_c[rr, 1:2], None, MUL))
            link(nc.vector.stream_shuffle(t_, k_, swap))
            link(tt(t_, t_, s_, MUL))
            link(tt(k_, k_, c_, MUL))
            link(tt(k_, k_, t_, ADD))
            cp(lk[rr, :, :], kpe_raw[rr, :].rearrange("p (a t) -> p a t", a=1).broadcast_to([32, MH, T]))\
                .then_inc(rope_ready, 1)
            for s in range(2):
                n = FIRST["ukv"] + s
                split(n + 1)
                for i in range(12):
                    if i < 11:
                        dve.wait_ge(kv_tile, 11 * s + i + 1)
                    else:
                        dve.wait_ge(slab_half, 2 * n + 2)
                    b = bank[(TILE0["ukv"] + 12 * s + i) % 4]
                    if i < 8:
                        cp(lk[0:NOPE, 8 * s + i, :], b[0:NOPE, :]).then_inc(tile_free, 1)
                    else:
                        cp(lv[:, i - 8, 512 * s:512 * s + 512], b[:, :]).then_inc(tile_free, 1)
            split(FIRST["uq"] + 1)

            def queries(pair):
                n = FIRST["uq"] + pair
                for j in range(2):
                    h = 2 * pair + j
                    dve.wait_ge(slab_half, 2 * n + 1 + j)
                    wait(dve, ls_ready, 4 * (h - 3))
                    ts(lq[0:QKD, h % 4, :], bank[(TILE0["uq"] + h) % 4][0:QKD, :], MLA_SCALE, None, MUL)\
                        .then_inc(tile_free, 1)
                    dve.wait_ge(tile_free, TILE0["uq"] + h + 1)
                    wait(dve, q_ready, h - 1)
                    nc.vector.stream_shuffle(lsh[h % 2][rr, :], lq[rr, h % 4, :], swap).then_inc(q_base, 1)

            queries(0)
            for h in range(MH + 1):
                e = h - 1
                if h < MH:
                    for i in range(NB):
                        dve.wait_ge(ls_ready, 4 * h + i + 1)
                        nc.vector.tensor_reduce(nmax[:, h % 2, i:i + 1], bank[4 + LQ_AT[("S", h, i)] % 3][:, 0:(i + 1) * P],
                                                AX.X, MAX, negate=True).then_inc(lmax_done, 1)
                    if h % 2 == 0 and h // 2 + 2 <= MH // 2:
                        split(FIRST["uq"] + h // 2 + 2)
                    if h % 2 == 0 and h // 2 + 1 < MH // 2:
                        queries(h // 2 + 1)
                if h:
                    for j in range(NB):
                        dve.wait_ge(lt_ready, 4 * e + j + 1)
                        wait(dve, lo_ready, e)
                        n = (NB - j) * P
                        cp(lpT[:, KOFF[j]:KOFF[j] + n], bank[4 + LQ_AT[("T", e, j)] % 3][:, 0:n]).then_inc(lt_done, 1)
                    if e % 2:
                        dve.wait_ge(lo_hi, e // 2 + 1)
                        low(h_lo[:, e // 2, :], stat[:, :], h_hi[:, e // 2, :]).then_inc(lo_lo, 1)
                if h < MH:
                    dve.wait_ge(lexp_done, 4 * h + 4)
                    link(nc.vector.reciprocal(rinv[:, h % 2, :], rsum[:, h % 2, :]))
                    for i in range(NB):
                        v = lp[:, h % 2, QOFF[i]:QOFF[i] + (i + 1) * P]
                        ts(v, v, rinv[:, h % 2, i:i + 1], None, MUL).then_inc(lp_ready, 1)
            add_to_x("mla_o")
            if stop == "mla_o":
                return finish_early(dve, stop)
            cross(1)
            if stop in ("wo1", "down1"):
                return finish_early(dve, stop)
            norm_in_place("final1")
            norm_apply("second")

            for s in range(13):
                n = FIRST["w_in"] + s
                split(n + 1)
                for j in range(2):
                    b = bank[(TILE0["w_in"] + 2 * s + j) % 4]
                    dve.wait_ge(slab_half, 2 * n + 1 + j)
                    i = 2 * s + j
                    if s < 2:
                        m = ts(sq_T[:, i, :], b[:, :], HSCALE, None, MUL)
                    elif s < 4:
                        m = cp(sk_T[:, i - 4, :], b[:, :])
                    elif s < 6:
                        m = cp(sv_N[:, 2 * j:2 * j + 2, (s - 4) * 256:(s - 3) * 256],
                               b[:, :].rearrange("p (a n) -> p a n", a=2))
                    elif s < 8:
                        m = cp(sg_T[:, i - 12, :], b[:, :])
                    elif s < 10:
                        m = ts(wq_T[:, i - 16, :], b[:, :], HSCALE, None, MUL)
                    elif i == 20:
                        cp(wk_T[0:HD, 0, :], b[0:HD, :])
                        m = cp(wk_T[HD:, 1, :], b[HD:, :])
                    elif i == 21:
                        m = cp(wv_N[:, :, :], b[:, :].rearrange("p (a n) -> p a n", a=NB))
                    else:
                        m = cp(wg_T[:, i - 22, :], b[:, :])
                    m.then_inc(tile_free, 1)

            dve.wait_ge(sb_masks, 5)
            dve.wait_ge(gate_act, 4)
            for h in range(SBH):
                for j in range(NB - 1, -1, -1):
                    v = sp_T[:, j, j * P:]
                    dve.wait_ge(ln_done, 4 * h + NB - j)
                    link(stt(v, bank[4 * (h % 2) + j][:, 0:(NB - j) * P], 0.0, v, MAX, ADD))
                    tt(v[:, 0:P], v[:, 0:P], before[:, :], MUL).then_inc(sp_ready, 1)
                r0 = (h % 2) * HD
                dve.wait_ge(so_ready, h + 1)
                o = fb[h % 2][r0:r0 + HD, :]
                tt(o, bank[4 * (h % 2) + 3][r0:r0 + HD, :], sg_T[r0:r0 + HD, h // 2, :], MUL).then_inc(so_scaled, 1)
                dve.wait_ge(so_hi, h + 1)
                low(h_lo[r0:r0 + HD, h // 2, :], o, h_hi[r0:r0 + HD, h // 2, :]).then_inc(so_lo, 1)

            for b in range(2):
                link(nc.vector.memset(wp[:, b, 0, 0:P], NEG))
            dve.wait_ge(gate_act, 8)
            for h in range(SWH + 1):
                e = h - 1
                if h < SWH:
                    slope = 2.0 ** (-8.0 * (h + 1) / SWH)
                    for q in range(NB):
                        c0 = P if q == 0 else 0
                        dve.wait_ge(ws_ready, 2 * h + q // 2 + 1)
                        wait(dve, wt_ready, 2 * (h - 1) if h >= 2 else 0)
                        b = bank[4 + SW_AT[("S", h, q // 2)] % 4]
                        stt(wp[:, h % 2, q, c0:], relm[:, c0:], -slope, b[:, (q % 2) * 2 * P + c0:(q % 2 + 1) * 2 * P],
                            MUL, ADD).then_inc(wl_done, 1)
                    dve.wait_ge(wl_done, 4 * h + 4)
                    link(nc.vector.tensor_reduce(nmax[:, h % 2, :], wp[:, h % 2, :, :], AX.X, MAX))
                    ts(nmax[:, h % 2, :], nmax[:, h % 2, :], sinks[:, h:h + 1], -1.0, MAX, MUL).then_inc(wmax_done, 1)
                if h:
                    r0 = (e % 2) * HD
                    flat = wpT[:, :, :].rearrange("p a n -> p (a n)")
                    for b in range(2):
                        dve.wait_ge(wt_ready, 2 * e + b + 1)
                        wait(dve, wo_ready, e)
                        n = 4 * P - b * P
                        cp(flat[:, b * 512:b * 512 + n], bank[4 + SW_AT[("T", e, b)] % 4][:, 0:n]).then_inc(wt_done, 1)
                    dve.wait_ge(wo_ready, e + 1)
                    o = fb[e % 2][r0:r0 + HD, :]
                    tt(o, bank[4 + SW_AT[("O", e, 0)] % 4][r0:r0 + HD, :], wg_T[r0:r0 + HD, e // 2, :], MUL)\
                        .then_inc(wo_scaled, 1)
                    dve.wait_ge(wo_hi, e + 1)
                    low(h_lo[r0:r0 + HD, 4 + e // 2, :], o, h_hi[r0:r0 + HD, 4 + e // 2, :]).then_inc(wo_lo, 1)
                if h < SWH:
                    dve.wait_ge(wexp_done, 5 * h + 5)
                    link(tt(rsum[:, h % 2, :], rsum[:, h % 2, :], esink[:, h % 2, :], ADD))
                    link(nc.vector.reciprocal(rinv[:, h % 2, :], rsum[:, h % 2, :]))
                    for q in range(NB):
                        v = wp[:, h % 2, q, P if q == 0 else 0:]
                        ts(v, v, rinv[:, h % 2, q:q + 1], None, MUL).then_inc(wp_ready, 1)
            for s in range(4):
                n = FIRST["w_out"] + s
                split(n + 1)
                for j in range(2):
                    i = 2 * s + j
                    dve.wait_ge(slab_half, 2 * n + 1 + j)
                    stt(x[:, i, :], bank[(TILE0["w_out"] + i) % 4][:, :], mod[:, 16 + i:17 + i], x[:, i, :], MUL, ADD)\
                        .then_inc(tile_free, 1)
            norm_in_place("final2")
            for t in range(NB):
                dve.wait_ge(out_tr, 2 * t + 2)
                cp(x_nat[:, t, 512:], bank[2 * t + 1][:, :]).then_inc(out_copied, 1)


_INS = ["x", "mem", "positions", "norm_mix_g", "norm_xa_g", "norm_mem_g", "xa_wq", "xa_wkv", "xa_wo", "norm_ffn_g",
        "ffn_w_up", "ffn_conv_w", "ffn_conv_b", "ffn_w_down", "pc_w_in", "pool_w", "pool_scale", "conv_dw_w",
        "conv_dw_b", "conv_ln_g", "conv_ln_b", "pc_w_out", "mla_w_dq_dkv", "mla_q_norm_g", "mla_w_uq",
        "mla_kv_norm_g", "mla_w_ukv", "mla_w_o", "final_norm_g", "c_2", "w_ada_2", "b_ada_2", "norm_g_2", "w_in_2",
        "sinks_2", "w_out_2", "final_g_2"]


def kernel(**inputs):
    import numpy as _np
    import concourse.bacc as _bacc
    from concourse import mybir as _mybir
    from concourse.bass_utils import run_bass_kernel_spmd as _run

    nc = _bacc.Bacc("TRN2", target_bir_lowering=False, num_devices=1)
    arrays, args = {}, {}
    given = {name: _np.ascontiguousarray(inputs[name]) for name in _INS}
    half = ROPE // 2
    freq = 1.0 / 10000.0 ** (_np.arange(0, ROPE, 2, dtype=_np.float64) / ROPE)
    given["rope_const"] = _np.stack([_np.tile(freq, 2), _np.repeat([-1.0, 1.0], half)], 1).astype(_np.float32)
    for name, a in given.items():
        arrays[f"in_{name}_dram"] = a
        args[name] = nc.dram_tensor(f"in_{name}_dram", a.shape, _mybir.dt.from_np(a.dtype), kind="ExternalInput").ap()
    out = nc.dram_tensor("out_0_dram", (1, T, D), _mybir.dt.float32, kind="ExternalOutput").ap()
    build(nc, args, out, None)
    r = _run(nc, [arrays], core_ids=[0])
    return r.results[0]["out_0_dram"]
```

```python
import concourse.bass as bass
from concourse import mybir
from contextlib import ExitStack

P = 128
D = 1024
T = 512
DT = D // P
MEM = 256
XH = 4
XHD = D // XH
FF = 2816
FT = FF // P
CK = 31
MH = 16
NOPE, ROPE, VD = 64, 32, 64
QL, KVL = 384, 256
QKD = NOPE + ROPE
MLA_SCALE = QKD ** -0.5
SBH = SWH = 8
HD = 64
HSCALE = HD ** -0.5
WINDOWS = (2, 4, 8, 16)
EPS = 1e-6
NEG = -1e30
NB = T // P
SLAB = 2048

STAGES = [("pc_in", 6), ("kv0", 8), ("ada", 12), ("pc_out", 4), ("wq0", 4), ("wo0", 4), ("up0", 22),
          ("down0", 12), ("dq", 3), ("ukv", 2), ("uq", 8), ("mla_o", 4), ("wq1", 4), ("kv1", 8), ("wo1", 4),
          ("up1", 22), ("down1", 12), ("w_in", 13), ("w_out", 4)]
FIRST, COUNT = {}, {}
NSLAB = 0
for _name, _count in STAGES:
    FIRST[_name], COUNT[_name] = NSLAB, _count
    NSLAB += _count


def splits_before(n):
    return n - min(max(n - FIRST["ada"], 0), COUNT["ada"])


def slab_columns(n):
    if 0 <= n - FIRST["uq"] < COUNT["uq"]:
        return QL // P * 2 * QKD
    if n == FIRST["dq"] + 2:
        return DT * 160
    for down in ("down0", "down1"):
        if 0 <= n - FIRST[down] < COUNT[down] and (n - FIRST[down]) % 3 == 2:
            return (FT - 16) * 256
    return SLAB


def is_ada(n):
    return 0 <= n - FIRST["ada"] < COUNT["ada"]


TILES = {"ada": 0, "down0": 8, "down1": 8, "ukv": 24}
TILE0 = {}
_t = 0
for _name, _count in STAGES:
    TILE0[_name] = _t
    _t += TILES.get(_name, 2 * _count)

NORMS = [("mix0", 8), ("mem", 8), ("xa0", 8), ("ffn0", 8), ("mix1", 8), ("ckv", 2), ("cq", 3), ("xa1", 8),
         ("ffn1", 8), ("final1", 8), ("second", 8), ("final2", 8)]
POOLED = ["mem", "xa0", "ffn0", "mix1", "ckv", "cq", "xa1", "ffn1"]
NORM0, NORMI, NORMT = {}, {}, {}
_t = 0
for _i, (_name, _count) in enumerate(NORMS):
    NORM0[_name], NORMI[_name], NORMT[_name] = _t, _i, _count
    if _name not in POOLED:
        _t += _count

PROW = {"norm_mix_g": (0, 0), "norm_xa_g": (0, 16), "norm_mem_g": (0, 32), "norm_ffn_g": (0, 48),
        "final_norm_g": (0, 64), "norm_g_2": (0, 72), "final_g_2": (0, 80), "pool_scale": (0, 88),
        "conv_dw_b": (0, 92), "conv_ln_g": (0, 96), "conv_ln_b": (0, 100), "mla_q_norm_g": (0, 104),
        "mla_kv_norm_g": (0, 107), "c_2": (0, 109), "b_ada_2": (1, 0), "ffn_conv_w1": (1, 24),
        "conv_dw_w": (2, 0), "ffn_conv_w0": (3, 0), "ffn_conv_b": (3, 66)}
PROWS = (117, 90, 124, 110)

TWO_PI = 6.283185307179586
PI2_A = 6.28125
PI2_B = 0.0019350051879882812
PI2_C = TWO_PI - PI2_A - PI2_B
ROUNDER = 12582912.0

SPLITS = ["mix0", "xa0", "ffn0", "mix1", "ckv", "cq", "xa1", "ffn1", "second"]
SPLIT0, SCALED0 = {}, {}
_t, _u = 0, 0
for _name in SPLITS:
    SPLIT0[_name] = _t
    _t += NORMT[_name]
    if _name not in POOLED:
        SCALED0[_name] = _u
        _u += NORMT[_name]


def build(nc, ins, out):
    f32 = mybir.dt.float32
    f32r = mybir.dt.float32r
    i32 = mybir.dt.int32
    ALU = mybir.AluOpType
    ACT = mybir.ActivationFunctionType
    AX = mybir.AxisListType
    MUL, ADD, SUB, MAX = ALU.mult, ALU.add, ALU.subtract, ALU.max

    ctx = ExitStack()
    with ctx:
        top = [(nc.sbuf_base + 31) // 32 * 32]

        def at(name, shape, offset, dt=f32):
            return nc.alloc_sbuf_tensor_at(name, shape, dt, offset=offset)

        def size(shape):
            n = 4
            for s in shape[1:]:
                n *= s
            return (n + 31) // 32 * 32

        def sb(name, shape, dt=f32):
            here = top[0]
            top[0] += size(shape)
            return at(name, shape, here, dt)

        x = sb("x", [P, DT, T])
        h_hi = sb("h_hi", [P, DT, T], f32r)
        h_lo = sb("h_lo", [P, DT, T], f32r)
        raw = [sb(f"w_raw{i}", [P, SLAB]) for i in range(2)]
        w_hi = [sb(f"w_hi{i}", [P, SLAB], f32r) for i in range(2)]
        w_lo = [sb(f"w_lo{i}", [P, SLAB], f32r) for i in range(2)]
        memn = sb("memn", [P, DT, MEM])
        fb = [sb(f"fb{i}", [P, T]) for i in range(2)]
        sq = [sb(f"sq{i}", [P, T]) for i in range(2)]
        rstd = sb("rstd", [P, T])
        prm = sb("prm", [P, 4, P])
        ident = sb("ident", [P, P])
        ones = sb("ones", [P, P])
        relm = sb("relm", [P, 2 * P])
        c_silu = sb("c_silu", [P, DT])
        mod = sb("mod", [P, 24])
        gs2 = sb("gs2", [P, DT])
        eps = sb("eps", [P, 1])
        inv16 = sb("inv16", [P, 16])
        sinks = sb("sinks", [P, SWH])
        rope_c = sb("rope_const", [P, 2])
        kv_col = sb("kv_col", [P, NB])
        ident_b = sb("ident_b", [P, P], mybir.dt.bfloat16)
        later_b = sb("later_b", [P, P], mybir.dt.bfloat16)
        nmax = sb("nmax", [P, 2, NB])
        rsum = sb("rsum", [P, 2, NB])
        rinv = sb("rinv", [P, 2, NB])
        esink = sb("esink", [P, 2, NB])
        arena = top[0]

        def area():
            here = [arena]

            def put(name, shape, dt=f32):
                o = here[0]
                here[0] += size(shape)
                return at(name, shape, o, dt)
            return put, here

        put, _ = area()
        x_nat = put("x_nat", [P, NB, D])
        mem_nat = put("mem_nat", [P, 2, D])
        prow = put("prow", [P, 4, P])
        iota_i = put("iota_i", [P, 2 * P], i32)
        later = put("later", [P, P])
        put, here = area()
        glu = put("glu", [P, 4, CK - 1 + T])
        cv = put("cv", [P, 4, T])
        u_pad = put("u_pad", [P, 4, 16 + T])
        pool_a = put("pool_a", [P, 16 + T])
        pool_b = put("pool_b", [P, 16 + T])
        pooled = put("pooled", [P, T])
        pooled_hi = put("pooled_hi", [P, 4, T], f32r)
        pooled_lo = put("pooled_lo", [P, 4, T], f32r)
        pw_raw = put("pw_raw", [P, 4, P])
        pw_hi = put("pw_hi", [P, 4, P], f32r)
        pw_lo = put("pw_lo", [P, 4, P], f32r)
        xa_at = here[0]
        m_hi = put("m_hi", [P, DT, MEM], f32r)
        m_lo = put("m_lo", [P, DT, MEM], f32r)
        kT = put("xa_kT", [P, DT, MEM])
        vN = put("xa_v", [P, 2, D])
        ends = [here[0]]
        put, here = area()
        qT = put("xa_qT", [P, DT, T])
        xp = put("xa_p", [P, 2, NB, MEM])
        xpT = put("xa_pT", [P, 2, 2, T])
        assert here[0] <= xa_at
        put, here = area()
        g_hi = put("g_hi", [P, FT, T], f32r)
        g_lo = put("g_lo", [P, FT, T], f32r)
        ends.append(here[0])
        put, here = area()
        lk = put("mla_k", [P, MH, T])
        lv = put("mla_v", [P, NB, MH * VD])
        lq = put("mla_q", [P, 4, T])
        cq_hi = put("cq_hi", [P, 3, T], f32r)
        cq_lo = put("cq_lo", [P, 3, T], f32r)
        lp_at = here[0]
        lp = put("mla_p", [P, 2, 10 * P])
        lpT = put("mla_pT", [P, 10 * P])
        r_cos = put("rope_cos", [P, T])
        r_sin = put("rope_sin", [P, T])
        ends.append(here[0])
        here[0] = lp_at
        cq_raw = put("cq_raw", [P, 3, T])
        ckv_raw = put("ckv_raw", [P, 2, T])
        kpe_raw = put("kpe_raw", [P, T])
        pos_i = put("pos_i", [P, T], i32)
        assert here[0] <= lp_at + 15 * P * 2 * 4
        here[0] = arena + size([P, MH, T]) + size([P, NB, MH * VD])
        ckv_hi = put("ckv_hi", [P, 2, T], f32r)
        ckv_lo = put("ckv_lo", [P, 2, T], f32r)
        lsh = sq
        put, here = area()
        sq_T = put("sb_q", [P, 4, T])
        sk_T = put("sb_k", [P, 4, T])
        sv_N = put("sb_v", [P, NB, 512])
        sg_T = put("sb_gate", [P, 4, T])
        wq_T = put("sw_q", [P, 4, T])
        wk_T = put("sw_k", [P, 2, T])
        wv_N = put("sw_v", [P, NB, P])
        wg_T = put("sw_gate", [P, 4, T])
        sp_T = put("softplus", [P, NB, T])
        sw_T = put("sb_w", [P, NB, T])
        sp_at = here[0]
        wp = put("sw_p", [P, 2, NB, 2 * P])
        wpT = put("sw_pT", [P, NB, 2 * P])
        minus = put("minus", [P, P])
        before = put("before", [P, P])
        not_before = put("not_before", [P, P])
        from_here = put("from_here", [P, P])
        ends.append(here[0])
        here[0] = sp_at
        softplus = [sp_T, put("softplus_b", [P, NB, T])]
        assert max(ends) <= nc.sbuf_usable_end, (max(ends) - nc.sbuf_usable_end)

        bank = [ctx.enter_context(nc.psum_tensor(f"bank{i}", [P, T], f32)) for i in range(8)]
        stat = bank[7]

        def sem(name):
            return ctx.enter_context(nc.semaphore(name))

        masks_ready = sem("masks_ready")
        iota_ready = sem("iota_ready")
        x_loaded = [sem(f"x_loaded{i}") for i in range(2)]
        mem_loaded = sem("mem_loaded")
        rows_loaded = sem("rows_loaded")
        rows_loaded_a = sem("rows_loaded_a")
        small_loaded = sem("small_loaded")
        poolw_loaded = sem("poolw_loaded")
        pre_ready = sem("pre_ready")
        pre_done = sem("pre_done")
        csilu_done = sem("csilu_done")
        ada_copied = sem("ada_copied")
        ada_cols = sem("ada_cols")
        mod_done = sem("mod_done")
        consts_done = sem("consts_done")
        raw_loaded = [sem(f"raw_loaded{i}") for i in range(2)]
        hi_done = sem("hi_done")
        lo_done = sem("lo_done")
        slab_half = sem("slab_half")
        tile_free = sem("tile_free")
        sq_done = sem("sq_done")
        sum_done = sem("sum_done")
        squares_ready = sem("squares_ready")
        stat_done = sem("stat_done")
        sqrt_done = sem("sqrt_done")
        scaled = sem("scaled")
        split_hi = sem("split_hi")
        split_lo = sem("split_lo")
        memn_done = sem("memn_done")
        mem_hi = sem("mem_hi")
        mem_lo = sem("mem_lo")
        fin_done = sem("fin_done")
        dve_step = sem("dve_step")
        sig_done = sem("sig_done")
        pads_ready = sem("pads_ready")
        pool_step = sem("pool_step")
        pooled_ready = sem("pooled_ready")
        poolhi_done = sem("poolhi_done")
        poollo_done = sem("poollo_done")
        pwhi_done = sem("pwhi_done")
        pwlo_done = sem("pwlo_done")
        pool_out = sem("pool_out")
        ya_scaled = sem("ya_scaled")
        ya_hi = sem("ya_hi")
        y_lo = sem("y_lo")
        cv_ready = sem("cv_ready")
        conv_step = sem("conv_step")
        cv_summed = sem("cv_summed")
        xc_ready = sem("xc_ready")
        xc_sq = sem("xc_sq")
        xc_summed = sem("xc_summed")
        ln_sqrt = sem("ln_sqrt")
        ln_norm = sem("ln_norm")
        ln_silu = sem("ln_silu")
        yb_hi = sem("yb_hi")
        xs_ready = sem("xs_ready")
        xmax_done = sem("xmax_done")
        xexp_done = sem("xexp_done")
        xrinv_ready = sem("xrinv_ready")
        xp_ready = sem("xp_ready")
        xt_ready = sem("xt_ready")
        xt_done = sem("xt_done")
        xo_ready = sem("xo_ready")
        xo_hi = sem("xo_hi")
        xo_lo = sem("xo_lo")
        tap2 = sem("tap2")
        tap1 = sem("tap1")
        taps_done = sem("taps_done")
        gate_silu = sem("gate_silu")
        silu_scaled = sem("silu_scaled")
        g_hi_done = sem("g_hi_done")
        g_lo_done = sem("g_lo_done")
        sin_done = sem("sin_done")
        pos_loaded = sem("pos_loaded")
        angle_ready = sem("angle_ready")
        k_rotated = sem("k_rotated")
        rope_ready = sem("rope_ready")
        kv_tile = sem("kv_tile")
        kv_cols = sem("kv_cols")
        kv_col_sqrt = sem("kv_col_sqrt")
        rinv_ready = sem("rinv_ready")
        q_base = sem("q_base")
        q_ready = sem("q_ready")
        ls_ready = sem("ls_ready")
        lmax_done = sem("lmax_done")
        lexp_done = sem("lexp_done")
        lp_ready = sem("lp_ready")
        lt_ready = sem("lt_ready")
        lt_done = sem("lt_done")
        lo_ready = sem("lo_ready")
        lo_hi = sem("lo_hi")
        lo_lo = sem("lo_lo")
        gate_act = sem("gate_act")
        k_shift = sem("k_shift")
        sb_masks = sem("sb_masks")
        z_ready = sem("z_ready")
        abs_done = sem("abs_done")
        exp_done = sem("exp_done")
        ln_done = sem("ln_done")
        sp_ready = sem("sp_ready")
        c_ready = sem("c_ready")
        w_ready = sem("w_ready")
        so_ready = sem("so_ready")
        so_scaled = sem("so_scaled")
        so_hi = sem("so_hi")
        so_lo = sem("so_lo")
        ws_ready = sem("ws_ready")
        wl_done = sem("wl_done")
        wmax_done = sem("wmax_done")
        wexp_done = sem("wexp_done")
        wrinv_ready = sem("wrinv_ready")
        wp_ready = sem("wp_ready")
        wt_ready = sem("wt_ready")
        wt_done = sem("wt_done")
        wo_ready = sem("wo_ready")
        wo_scaled = sem("wo_scaled")
        wo_hi = sem("wo_hi")
        wo_lo = sem("wo_lo")
        out_tr = sem("out_tr")
        out_copied = sem("out_copied")
        out_copied_a = sem("out_copied_a")
        out_stored = sem("out_stored")

        def wait(eng, s, value):
            if value > 0:
                eng.wait_ge(s, value)

        def hold(eng, s, value):
            if isinstance(value, int):
                wait(eng, s, value)
            else:
                eng.wait_ge(s, value)
                eng.nop(nofuse=True)

        def param(name, i=0):
            j, r = PROW[name]
            return prm[:, j, r + i:r + i + 1]

        def free_before(stage, tile):
            return TILE0[stage] + tile - 3

        def tap(layer, k, tile, moved):
            j, r = PROW[f"ffn_conv_w{layer}"]
            return prm[:, j, bass.ds(moved + (r + FT * k + tile), 1)]

        def conv_bias(layer, tile, moved):
            j, r = PROW["ffn_conv_b"]
            return prm[:, j, bass.ds(moved + (r + FT * layer + tile), 1)]

        LQ_SEQ = [("S", 0, i) for i in range(NB)]
        for _h in range(1, MH + 1):
            if _h < MH:
                LQ_SEQ += [("S", _h, i) for i in range(NB)]
            LQ_SEQ += [("T", _h - 1, j) for j in range(NB)]
        LQ_AT = {u: n for n, u in enumerate(LQ_SEQ)}
        QOFF = [0, P, 3 * P, 6 * P]
        KOFF = [0, 4 * P, 7 * P, 9 * P]
        XA_SEQ, SW_SEQ = [], []
        for _h in range(XH + 1):
            if _h < XH:
                XA_SEQ += [("S", _h, 0), ("S", _h, 1)]
            if _h:
                XA_SEQ += [("T", _h - 1, 0), ("T", _h - 1, 1), ("O", _h - 1, 0), ("O", _h - 1, 1)]
        for _h in range(SWH + 2):
            if _h < SWH:
                SW_SEQ += [("S", _h, 0), ("S", _h, 1)]
            if _h >= 2:
                SW_SEQ += [("O", _h - 2, 0)]
            if 1 <= _h <= SWH:
                SW_SEQ += [("T", _h - 1, 0), ("T", _h - 1, 1)]
        XA_AT = {u: n for n, u in enumerate(XA_SEQ)}
        SW_AT = {u: n for n, u in enumerate(SW_SEQ)}

        def norm_source(name, i):
            after = {"xa0": "pc_out", "ffn0": "wo0", "mix1": "down0", "xa1": "mla_o", "ffn1": "wo1",
                     "final1": "down1", "final2": "w_out"}
            if name in after:
                return tile_free, TILE0[after[name]] + i + 1
            if name == "mem":
                return pre_done, 4 + DT + i + 1
            if name == "mix0":
                return pre_done, 4 + i + 1
            if name == "second":
                return fin_done, i + 1
            return tile_free, TILE0["dq"] + i + 1 + (3 if name == "ckv" else 0)

        NORM_SRC = {"mem": (lambda i: memn[:, i, :], MEM, D), "cq": (lambda i: cq_raw[:, i, :], T, QL),
                    "ckv": (lambda i: ckv_raw[:, i, :], T, KVL)}
        for _n in NORM0:
            NORM_SRC.setdefault(_n, (lambda i: x[:, i, :], T, D))
        NORM_DST = {"cq": (cq_hi, cq_lo), "ckv": (ckv_hi, ckv_lo)}
        NORM_GAIN = {"mix0": ("norm_mix_g", 0), "mix1": ("norm_mix_g", 8), "xa0": ("norm_xa_g", 0),
                     "xa1": ("norm_xa_g", 8), "ffn0": ("norm_ffn_g", 0), "ffn1": ("norm_ffn_g", 8),
                     "cq": ("mla_q_norm_g", 0), "ckv": ("mla_kv_norm_g", 0), "final1": ("final_norm_g", 0),
                     "final2": ("final_g_2", 0)}

        BEFORE = {"xa0": "pc_out", "ffn0": "wo0", "mix1": "up0", "xa1": "mla_o", "ffn1": "wo1"}
        RSTD_FREE = {"mix0": None, "mem": (split_lo, 8), "xa0": (ln_norm, 4), "ffn0": (tile_free, TILE0["wq0"] + 8),
                     "mix1": (tile_free, TILE0["down0"] + 1), "ckv": (stat_done, POOLED.index("ckv") + 1),
                     "cq": (tile_free, TILE0["dq"] + 6), "xa1": (tile_free, TILE0["uq"] + MH),
                     "ffn1": (tile_free, TILE0["wq1"] + 8), "final1": (tile_free, TILE0["down1"] + 1),
                     "second": (fin_done, 8), "final2": (scaled, 8 + 8)}

        def acc_of(name):
            return {"mem": (pool_a, pool_b), "ckv": (fb[1], sq[1])}.get(name, (sq[0], sq[1]))

        def root_to(name):
            return fb[1] if name == "ckv" else rstd

        def slab_source(n):
            for stage, _ in STAGES:
                if FIRST[stage] <= n < FIRST[stage] + COUNT[stage]:
                    break
            s = n - FIRST[stage]

            def cols(w, start, width, rows=None):
                return w.rearrange("(k p) n -> p k n", p=P)[:, :, start:start + width], w.shape[0] // P, width
            if stage == "ada":
                return cols(ins["w_ada_2"][0], 256 * s, 256)
            if stage == "pc_in":
                return cols(ins["pc_w_in"][0], [1024, 512, 1280, 768, 0, 256][s], 256)
            if stage[:2] == "kv":
                return cols(ins["xa_wkv"][int(stage[2])], 256 * s, 256)
            if stage == "pc_out":
                return cols(ins["pc_w_out"][0], 256 * s, 256)
            if stage[:2] == "wq":
                return cols(ins["xa_wq"][int(stage[2])], 256 * s, 256)
            if stage[:2] == "wo":
                return cols(ins["xa_wo"][int(stage[2])], 256 * s, 256)
            if stage[:2] == "up":
                return cols(ins["ffn_w_up"][int(stage[2])], (s // 2) * 256 + (0 if s % 2 else FF), 256)
            if stage[:4] == "down":
                part = s % 3
                k0, k1 = 8 * part, min(8 * part + 8, FT)
                return cols(ins["ffn_w_down"][int(stage[4])][k0 * P:k1 * P, :], (s // 3) * 256, 256)
            if stage == "dq":
                return cols(ins["mla_w_dq_dkv"][0], 256 * s, 256 if s < 2 else 160)
            if stage == "ukv":
                return cols(ins["mla_w_ukv"][0], 1024 * s, 1024)
            if stage == "uq":
                return cols(ins["mla_w_uq"][0], 192 * s, 192)
            if stage == "mla_o":
                return cols(ins["mla_w_o"][0], 256 * s, 256)
            if stage == "w_in":
                return cols(ins["w_in_2"][0], 256 * s, 256)
            return cols(ins["w_out_2"][0], 256 * s, 256)

        def view(buf, nk, width):
            return buf[:, 0:nk * width].rearrange("p (k n) -> p k n", k=nk)

        def rows(eng, name, loaded):
            j, r = PROW[name]
            if name in ("ffn_conv_w0", "ffn_conv_w1"):
                v = ins["ffn_conv_w"][int(name[-1])].rearrange("k d -> (k d)")
            elif name == "conv_dw_w":
                v = ins[name][0].rearrange("k d -> (k d)")
            elif name in ("final_norm_g", "final_g_2"):
                v = ins[name]
            else:
                v = ins[name].rearrange("l d -> (l d)")
            v = v.rearrange("(r p) -> r p", p=P)
            eng.dma_start(prow[r:r + v.shape[0], j, :], v).then_inc(loaded, 16)

        block = ctx.enter_context(nc.Block())

        @block.sync
        def _(sp):
            for half in range(2):
                v = slice(half * 512, (half + 1) * 512)
                sp.dma_start(x_nat[:, :, v], ins["x"][0].rearrange("(t p) d -> p t d", p=P)[:, :, v]).then_inc(x_loaded[half], 16)

            def load(n):
                src, nk, width = slab_source(n)
                if n >= 2 and is_ada(n - 2):
                    sp.wait_ge(slab_half, 2 * (n - 1))
                elif n >= 2:
                    sp.wait_ge(lo_done, splits_before(n - 2) + 1)
                sp.dma_start(view(raw[n % 2], nk, width), src).then_inc(raw_loaded[n % 2], 16)

            def load_up(layer):
                n0 = FIRST[f"up{layer}"]
                w = ins["ffn_w_up"][layer].rearrange("(k p) (a s n) -> p a s k n", p=P, a=2, n=256)
                with sp.Fori(0, COUNT[f"up{layer}"] // 2) as it:
                    for u in range(2):
                        hold(sp, lo_done, 2 * it + (splits_before(n0 + u - 2) + 1))
                        src = w[:, 1 - u, bass.ds(it, 1)].rearrange("p s k n -> p (s k) n")
                        sp.dma_start(view(raw[(n0 + u) % 2], 8, 256), src).then_inc(raw_loaded[(n0 + u) % 2], 16)

            n = 0
            while n < NSLAB:
                layer = {FIRST["up0"]: 0, FIRST["up1"]: 1}.get(n)
                if n == 2:
                    sp.dma_start(mem_nat[:, :, :], ins["mem"][0].rearrange("(t p) d -> p t d", p=P)).then_inc(mem_loaded, 16)
                if layer is None:
                    load(n)
                    n += 1
                else:
                    load_up(layer)
                    n += COUNT["up0"]
            for t in range(NB):
                sp.wait_ge(out_copied, t + 1)
                sp.wait_ge(out_copied_a, t + 1)
                sp.dma_start(out[0, t * P:(t + 1) * P, :], x_nat[:, t, :]).then_inc(out_stored, 16)
            sp.wait_ge(out_stored, 16 * NB)

        @block.gpsimd
        def _(pool):
            for name in ("final_norm_g", "final_g_2", "ffn_conv_b", "mla_q_norm_g", "mla_kv_norm_g", "b_ada_2",
                         "conv_dw_w", "ffn_conv_w0", "ffn_conv_w1"):
                rows(pool, name, rows_loaded)
            pool.dma_start(sinks[:, :], ins["sinks_2"].broadcast_to([P, SWH])).then_inc(small_loaded, 16)
            pool.dma_start(rope_c[64:96, :], ins["rope_const"]).then_inc(small_loaded, 16)
            pool.dma_start(pw_raw[:, :, :], ins["pool_w"][0].rearrange("g c d -> c g d")).then_inc(poolw_loaded, 16)

            nc.gpsimd.memset(ident[:, :], 0.0).then_inc(iota_ready, 1)
            nc.gpsimd.memset(ones[:, :], 1.0).then_inc(masks_ready, 1)
            nc.gpsimd.memset(later[:, :], 0.0).then_inc(iota_ready, 1)
            nc.gpsimd.iota(iota_i[:, :], pattern=[[-1, 2 * P]], base=P, channel_multiplier=1).then_inc(iota_ready, 1)
            pool.wait_ge(iota_ready, 3)
            nc.gpsimd.affine_select(out=ident[:, :], in_=ident[:, :], compare_op=ALU.not_equal, fill=1.0, base=0,
                                    pattern=[[-1, P]], channel_multiplier=1).then_inc(masks_ready, 1)
            nc.gpsimd.affine_select(out=later[:, :], in_=later[:, :], compare_op=ALU.is_ge, fill=NEG, base=0,
                                    pattern=[[-1, P]], channel_multiplier=1).then_inc(masks_ready, 1)
            nc.gpsimd.tensor_copy(relm[:, :], iota_i[:, :]).then_inc(iota_ready, 1)
            pool.wait_ge(iota_ready, 4)
            nc.gpsimd.affine_select(out=relm[:, :], in_=relm[:, :], compare_op=ALU.is_ge, fill=-NEG, base=P,
                                    pattern=[[-1, 2 * P]], channel_multiplier=1).then_inc(iota_ready, 1)
            pool.wait_ge(iota_ready, 5)
            nc.gpsimd.affine_select(out=relm[:, :], in_=relm[:, :], compare_op=ALU.is_gt, fill=-NEG, base=0,
                                    pattern=[[1, 2 * P]], channel_multiplier=-1).then_inc(masks_ready, 1)
            pool.wait_ge(iota_ready, 5)
            nc.gpsimd.iota(iota_i[:, 0:16], pattern=[[1, 16]], base=1, channel_multiplier=0).then_inc(iota_ready, 1)
            pool.wait_ge(iota_ready, 6)
            nc.gpsimd.tensor_copy(inv16[:, :], iota_i[:, 0:16]).then_inc(masks_ready, 1)
            nc.gpsimd.memset(eps[:, :], EPS).then_inc(masks_ready, 1)

            pool.wait_ge(pre_ready, 20)
            nc.gpsimd.memset(glu[:, :, 0:CK - 1], 0.0).then_inc(pads_ready, 1)
            nc.gpsimd.memset(u_pad[:, :, 0:16], 0.0).then_inc(pads_ready, 1)
            pool.wait_ge(pads_ready, 2)
            step = [0]

            def link(ins_):
                step[0] += 1
                ins_.then_inc(pool_step, 1)
                pool.wait_ge(pool_step, step[0])

            def squares(name):
                src, N, _ = NORM_SRC[name]
                acc, tmp = (b[:, 0:N] for b in acc_of(name))
                for i in range(NORMT[name]):
                    pool.wait_ge(*norm_source(name, i))
                    if i == 0:
                        wait(pool, stat_done, POOLED.index(name))
                        link(nc.gpsimd.tensor_tensor(acc, src(i), src(i), MUL))
                        continue
                    link(nc.gpsimd.tensor_tensor(tmp, src(i), src(i), MUL))
                    m = nc.gpsimd.tensor_tensor(acc, acc, tmp, ADD)
                    if i < NORMT[name] - 1:
                        link(m)
                m.then_inc(squares_ready, 1)

            squares("mem")
            pool.wait_ge(stat_done, 1)
            pool.wait_ge(consts_done, 1)
            for g, w in enumerate(WINDOWS):
                pool.wait_ge(tile_free, TILE0["pc_in"] + 8 + g + 1)
                wait(pool, pooled_ready, g)
                src, n = u_pad[:, g, :], 1
                bufs = [pool_a, pool_b]
                while n < w:
                    dst = bufs[0]
                    link(nc.gpsimd.tensor_tensor(dst[:, 2 * n - 1:], src[:, 2 * n - 1:], src[:, n - 1:16 + T - n], ADD))
                    src, n = dst, 2 * n
                    bufs.reverse()
                dst = bufs[0]
                link(nc.gpsimd.tensor_scalar(dst[:, 16:], src[:, 16:], 1.0 / w, 1.0, MUL, MUL))
                link(nc.gpsimd.tensor_tensor(dst[:, 16:16 + w], src[:, 16:16 + w], inv16[:, 0:w], MUL))
                wait(pool, poollo_done, g)
                nc.gpsimd.tensor_tensor(pooled[:, :], dst[:, 16:], u_pad[:, g, 16:], SUB).then_inc(pooled_ready, 1)

            squares("xa0")
            squares("ffn0")
            squares("mix1")
            squares("ckv")
            squares("cq")
            for h in range(MH):
                pool.wait_ge(q_base, h + 1)
                q = lq[64:96, h % 4, :]
                link(nc.gpsimd.tensor_tensor(lsh[h % 2][64:96, :], lsh[h % 2][64:96, :], r_sin[64:96, :], MUL))
                link(nc.gpsimd.tensor_tensor(q, q, r_cos[64:96, :], MUL))
                nc.gpsimd.tensor_tensor(q, q, lsh[h % 2][64:96, :], ADD).then_inc(q_ready, 1)

            squares("xa1")
            squares("ffn1")
            pool.wait_ge(tile_free, TILE0["down1"] + 8)
            nc.gpsimd.memset(minus[:, :], -1.0).then_inc(sb_masks, 1)
            nc.gpsimd.memset(not_before[:, :], NEG).then_inc(sb_masks, 1)
            pool.wait_ge(sb_masks, 2)
            nc.gpsimd.affine_select(out=before[:, :], in_=ones[:, :], compare_op=ALU.is_gt, fill=0.0, base=0,
                                    pattern=[[1, P]], channel_multiplier=-1).then_inc(sb_masks, 1)
            nc.gpsimd.affine_select(out=from_here[:, :], in_=minus[:, :], compare_op=ALU.is_ge, fill=0.0, base=0,
                                    pattern=[[-1, P]], channel_multiplier=1).then_inc(sb_masks, 1)
            nc.gpsimd.affine_select(out=not_before[:, :], in_=not_before[:, :], compare_op=ALU.is_ge, fill=0.0, base=0,
                                    pattern=[[1, P]], channel_multiplier=-1).then_inc(sb_masks, 1)
            pool.wait_ge(tile_free, TILE0["w_in"] + 21)
            pool.dma_start(wk_T[HD:, 0, :], wk_T[0:HD, 0, :]).then_inc(k_shift, 16)
            pool.dma_start(wk_T[0:HD, 1, :], wk_T[HD:, 1, :]).then_inc(k_shift, 16)

        @block.tensor
        def _(pe):
            def mm(o, w, v, start, stop_, **kw):
                return nc.tensor.matmul(o, w, v, start=start, stop=stop_, **kw)

            def slab_tile(stage, n, tile, o, nk, weights, operand, ready=None, first=True, last=True, k0=0, inc=1,
                          inc_sem=None, shift=0, free=True):
                if free:
                    value = free_before(stage, tile) + shift
                    if not isinstance(shift, int) or value > 0:
                        pe.wait_ge(tile_free, value)
                for k in range(nk):
                    if ready is not None:
                        pe.wait_ge(ready[0], ready[1] + k + 1)
                    wh, wl = weights(k)
                    vh, vl = operand(k0 + k)
                    mm(o, wh, vh, first and k == 0, False)
                    mm(o, wh, vl, False, False)
                    m = mm(o, wl, vh, False, last and k == nk - 1)
                m.then_inc(inc_sem or slab_half, inc)

            def slab(stage, n, tiles, nk, width, operand, N=T, ready=None, part=(0, 2), rows=None, shift=0, step=0):
                pe.wait_ge(lo_done, splits_before(n) + 1 + step)
                wh, wl = view(w_hi[n % 2], nk, width), view(w_lo[n % 2], nk, width)
                for i, (tile, c0, cn) in enumerate(tiles):
                    o = bank[(TILE0[stage] + tile) % 4][0:cn, 0:N]
                    slab_tile(stage, n, tile, o, nk, lambda k: (wh[:, k, c0:c0 + cn], wl[:, k, c0:c0 + cn]), operand,
                              ready=ready if i == 0 else None, shift=shift)

            def h_operand(k):
                return h_hi[:, k, :], h_lo[:, k, :]

            def linear(stage, ready, after=lambda s: None):
                for s in range(COUNT[stage]):
                    slab(stage, FIRST[stage] + s, [(2 * s, 0, P), (2 * s + 1, P, P)], DT, 256, h_operand,
                         ready=ready if s == 0 else None)
                    after(s)

            def stat_sum(name):
                N = NORM_SRC[name][1]
                pe.wait_ge(squares_ready, POOLED.index(name) + 1)
                wait(pe, sqrt_done, NORMI[name])
                mm(stat[:, 0:N], ones[:, :], acc_of(name)[0][:, 0:N], True, True).then_inc(stat_done, 1)

            def norm_sums(name):
                _, N, _ = NORM_SRC[name]
                n0, nt = NORM0[name], NORMT[name]
                wait(pe, sqrt_done, NORMI[name])
                for i in range(nt):
                    pe.wait_ge(sq_done, n0 + i + 1)
                    mm(stat[:, 0:N], ones[:, :], sq[(n0 + i) % 2][:, 0:N], i == 0, i == nt - 1).then_inc(sum_done, 1)

            pe.wait_ge(masks_ready, 2)
            pe.wait_ge(rows_loaded, 16 * 9)
            pe.wait_ge(rows_loaded_a, 16 * 10)
            for j, r in enumerate(PROWS):
                nc.tensor.transpose(bank[4 + j][:, 0:r], prow[0:r, j, :], ident[0:r, 0:r]).then_inc(pre_ready, 1)
            def turn_tiles(src, r0, nt):
                for r in range(r0, r0 + DT):
                    if r >= 4:
                        pe.wait_ge(pre_done, r - 3)
                    for t in range(nt):
                        m = nc.tensor.transpose(bank[4 + r % 4][:, t * P:(t + 1) * P],
                                                src[:, t, (r - r0) * P:(r - r0 + 1) * P], ident[:, :])
                    m.then_inc(pre_ready, 1)
                    if r == 7:
                        pe.wait_ge(x_loaded[1], 16)

            pe.wait_ge(x_loaded[0], 16)
            turn_tiles(x_nat, 4, NB)
            pe.wait_ge(pre_done, 4 + DT)
            norm_sums("mix0")

            def mem_meanwhile(s):
                if s == 0:
                    pe.wait_ge(mem_loaded, 16)
                    pe.wait_ge(sqrt_done, 1)
                    turn_tiles(mem_nat, 4 + DT, 2)
                    pe.wait_ge(pre_done, 4 + 2 * DT)
                if s == 1:
                    stat_sum("mem")

            linear("pc_in", (split_lo, SPLIT0["mix0"]), mem_meanwhile)

            def memory(layer):
                stage = f"kv{layer}"

                def m_operand(k):
                    return m_hi[:, k, :], m_lo[:, k, :]
                for s in range(4):
                    slab(stage, FIRST[stage] + s, [(2 * s, 0, P), (2 * s + 1, P, P)], DT, 256, m_operand, N=MEM,
                         ready=(mem_lo, 8 * layer) if s == 0 else None)
                for s in range(4, 8):
                    n = FIRST[stage] + s
                    pe.wait_ge(lo_done, splits_before(n) + 1)
                    wh, wl = view(w_hi[n % 2], DT, 256), view(w_lo[n % 2], DT, 256)
                    for j in range(2):
                        o = bank[(TILE0[stage] + 2 * s + j) % 4][:, 0:256]
                        slab_tile(stage, n, 2 * s + j, o, DT,
                                  lambda k: (m_hi[:, k, j * P:(j + 1) * P], m_lo[:, k, j * P:(j + 1) * P]),
                                  lambda k: (wh[:, k, :], wl[:, k, :]))

            memory(0)
            pe.wait_ge(pwlo_done, 1)
            for g in range(4):
                pe.wait_ge(poollo_done, g + 1)
                wait(pe, ya_scaled, g - 1)
                o = bank[4 + g % 2][:, :]
                mm(o, pw_hi[:, g, :], pooled_hi[:, g, :], True, False)
                mm(o, pw_hi[:, g, :], pooled_lo[:, g, :], False, False)
                mm(o, pw_lo[:, g, :], pooled_hi[:, g, :], False, True).then_inc(pool_out, 1)
            pe.wait_ge(csilu_done, 1)
            pe.wait_ge(ya_scaled, 4)
            with pe.Fori(0, COUNT["ada"] // 2) as it:
                for u in range(2):
                    n = FIRST["ada"] + u
                    pe.wait_ge(raw_loaded[n % 2], 16 * it + 16 * (n // 2 + 1))
                    w = view(raw[n % 2], DT, 256)
                    row = bank[4 + u][0:1, 0:256]
                    for k in range(DT):
                        m = mm(row, c_silu[:, k:k + 1], w[:, k, :], k == 0, k == DT - 1)
                    m.then_inc(slab_half, 2)
                    pe.wait_ge(ada_copied, 2 * it + (u + 1))
                    for j in range(2):
                        m = mm(bank[6][:, bass.ds(4 * it + (2 * u + j), 1)], sq[u][0:1, j * P:(j + 1) * P],
                               ones[0:1, 0:1], True, True)
                    m.then_inc(ada_cols, 1)
            pe.wait_ge(mod_done, 1)
            for i in range(4):
                pe.wait_ge(cv_ready, i + 1)
                mm(bank[6][:, :], ones[:, :], cv[:, i, :], i == 0, i == 3).then_inc(cv_summed, 1)
            for i in range(4):
                pe.wait_ge(xc_sq, i + 1)
                mm(stat[:, :], ones[:, :], sq[i % 2][:, :], i == 0, i == 3).then_inc(xc_summed, 1)
            linear("pc_out", (y_lo, 0))

            def cross_attention(layer):
                base = layer

                def place(kind, h, j):
                    r = XA_AT[(kind, h, j)]
                    if r >= 4:
                        k, g, i = XA_SEQ[r - 4]
                        if k == "S":
                            pe.wait_ge(xexp_done, 16 * base + 4 * g + 2 * i + 2)
                        elif k == "T":
                            pe.wait_ge(xt_done, 8 * base + 2 * g + i + 1)
                        else:
                            pe.wait_ge(xo_lo, 8 * base + 2 * g + i + 1)
                    return bank[4 + r % 4]

                for h in range(XH + 1):
                    if h < XH:
                        for i in range(2):
                            o = place("S", h, i)
                            for b in range(2):
                                q0 = (2 * i + b) * P
                                for k in range(2):
                                    m = mm(o[:, b * MEM:(b + 1) * MEM], qT[:, 2 * h + k, q0:q0 + P],
                                           kT[:, 2 * h + k, :], k == 0, k == 1)
                            m.then_inc(xs_ready, 1)
                    if h:
                        g = h - 1
                        for j in range(2):
                            o = place("T", g, j)
                            for t in range(NB):
                                if j == 0:
                                    pe.wait_ge(xp_ready, 16 * base + 4 * g + t + 1)
                                m = nc.tensor.transpose(o[:, t * P:(t + 1) * P], xp[:, g % 2, t, j * P:(j + 1) * P],
                                                        ident[:, :])
                            m.then_inc(xt_ready, 1)
                        for d in range(2):
                            o = place("O", g, d)
                            for j in range(2):
                                pe.wait_ge(xt_done, 8 * base + 2 * g + j + 1)
                                c0 = g * XHD + d * P
                                m = mm(o[:, :], vN[:, j, c0:c0 + P], xpT[:, g % 2, j, :], j == 0, j == 1)
                            m.then_inc(xo_ready, 1)

            def ffn(layer):
                up, down = f"up{layer}", f"down{layer}"

                def up_step(it, first=False):
                    for u in range(2):
                        slab(up, FIRST[up] + u, [(2 * u, 0, P), (2 * u + 1, P, P)], DT, 256, h_operand,
                             ready=(split_lo, SPLIT0[f"ffn{layer}"]) if first and u == 0 else None,
                             shift=4 * it, step=2 * it)
                        if first and u == 0:
                            stat_sum(f"ffn{layer}")

                up_step(0, first=True)
                with pe.Fori(1, COUNT[up] // 2) as it:
                    up_step(it)
                with pe.Fori(0, 2) as it:
                    for s in range(6):
                        n = FIRST[down] + s
                        part, nk = s % 3, (8, 8, 6)[s % 3]
                        pe.wait_ge(lo_done, splits_before(n) + 1 + 6 * it)
                        wh, wl = view(w_hi[n % 2], nk, 256), view(w_lo[n % 2], nk, 256)
                        for j in range(2):
                            tile = 2 * (s // 3) + j
                            slab_tile(down, n, tile, bank[(TILE0[down] + tile) % 4][:, :], nk,
                                      lambda k: (wh[:, k, j * P:(j + 1) * P], wl[:, k, j * P:(j + 1) * P]),
                                      lambda k: (g_hi[:, k, :], g_lo[:, k, :]), k0=8 * part, first=part == 0,
                                      last=part == 2, free=part == 0, shift=4 * it,
                                      ready=(g_lo_done, FT * layer + 8 * part) if j == 0 else None)

            def cross(layer):
                linear(f"wq{layer}", (split_lo, SPLIT0[f"xa{layer}"]), lambda s: stat_sum(f"xa{layer}") if s == 0 else None)
                if layer:
                    memory(1)
                pe.wait_ge(tile_free, TILE0[f"wo{layer}"])
                cross_attention(layer)
                linear(f"wo{layer}", (xo_lo, 8 * layer))
                ffn(layer)

            cross(0)

            for s, tiles in enumerate(([(0, 0, P), (1, P, P)], [(2, 0, P), (3, P, P)], [(4, 0, P), (5, 64, 96)])):
                slab("dq", FIRST["dq"] + s, tiles, DT, 256 if s < 2 else 160, h_operand,
                     ready=(split_lo, SPLIT0["mix1"]) if s == 0 else None)
                if s == 0:
                    stat_sum("mix1")
            for s in range(2):
                n = FIRST["ukv"] + s
                pe.wait_ge(lo_done, splits_before(n) + 1)
                wh, wl = view(w_hi[n % 2], 2, 1024), view(w_lo[n % 2], 2, 1024)
                for i in range(12):
                    tile = 12 * s + i
                    ready = (split_lo, SPLIT0["ckv"]) if tile == 0 else None
                    last = dict(inc=2) if i == 11 else dict(inc_sem=kv_tile)
                    b = bank[(TILE0["ukv"] + tile) % 4]
                    if i < 8:
                        c0 = i * P
                        slab_tile("ukv", n, tile, b[0:NOPE, :], 2,
                                  lambda k: (wh[:, k, c0:c0 + NOPE], wl[:, k, c0:c0 + NOPE]),
                                  lambda k: (ckv_hi[:, k, :], ckv_lo[:, k, :]), ready=ready, **last)
                        if tile == 1:
                            stat_sum("ckv")
                            for t in range(NB):
                                m = mm(bank[6][:, t:t + 1], fb[1][:, t * P:(t + 1) * P], ones[:, 0:1], True, True)
                            m.then_inc(kv_cols, 1)
                    else:
                        t = i - 8
                        vh, vl = (v.rearrange("p k (h c) -> p k h c", c=P)[:, :, :, NOPE:] for v in (wh, wl))
                        slab_tile("ukv", n, tile, b[:, :].rearrange("p (h c) -> p h c", c=VD), 2,
                                  lambda k: (ckv_hi[:, k, t * P:(t + 1) * P], ckv_lo[:, k, t * P:(t + 1) * P]),
                                  lambda k: (vh[:, k], vl[:, k]), **last)

            def queries(pair):
                n = FIRST["uq"] + pair
                pe.wait_ge(lo_done, splits_before(n) + 1)
                wh, wl = view(w_hi[n % 2], 3, 192), view(w_lo[n % 2], 3, 192)
                for j in range(2):
                    slab_tile("uq", n, 2 * pair + j, bank[(TILE0["uq"] + 2 * pair + j) % 4][0:QKD, :], 3,
                              lambda k: (wh[:, k, j * QKD:(j + 1) * QKD], wl[:, k, j * QKD:(j + 1) * QKD]),
                              lambda k: (cq_hi[:, k, :], cq_lo[:, k, :]),
                              ready=(split_lo, SPLIT0["cq"]) if pair + j == 0 else None)

            def lq_place(kind, h, j):
                r = LQ_AT[(kind, h, j)]
                if r >= 3:
                    k, g, i = LQ_SEQ[r - 3]
                    pe.wait_ge(lexp_done if k == "S" else lt_done, 4 * g + i + 1)
                return bank[4 + r % 3]

            def scores(h):
                pe.wait_ge(q_ready, h + 1)
                for i in range(NB):
                    o = lq_place("S", h, i)
                    n = (i + 1) * P
                    mm(o[:, 0:n], lq[0:QKD, h % 4, i * P:(i + 1) * P], lk[0:QKD, h, 0:n], True, False)
                    mm(o[:, i * P:n], ident_b[:, :], later_b[:, :], False, True).then_inc(ls_ready, 1)

            def turn(h):
                for j in range(NB):
                    o = lq_place("T", h, j)
                    for i in range(j, NB):
                        if j == 0:
                            pe.wait_ge(lp_ready, 4 * h + i + 1)
                        c0 = QOFF[i] + j * P
                        m = nc.tensor.transpose(o[:, (i - j) * P:(i - j + 1) * P], lp[:, h % 2, c0:c0 + P], ident[:, :])
                    m.then_inc(lt_ready, 1)

            def values(h):
                if h % 2 == 0:
                    wait(pe, lo_lo, h // 2)
                r0 = (h % 2) * VD
                for j in range(NB):
                    pe.wait_ge(lt_done, 4 * h + j + 1)
                    m = mm(stat[r0:r0 + VD, j * P:], lv[:, j, h * VD:(h + 1) * VD], lpT[:, KOFF[j]:KOFF[j] + (NB - j) * P],
                           j == 0, j == NB - 1, skip_group_check=True)
                m.then_inc(lo_ready, 1)

            stat_sum("cq")
            queries(0)
            pe.wait_ge(tile_free, TILE0["uq"])
            pe.wait_ge(rope_ready, 1)
            for h in range(MH + 1):
                if h < MH:
                    scores(h)
                    if h % 2 == 0 and h // 2 + 1 < MH // 2:
                        queries(h // 2 + 1)
                if h:
                    turn(h - 1)
                    values(h - 1)
            linear("mla_o", (lo_lo, 0))
            cross(1)
            norm_sums("final1")
            norm_sums("second")

            for s in range(13):
                n = FIRST["w_in"] + s
                if s in (4, 5):
                    pe.wait_ge(lo_done, splits_before(n) + 1)
                    wh, wl = view(w_hi[n % 2], DT, 256), view(w_lo[n % 2], DT, 256)
                    for j in range(2):
                        tile = 2 * s + j
                        b = bank[(TILE0["w_in"] + tile) % 4]
                        wait(pe, tile_free, free_before("w_in", tile))
                        for half in range(2):
                            t = 2 * j + half
                            for k in range(DT):
                                o, hh, hl = b[:, half * 256:(half + 1) * 256], h_hi[:, k, t * P:(t + 1) * P], h_lo[:, k, t * P:(t + 1) * P]
                                mm(o, hh, wh[:, k, :], k == 0, False)
                                mm(o, hh, wl[:, k, :], False, False)
                                m = mm(o, hl, wh[:, k, :], False, k == DT - 1)
                        m.then_inc(slab_half, 1)
                elif s == 10:
                    pe.wait_ge(lo_done, splits_before(n) + 1)
                    wh, wl = view(w_hi[n % 2], DT, 256), view(w_lo[n % 2], DT, 256)
                    slab_tile("w_in", n, 20, bank[(TILE0["w_in"] + 20) % 4][:, :], DT,
                              lambda k: (wh[:, k, 0:P], wl[:, k, 0:P]), h_operand)
                    b = bank[(TILE0["w_in"] + 21) % 4]
                    wait(pe, tile_free, free_before("w_in", 21))
                    for t in range(NB):
                        for k in range(DT):
                            o, hh, hl = b[:, t * P:(t + 1) * P], h_hi[:, k, t * P:(t + 1) * P], h_lo[:, k, t * P:(t + 1) * P]
                            mm(o, hh, wh[:, k, P:], k == 0, False)
                            mm(o, hh, wl[:, k, P:], False, False)
                            m = mm(o, hl, wh[:, k, P:], False, k == DT - 1)
                    m.then_inc(slab_half, 1)
                else:
                    slab("w_in", n, [(2 * s, 0, P), (2 * s + 1, P, P)], DT, 256, h_operand,
                         ready=(split_lo, SPLIT0["second"]) if s == 0 else None)

            pe.wait_ge(tile_free, TILE0["w_out"])

            pe.wait_ge(sb_masks, 5)

            def logits(h):
                wait(pe, so_scaled, h - 1)
                r0, p = (h % 2) * HD, h // 2
                for j in range(NB - 1, -1, -1):
                    mm(bank[4 * (h % 2) + j][:, 0:(NB - j) * P], sk_T[r0:r0 + HD, p, j * P:(j + 1) * P],
                       sq_T[r0:r0 + HD, p, j * P:], True, True).then_inc(z_ready, 1)

            def sticks(h):
                for j in range(NB - 1, -1, -1):
                    pe.wait_ge(sp_ready, 4 * h + NB - j)
                    o = bank[4 * (h % 2) + j]
                    mm(o[:, 0:P], not_before[:, :], ident[:, :], False, False, skip_group_check=True)
                    for i in range(NB - 1, j, -1):
                        mm(o[:, (i - j) * P:(NB - j) * P], minus[:, :], softplus[h % 2][:, i, i * P:], False, False,
                           skip_group_check=True)
                    mm(o[:, 0:(NB - j) * P], from_here[:, :], softplus[h % 2][:, j, j * P:], False, True,
                       skip_group_check=True).then_inc(c_ready, 1)

            def stick_values(h):
                r0 = (h % 2) * HD
                o = bank[4 * (h % 2) + 3][r0:r0 + HD, :]
                pe.wait_ge(w_ready, 4 * h + NB)
                for j in range(NB):
                    m = mm(o[:, j * P:], sv_N[:, j, h * HD:(h + 1) * HD], sw_T[:, j, j * P:], j == 0, j == NB - 1)
                m.then_inc(so_ready, 1)

            logits(0)
            for h in range(SBH):
                if h + 1 < SBH:
                    logits(h + 1)
                sticks(h)
                stick_values(h)

            def w_place(kind, h, j):
                r = SW_AT[(kind, h, j)]
                if r >= 4:
                    k, g, i = SW_SEQ[r - 4]
                    if k == "O":
                        pe.wait_ge(wo_scaled, g + 1)
                    else:
                        pe.wait_ge(wl_done if k == "S" else wt_done, (4 if k == "S" else 2) * g + (2 * i + 2 if k == "S" else i + 1))
                return bank[4 + r % 4]

            pe.wait_ge(so_scaled, SBH)
            pe.wait_ge(k_shift, 32)
            for h in range(SWH + 2):
                if h < SWH:
                    r0, p, g = (h % 2) * HD, h // 2, h // 4
                    for i in range(2):
                        o = w_place("S", h, i)
                        for b in range(2):
                            q = 2 * i + b
                            c0 = P if q == 0 else 0
                            m = mm(o[:, b * 2 * P + c0:(b + 1) * 2 * P], wq_T[r0:r0 + HD, p, q * P:(q + 1) * P],
                                   wk_T[r0:r0 + HD, g, (q - 1) * P + c0:(q + 1) * P], True, True)
                        m.then_inc(ws_ready, 1)
                if h >= 2:
                    e = h - 2
                    r0, g = (e % 2) * HD, e // 4
                    o = w_place("O", e, 0)
                    pe.wait_ge(wt_done, 2 * e + 2)
                    for q in range(NB):
                        v = slice(g * HD, (g + 1) * HD)
                        m = mm(o[r0:r0 + HD, q * P:(q + 1) * P], wv_N[:, q, v], wpT[:, q, 0:P], True, q == 0)
                        if q:
                            m = mm(o[r0:r0 + HD, q * P:(q + 1) * P], wv_N[:, q - 1, v], wpT[:, q - 1, P:], False, True)
                    m.then_inc(wo_ready, 1)
                if 1 <= h <= SWH:
                    e = h - 1
                    for b in range(2):
                        o = w_place("T", e, b)
                        pe.wait_ge(wp_ready, 4 * e + 4)
                        for j in (2 * b, 2 * b + 1):
                            for q in (j, j + 1):
                                if q < NB:
                                    c0 = P if q == j else 0
                                    o0 = (j % 2) * 2 * P + (q - j) * P
                                    m = nc.tensor.transpose(o[:, o0:o0 + P], wp[:, e % 2, q, c0:c0 + P], ident[:, :])
                        m.then_inc(wt_ready, 1)
            pe.wait_ge(so_lo, SBH)
            pe.wait_ge(wo_lo, SWH)
            for s in range(4):
                slab("w_out", FIRST["w_out"] + s, [(2 * s, 0, P), (2 * s + 1, P, P)], DT, 256, h_operand)
            norm_sums("final2")
            pe.wait_ge(sqrt_done, len(NORMS))
            pe.wait_ge(tile_free, TILE0["w_out"] + 8)
            pe.wait_ge(wo_scaled, SWH)
            for t in range(NB):
                for half in range(2):
                    for d in range(4):
                        if t == 0:
                            pe.wait_ge(fin_done, 9 + 4 * half + d)
                        m = nc.tensor.transpose(bank[2 * t + half][:, d * P:(d + 1) * P],
                                                x[:, 4 * half + d, t * P:(t + 1) * P], ident[:, :])
                    m.then_inc(out_tr, 1)

        @block.scalar
        def _(act):
            def a(o, i, f, **kw):
                return nc.scalar.activation(o, i, f, **kw)

            def split(n, step=0):
                if isinstance(step, int) and (n + step >= NSLAB or is_ada(n + step)):
                    return
                last = n - 2 - (COUNT["ada"] if is_ada(n - 2) else 0)
                hold(act, raw_loaded[n % 2], 16 * (n // 2 + 1) + 8 * step)
                hold(act, slab_half, 2 * (last + 1) + 2 * step)
                c = slab_columns(n)
                a(w_hi[n % 2][:, 0:c], raw[n % 2][:, 0:c], ACT.Copy).then_inc(hi_done, 1)

            def norm_squares(name):
                src, N, width = NORM_SRC[name]
                n0, nt = NORM0[name], NORMT[name]
                for i in range(nt):
                    act.wait_ge(*norm_source(name, i))
                    wait(act, sum_done, n0 + i - 1)
                    a(sq[(n0 + i) % 2][:, 0:N], src(i), ACT.Square).then_inc(sq_done, 1)
                act.wait_ge(sum_done, n0 + nt)
                if RSTD_FREE[name]:
                    act.wait_ge(*RSTD_FREE[name])
                a(rstd[:, 0:N], stat[:, 0:N], ACT.Sqrt, scale=1.0 / width, bias=eps[:, :]).then_inc(sqrt_done, 1)

            def norm_hi(name):
                dst = NORM_DST.get(name, (h_hi, h_lo))[0]
                n0 = SPLIT0[name]
                for i in range(NORMT[name]):
                    act.wait_ge(scaled, SCALED0[name] + i + 1)
                    a(dst[:, i, :], fb[i % 2][:, :], ACT.Copy).then_inc(split_hi, 1)

            def root_of(name):
                _, N, width = NORM_SRC[name]
                act.wait_ge(stat_done, POOLED.index(name) + 1)
                act.wait_ge(*RSTD_FREE[name])
                if name == "ckv":
                    act.wait_ge(kv_cols, 1)
                    a(kv_col[:, :], bank[6][:, 0:NB], ACT.Sqrt, scale=1.0 / width, bias=eps[:, :]).then_inc(kv_col_sqrt, 1)
                a(root_to(name)[:, 0:N], stat[:, 0:N], ACT.Sqrt, scale=1.0 / width, bias=eps[:, :]).then_inc(sqrt_done, 1)

            def gain_hi(name):
                if name in BEFORE:
                    act.wait_ge(slab_half, 2 * (FIRST[BEFORE[name]] + COUNT[BEFORE[name]]))
                g, o = NORM_GAIN[name]
                src, hi = NORM_SRC[name][0], NORM_DST.get(name, (h_hi, h_lo))[0]
                for i in range(NORMT[name]):
                    act.wait_ge(*norm_source(name, i))
                    a(hi[:, i, :], src(i), ACT.Copy, scale=param(g, o + i)).then_inc(split_hi, 1)

            def memory_hi(layer, tiles):
                act.wait_ge(memn_done, 8)
                for i in tiles:
                    a(m_hi[:, i, :], memn[:, i, :], ACT.Copy, scale=param("norm_mem_g", 8 * layer + i)).then_inc(mem_hi, 1)

            def splits(stage):
                for s in range(COUNT[stage]):
                    split(FIRST[stage] + s + 1)

            for name in ("norm_mix_g", "c_2", "norm_xa_g", "norm_mem_g", "norm_ffn_g", "norm_g_2", "pool_scale",
                         "conv_dw_b", "conv_ln_g", "conv_ln_b"):
                rows(act, name, rows_loaded_a)
            act.wait_ge(pre_done, 1)
            c0 = PROW["c_2"][1]
            a(c_silu[:, :], prm[:, 0, c0:c0 + DT], ACT.Silu).then_inc(csilu_done, 1)
            act.wait_ge(masks_ready, 6)
            split(0)
            norm_squares("mix0")
            norm_hi("mix0")
            for s in range(6):
                n = FIRST["pc_in"] + s
                split(n + 1)
                if s in (0, 2):
                    for j in range(2):
                        act.wait_ge(slab_half, 2 * n + 1 + j)
                        if s:
                            act.wait_ge(tile_free, TILE0["pc_in"] + 4)
                        b = bank[(TILE0["pc_in"] + 2 * s + j) % 4]
                        a(sq[j][:, :], b[:, :], ACT.Sigmoid).then_inc(sig_done, 1)
                if s == 2:
                    root_of("mem")
                    act.wait_ge(poolw_loaded, 16)
                    a(pw_hi[:, :, :], pw_raw[:, :, :], ACT.Copy).then_inc(pwhi_done, 1)
                if s in (4, 5):
                    memory_hi(0, range(4 * (s - 4), 4 * (s - 3)))
            for s in range(8):
                split(FIRST["kv0"] + s + 1)
                if s % 2:
                    act.wait_ge(pooled_ready, s // 2 + 1)
                    a(pooled_hi[:, s // 2, :], pooled[:, :], ACT.Copy).then_inc(poolhi_done, 1)
            for g in range(4):
                act.wait_ge(ya_scaled, g + 1)
                a(h_hi[:, g, :], fb[g % 2][:, :], ACT.Copy).then_inc(ya_hi, 1)
            act.wait_ge(tile_free, TILE0["pc_in"] + 8)
            with act.Fori(0, COUNT["ada"] // 2) as it:
                for u in range(2):
                    hold(act, slab_half, 4 * it + 2 * (FIRST["ada"] + u + 1))
                    a(sq[u][0:1, 0:256], bank[4 + u][0:1, 0:256], ACT.Copy).then_inc(ada_copied, 1)
            split(FIRST["pc_out"])
            for i in range(4):
                act.wait_ge(xc_ready, i + 1)
                wait(act, xc_summed, i - 1)
                a(sq[i % 2][:, :], cv[:, i, :], ACT.Square).then_inc(xc_sq, 1)
            act.wait_ge(xc_summed, 4)
            a(rstd[:, :], stat[:, :], ACT.Sqrt, scale=1.0 / (4 * P), bias=eps[:, :]).then_inc(ln_sqrt, 1)
            for i in range(4):
                act.wait_ge(ln_norm, i + 1)
                a(cv[:, i, :], cv[:, i, :], ACT.Silu, scale=param("conv_ln_g", i),
                  bias=param("conv_ln_b", i)).then_inc(ln_silu, 1)
                act.wait_ge(ln_silu, i + 1)
                a(h_hi[:, 4 + i, :], cv[:, i, :], ACT.Copy).then_inc(yb_hi, 1)
            splits("pc_out")

            def cross(layer):
                gain_hi(f"xa{layer}")
                for s in range(4):
                    split(FIRST[f"wq{layer}"] + s + 1)
                    if s == 0:
                        root_of(f"xa{layer}")
                    elif layer:
                        memory_hi(1, ((0, 1, 2), (3, 4, 5), (6, 7))[s - 1])
                if layer:
                    splits("kv1")
                for h in range(XH + 1):
                    if h < XH:
                        for t in range(NB):
                            act.wait_ge(xmax_done, 2 * XH * layer + 2 * h + t // 2 + 1)
                            if h >= 2:
                                act.wait_ge(xt_ready, 8 * layer + 2 * (h - 1))
                            b = bank[4 + XA_AT[("S", h, t // 2)] % 4]
                            a(xp[:, h % 2, t, :], b[:, (t % 2) * MEM:(t % 2 + 1) * MEM], ACT.Exp,
                              bias=nmax[:, h % 2, t:t + 1], accum_out=rsum[:, h % 2, t:t + 1]).then_inc(xexp_done, 1)
                        act.wait_ge(xrinv_ready, XH * layer + h + 1)
                        for t in range(NB):
                            v = xp[:, h % 2, t, :]
                            a(v, v, ACT.Copy, scale=rinv[:, h % 2, t:t + 1]).then_inc(xp_ready, 1)
                    if h:
                        for d in range(2):
                            act.wait_ge(xo_ready, 8 * layer + 2 * (h - 1) + d + 1)
                            b = bank[4 + XA_AT[("O", h - 1, d)] % 4]
                            a(h_hi[:, 2 * (h - 1) + d, :], b[:, :], ACT.Copy).then_inc(xo_hi, 1)
                splits(f"wo{layer}")
                gain_hi(f"ffn{layer}")
                up, down = f"up{layer}", f"down{layer}"
                n, tile = FIRST[up], TILE0[up]

                def up_step(it, first=False):
                    done = 2 * it + FT * layer
                    split(n + 1, 2 * it)
                    if first:
                        root_of(f"ffn{layer}")
                    for j in range(2):
                        hold(act, tile_free, 4 * it + (tile + j + 1))
                        hold(act, g_lo_done, done + (j - 1))
                        a(fb[j][:, :], sq[j][:, :], ACT.Identity, scale=tap(layer, 2, j, 2 * it),
                          bias=conv_bias(layer, j, 2 * it)).then_inc(tap2, 1)
                    for j in range(2):
                        hold(act, taps_done, done + (j + 1))
                        a(fb[j][:, :], fb[j][:, :], ACT.Silu).then_inc(gate_silu, 1)
                    split(n + 2, 2 * it)
                    for j in range(2):
                        hold(act, tile_free, 4 * it + (tile + 2 + j + 1))
                        a(g_hi[:, bass.ds(2 * it + j, 1), :].rearrange("p a t -> p (a t)"), fb[j][:, :],
                          ACT.Copy).then_inc(g_hi_done, 1)

                up_step(0, first=True)
                with act.Fori(1, COUNT[up] // 2) as it:
                    up_step(it)
                n = FIRST[down]
                with act.Fori(0, 2) as it:
                    for s in range(6):
                        split(n + s + 1, 6 * it)

            cross(0)
            gain_hi("mix1")
            act.dma_start(pos_i[64:96, :], ins["positions"].broadcast_to([32, T])).then_inc(pos_loaded, 16)
            for s in range(3):
                split(FIRST["dq"] + s + 1)
                if s == 0:
                    root_of("mix1")
            for i, (o, v) in enumerate(((r_sin, r_sin), (r_cos, r_cos))):
                act.wait_ge(angle_ready, i + 1)
                a(o[64:96, :], v[64:96, :], ACT.Sin).then_inc(sin_done, 1)
            gain_hi("ckv")
            split(FIRST["ukv"] + 1)
            root_of("ckv")
            gain_hi("cq")
            split(FIRST["ukv"] + 2)
            act.wait_ge(k_rotated, 1)
            a(lk[64:96, :, :], kpe_raw[64:96, :].rearrange("p (a t) -> p a t", a=1).broadcast_to([32, MH, T]),
              ACT.Copy).then_inc(rope_ready, 1)
            root_of("cq")
            split(FIRST["uq"] + 1)
            for h in range(MH + 1):
                if h < MH:
                    for i in range(NB):
                        act.wait_ge(lmax_done, 4 * h + i + 1)
                        if h >= 2:
                            act.wait_ge(lt_ready, 4 * (h - 1))
                        b = bank[4 + LQ_AT[("S", h, i)] % 3]
                        n = (i + 1) * P
                        a(lp[:, h % 2, QOFF[i]:QOFF[i] + n], b[:, 0:n], ACT.Exp, bias=nmax[:, h % 2, i:i + 1],
                          accum_out=rsum[:, h % 2, i:i + 1]).then_inc(lexp_done, 1)
                    if h % 2 == 0 and h // 2 + 2 <= MH // 2:
                        split(FIRST["uq"] + h // 2 + 2)
                    act.wait_ge(rinv_ready, h + 1)
                    for i in range(NB):
                        v = lp[:, h % 2, QOFF[i]:QOFF[i] + (i + 1) * P]
                        a(v, v, ACT.Copy, scale=rinv[:, h % 2, i:i + 1]).then_inc(lp_ready, 1)
                if h and h % 2 == 0:
                    act.wait_ge(lo_ready, h)
                    a(h_hi[:, h // 2 - 1, :], stat[:, :], ACT.Copy).then_inc(lo_hi, 1)
            splits("mla_o")
            cross(1)
            norm_squares("final1")
            norm_squares("second")
            norm_hi("second")
            for s in range(13):
                n = FIRST["w_in"] + s
                split(n + 1)
                if s in (6, 7, 11, 12):
                    for j in range(2):
                        act.wait_ge(tile_free, TILE0["w_in"] + 2 * s + j + 1)
                        g = (sg_T if s < 8 else wg_T)[:, 2 * ((s - 6) if s < 8 else (s - 11)) + j, :]
                        a(g, g, ACT.Silu).then_inc(gate_act, 1)
            chain = [0]
            def softplus_log(h):
                for j in range(NB - 1, -1, -1):
                    act.wait_ge(z_ready, 4 * h + NB - j)
                    wait(act, c_ready, 4 * (h - 1))
                    a(softplus[h % 2][:, j, j * P:], bank[4 * (h % 2) + j][:, 0:(NB - j) * P], ACT.Abs).then_inc(abs_done, 1)
                for j in range(NB - 1, -1, -1):
                    act.wait_ge(abs_done, 4 * h + NB - j)
                    v = softplus[h % 2][:, j, j * P:]
                    a(v, v, ACT.Exp, scale=-1.0).then_inc(exp_done, 1)
                for j in range(NB - 1, -1, -1):
                    act.wait_ge(exp_done, 4 * h + NB - j)
                    v = softplus[h % 2][:, j, j * P:]
                    a(v, v, ACT.Ln, bias=ones[:, 0:1]).then_inc(ln_done, 1)

            softplus_log(0)
            for h in range(SBH):
                if h + 1 < SBH:
                    softplus_log(h + 1)
                for j in range(NB - 1, -1, -1):
                    act.wait_ge(c_ready, 4 * h + NB - j)
                    wait(act, so_ready, h)
                    a(sw_T[:, j, j * P:], bank[4 * (h % 2) + j][:, 0:(NB - j) * P], ACT.Exp).then_inc(w_ready, 1)
                act.wait_ge(so_scaled, h + 1)
                r0 = (h % 2) * HD
                a(h_hi[r0:r0 + HD, h // 2, :], fb[h % 2][r0:r0 + HD, :], ACT.Copy).then_inc(so_hi, 1)
            for h in range(SWH + 2):
                if h < SWH:
                    act.wait_ge(wmax_done, h + 1)
                    for q in range(NB):
                        c0 = P if q == 0 else 0
                        v = wp[:, h % 2, q, c0:]
                        a(v, v, ACT.Exp, bias=nmax[:, h % 2, q:q + 1],
                          accum_out=rsum[:, h % 2, q:q + 1]).then_inc(wexp_done, 1)
                    a(esink[:, h % 2, :], nmax[:, h % 2, :], ACT.Exp, bias=sinks[:, h:h + 1]).then_inc(wexp_done, 1)
                if h >= 2:
                    e = h - 2
                    r0 = (e % 2) * HD
                    act.wait_ge(wo_scaled, e + 1)
                    a(h_hi[r0:r0 + HD, 4 + e // 2, :], fb[e % 2][r0:r0 + HD, :], ACT.Copy).then_inc(wo_hi, 1)
                if h < SWH:
                    act.wait_ge(wrinv_ready, h + 1)
                    for q in range(NB):
                        v = wp[:, h % 2, q, P if q == 0 else 0:]
                        a(v, v, ACT.Copy, scale=rinv[:, h % 2, q:q + 1]).then_inc(wp_ready, 1)
            splits("w_out")
            norm_squares("final2")
            for t in range(NB):
                act.wait_ge(out_tr, 2 * t + 1)
                a(x_nat[:, t, 0:512], bank[2 * t][:, :], ACT.Copy).then_inc(out_copied_a, 1)

        @block.vector
        def _(dve):
            tt, ts, stt, cp = nc.vector.tensor_tensor, nc.vector.tensor_scalar, nc.vector.scalar_tensor_tensor, \
                nc.vector.tensor_copy
            step = [0]

            def link(ins_):
                step[0] += 1
                ins_.then_inc(dve_step, 1)
                dve.wait_ge(dve_step, step[0])

            def low(lo_, v, hi):
                return tt(lo_, v, hi.bitcast(f32), SUB)

            def split(n, step_=0):
                if isinstance(step_, int) and (n + step_ >= NSLAB or is_ada(n + step_)):
                    return
                dve.wait_ge(hi_done, splits_before(n) + 1 + step_)
                c = slab_columns(n)
                low(w_lo[n % 2][:, 0:c], raw[n % 2][:, 0:c], w_hi[n % 2][:, 0:c]).then_inc(lo_done, 1)

            def splits(stage):
                for s in range(COUNT[stage]):
                    split(FIRST[stage] + s + 1)

            def root(name):
                dve.wait_ge(sqrt_done, NORMI[name] + 1)
                r = root_to(name)[:, 0:NORM_SRC[name][1]]
                link(nc.vector.reciprocal(r, r))

            def norm_apply(name):
                root(name)
                src, N, _ = NORM_SRC[name]
                n0, nt = SPLIT0[name], NORMT[name]
                hi, lo_ = NORM_DST.get(name, (h_hi, h_lo))
                for i in range(nt + 1):
                    if i < nt:
                        wait(dve, split_lo, n0 + max(i - 1, 0))
                        if name == "second":
                            link(stt(fb[i % 2][:, :], src(i), gs2[:, i:i + 1], rstd[:, :], MUL, MUL))
                            ts(fb[i % 2][:, :], fb[i % 2][:, :], mod[:, i:i + 1], None, ADD).then_inc(scaled, 1)
                        else:
                            g, o = NORM_GAIN[name]
                            stt(fb[i % 2][:, :], src(i), param(g, o + i), rstd[:, :], MUL, MUL).then_inc(scaled, 1)
                    if i:
                        dve.wait_ge(split_hi, n0 + i)
                        low(lo_[:, i - 1, :], fb[(i - 1) % 2][:, :], hi[:, i - 1, :]).then_inc(split_lo, 1)

            def norm_in_place(name):
                root(name)
                g, o = NORM_GAIN[name]
                for i in range(8):
                    stt(x[:, i, :], x[:, i, :], param(g, o + i), rstd[:, :], MUL, MUL).then_inc(fin_done, 1)

            def gain_low(name):
                g, o = NORM_GAIN[name]
                src, (hi, lo_) = NORM_SRC[name][0], NORM_DST.get(name, (h_hi, h_lo))
                for i in range(NORMT[name]):
                    dve.wait_ge(split_hi, SPLIT0[name] + i + 1)
                    stt(lo_[:, i, :], src(i), param(g, o + i), hi[:, i, :].bitcast(f32), MUL, SUB).then_inc(split_lo, 1)

            def memory_low(layer, tiles):
                for i in tiles:
                    dve.wait_ge(mem_hi, 8 * layer + i + 1)
                    stt(m_lo[:, i, :], memn[:, i, :], param("norm_mem_g", 8 * layer + i), m_hi[:, i, :].bitcast(f32),
                        MUL, SUB).then_inc(mem_lo, 1)

            def pre_copy(r):
                dve.wait_ge(pre_ready, r + 1)
                b = bank[4 + r % 4]
                if r < 4:
                    cp(prm[:, r, 0:PROWS[r]], b[:, 0:PROWS[r]]).then_inc(pre_done, 1)
                elif r < 4 + DT:
                    cp(x[:, r - 4, :], b[:, :]).then_inc(pre_done, 1)
                else:
                    cp(memn[:, r - 4 - DT, :], b[:, 0:MEM]).then_inc(pre_done, 1)

            for r in range(4):
                pre_copy(r)
            dve.wait_ge(masks_ready, 5)
            cp(ident_b[:, :], ident[:, :])
            cp(later_b[:, :], later[:, :])
            for r in range(4, 4 + DT):
                pre_copy(r)
            split(0)
            norm_apply("mix0")

            CONV = [(k, i) for pair in ((0, 1), (2, 3)) for k in range(CK) for i in pair]
            conv_at, n_conv = {}, 0
            for k, i in CONV:
                if k < CK - 1:
                    n_conv += 1
                    conv_at[(k, i)] = n_conv
            todo = list(CONV)

            def conv(count):
                for _ in range(min(count, len(todo))):
                    k, i = todo.pop(0)
                    src, o, w = glu[:, i, k:k + T], cv[:, i, :], param("conv_dw_w", 4 * k + i)
                    if k == 0:
                        m = ts(o, src, w, param("conv_dw_b", i), MUL, ADD)
                    else:
                        dve.wait_ge(conv_step, conv_at[(k - 1, i)])
                        m = stt(o, src, w, o, MUL, ADD)
                    m.then_inc(cv_ready if k == CK - 1 else conv_step, 1)

            T0 = TILE0["pc_in"]
            for s in range(6):
                n = FIRST["pc_in"] + s
                split(n + 1)
                if s == 0:
                    for r in range(4 + DT, 4 + 2 * DT):
                        pre_copy(r)
                    dve.wait_ge(masks_ready, 5)
                    nc.vector.reciprocal(inv16[:, :], inv16[:, :]).then_inc(consts_done, 1)
                for j in range(2):
                    tile = 2 * s + j
                    b = bank[(T0 + tile) % 4]
                    if s in (1, 3):
                        dve.wait_ge(slab_half, 2 * n + 1 + j)
                        dve.wait_ge(sig_done, s + j)
                        if s == 1 and j == 0:
                            dve.wait_ge(pads_ready, 2)
                        tt(glu[:, s - 1 + j, CK - 1:], sq[j][:, :], b[:, :], MUL).then_inc(tile_free, 3 if j else 1)
                    elif s >= 4:
                        dve.wait_ge(slab_half, 2 * n + 1 + j)
                        cp(u_pad[:, 2 * (s - 4) + j, 16:], b[:, :]).then_inc(tile_free, 1)
                if s == 1:
                    dve.wait_ge(tile_free, T0 + 4)
                if s == 3:
                    dve.wait_ge(tile_free, T0 + 8)
                if s == 2:
                    root("mem")
                    for i in range(DT):
                        tt(memn[:, i, :], memn[:, i, :], rstd[:, 0:MEM], MUL).then_inc(memn_done, 1)
                    dve.wait_ge(pwhi_done, 1)
                    low(pw_lo[:, :, :], pw_raw[:, :, :], pw_hi[:, :, :]).then_inc(pwlo_done, 1)
                if s in (4, 5):
                    memory_low(0, range(4 * (s - 4), 4 * (s - 3)))
                conv([0, 0, 6, 11, 11, 11][s])

            def memory_out(layer, after=lambda s: None):
                stage = f"kv{layer}"
                for s in range(8):
                    n = FIRST[stage] + s
                    split(n + 1)
                    for j in range(2):
                        dve.wait_ge(slab_half, 2 * n + 1 + j)
                        b = bank[(TILE0[stage] + 2 * s + j) % 4][:, 0:256]
                        o = kT[:, 2 * s + j, :] if s < 4 else vN[:, j, (s - 4) * 256:(s - 3) * 256]
                        cp(o, b).then_inc(tile_free, 1)
                    after(s)

            def mixer_meanwhile(s):
                if s % 2:
                    g = s // 2
                    dve.wait_ge(poolhi_done, g + 1)
                    low(pooled_lo[:, g, :], pooled[:, :], pooled_hi[:, g, :]).then_inc(poollo_done, 1)
                conv(4)

            memory_out(0, mixer_meanwhile)
            for g in range(5):
                if g < 4:
                    dve.wait_ge(pool_out, g + 1)
                    wait(dve, y_lo, g - 1)
                    ts(fb[g % 2][:, :], bank[4 + g % 2][:, :], param("pool_scale", g), None, MUL).then_inc(ya_scaled, 1)
                if g:
                    dve.wait_ge(ya_hi, g)
                    low(h_lo[:, g - 1, :], fb[(g - 1) % 2][:, :], h_hi[:, g - 1, :]).then_inc(y_lo, 1)
            conv(len(todo))
            dve.wait_ge(ada_cols, COUNT["ada"])
            tt(mod[:, :], bank[6][:, 0:24], prm[:, 1, 0:24], ADD).then_inc(mod_done, 1)
            dve.wait_ge(mod_done, 1)
            g0 = PROW["norm_g_2"][1]
            link(ts(gs2[:, :], mod[:, 8:16], 1.0, None, ADD))
            link(tt(gs2[:, :], gs2[:, :], prm[:, 0, g0:g0 + DT], MUL))
            split(FIRST["pc_out"])
            dve.wait_ge(cv_summed, 4)
            for i in range(4):
                dve.wait_ge(cv_ready, i + 1)
                stt(cv[:, i, :], bank[6][:, :], -1.0 / (4 * P), cv[:, i, :], MUL, ADD).then_inc(xc_ready, 1)
            dve.wait_ge(ln_sqrt, 1)
            link(nc.vector.reciprocal(rstd[:, :], rstd[:, :]))
            for i in range(4):
                tt(cv[:, i, :], cv[:, i, :], rstd[:, :], MUL).then_inc(ln_norm, 1)
            for i in range(4):
                dve.wait_ge(yb_hi, i + 1)
                low(h_lo[:, 4 + i, :], cv[:, i, :], h_hi[:, 4 + i, :]).then_inc(y_lo, 1)

            def add_to_x(stage):
                for s in range(4):
                    n = FIRST[stage] + s
                    split(n + 1)
                    for j in range(2):
                        i = 2 * s + j
                        dve.wait_ge(slab_half, 2 * n + 1 + j)
                        tt(x[:, i, :], x[:, i, :], bank[(TILE0[stage] + i) % 4][:, :], ADD).then_inc(tile_free, 1)

            add_to_x("pc_out")

            def cross(layer):
                gain_low(f"xa{layer}")
                stage = f"wq{layer}"
                for s in range(4):
                    n = FIRST[stage] + s
                    split(n + 1)
                    if s == 0:
                        root(f"xa{layer}")
                    for j in range(2):
                        i = 2 * s + j
                        dve.wait_ge(slab_half, 2 * n + 1 + j)
                        stt(qT[:, i, :], bank[(TILE0[stage] + i) % 4][:, :], XHD ** -0.5, rstd[:, :], MUL, MUL)\
                            .then_inc(tile_free, 1)
                    if layer and s:
                        memory_low(1, ((0, 1, 2), (3, 4, 5), (6, 7))[s - 1])
                if layer:
                    memory_out(1)
                for h in range(XH + 1):
                    e = h - 1
                    if h < XH:
                        for i in range(2):
                            dve.wait_ge(xs_ready, 8 * layer + 2 * h + i + 1)
                            b = bank[4 + XA_AT[("S", h, i)] % 4]
                            nc.vector.tensor_reduce(nmax[:, h % 2, 2 * i:2 * i + 2],
                                                    b[:, :].rearrange("p (a m) -> p a m", a=2), AX.X, MAX,
                                                    negate=True).then_inc(xmax_done, 1)
                        dve.wait_ge(xexp_done, 16 * layer + 4 * h + 4)
                        wait(dve, xp_ready, 16 * layer + 4 * (h - 1) if h >= 2 else 0)
                        nc.vector.reciprocal(rinv[:, h % 2, :], rsum[:, h % 2, :]).then_inc(xrinv_ready, 1)
                    if h:
                        for j in range(2):
                            dve.wait_ge(xt_ready, 8 * layer + 2 * e + j + 1)
                            wait(dve, xo_ready, 8 * layer + 2 * (e - 1) if e >= 2 else 0)
                            cp(xpT[:, e % 2, j, :], bank[4 + XA_AT[("T", e, j)] % 4][:, :]).then_inc(xt_done, 1)
                        for d in range(2):
                            i = 2 * e + d
                            dve.wait_ge(xo_hi, 8 * layer + i + 1)
                            low(h_lo[:, i, :], bank[4 + XA_AT[("O", e, d)] % 4][:, :], h_hi[:, i, :]).then_inc(xo_lo, 1)
                add_to_x(f"wo{layer}")
                gain_low(f"ffn{layer}")
                up, down = f"up{layer}", f"down{layer}"
                n, tile = FIRST[up], TILE0[up]

                def up_step(it, first=False):
                    done = 2 * it + FT * layer
                    split(n + 1, 2 * it)
                    if first:
                        root(f"ffn{layer}")
                    for j in range(2):
                        hold(dve, taps_done, done + (j - 1))
                        dve.wait_ge(slab_half, 4 * it + (2 * n + 1 + j))
                        tt(sq[j][:, :], bank[(tile + j) % 4][:, :], rstd[:, :], MUL).then_inc(tile_free, 1)
                    for j in range(2):
                        dve.wait_ge(tap2, done + (j + 1))
                        stt(fb[j][:, 1:], sq[j][:, :T - 1], tap(layer, 1, j, 2 * it), fb[j][:, 1:], MUL, ADD).then_inc(tap1, 1)
                        dve.wait_ge(tap1, done + (j + 1))
                        stt(fb[j][:, 2:], sq[j][:, :T - 2], tap(layer, 0, j, 2 * it), fb[j][:, 2:], MUL, ADD)\
                            .then_inc(taps_done, 1)
                    split(n + 2, 2 * it)
                    for j in range(2):
                        dve.wait_ge(gate_silu, done + (j + 1))
                        tt(fb[j][:, :], fb[j][:, :], rstd[:, :], MUL).then_inc(silu_scaled, 1)
                    for j in range(2):
                        hold(dve, silu_scaled, done + (j + 1))
                        dve.wait_ge(slab_half, 4 * it + (2 * n + 3 + j))
                        tt(fb[j][:, :], fb[j][:, :], bank[(tile + 2 + j) % 4][:, :], MUL).then_inc(tile_free, 1)
                    for j in range(2):
                        dve.wait_ge(g_hi_done, done + (j + 1))
                        i = bass.ds(2 * it + j, 1)
                        low(g_lo[:, i, :].rearrange("p a t -> p (a t)"), fb[j][:, :],
                            g_hi[:, i, :].rearrange("p a t -> p (a t)")).then_inc(g_lo_done, 1)

                up_step(0, first=True)
                with dve.Fori(1, COUNT[up] // 2) as it:
                    up_step(it)
                n, tile = FIRST[down], TILE0[down]
                with dve.Fori(0, 2) as it:
                    for s in range(6):
                        split(n + s + 1, 6 * it)
                        if s % 3 == 2:
                            for j in range(2):
                                i = 2 * (s // 3) + j
                                dve.wait_ge(slab_half, 12 * it + (2 * (n + s) + 1 + j))
                                v = x[:, bass.ds(4 * it + i, 1), :].rearrange("p a t -> p (a t)")
                                tt(v, v, bank[(tile + i) % 4][:, :], ADD).then_inc(tile_free, 1)

            cross(0)

            gain_low("mix1")
            rr = slice(64, 96)
            s_, c_, t_ = r_sin[rr, :], r_cos[rr, :], fb[0][rr, :]

            def angles():
                dve.wait_ge(pos_loaded, 16)
                dve.wait_ge(small_loaded, 32)
                link(cp(s_, pos_i[rr, :]))
                link(ts(c_, s_, rope_c[rr, 0:1], None, MUL))

            def reduce(o, shift):
                link(ts(t_, c_, 1.0 / TWO_PI, shift, MUL, ADD))
                link(ts(t_, t_, ROUNDER, None, ADD))
                link(ts(t_, t_, -ROUNDER, None, ADD))
                link(stt(o, t_, -PI2_A, c_, MUL, ADD))
                link(stt(o, t_, -PI2_B, o, MUL, ADD))
                link(stt(o, t_, -PI2_C, o, MUL, ADD))
                link(ts(o, o, shift * TWO_PI, 3.1415925, ADD, ALU.min))
                ts(o, o, -3.1415925, None, MAX).then_inc(angle_ready, 1)
                dve.wait_ge(angle_ready, 1 if shift == 0.0 else 2)

            T0 = TILE0["dq"]
            for s in range(3):
                n = FIRST["dq"] + s
                split(n + 1)
                if s == 0:
                    root("mix1")
                for j in range(2):
                    i = 2 * s + j
                    dve.wait_ge(slab_half, 2 * n + 1 + j)
                    b = bank[(T0 + i) % 4]
                    if i < 3:
                        tt(cq_raw[:, i, :], b[:, :], rstd[:, :], MUL).then_inc(tile_free, 1)
                    elif i < 5:
                        tt(ckv_raw[:, i - 3, :], b[:, :], rstd[:, :], MUL).then_inc(tile_free, 1)
                    else:
                        tt(kpe_raw[rr, :], b[rr, :], rstd[rr, :], MUL).then_inc(tile_free, 1)
                if s == 0:
                    angles()
                    reduce(s_, 0.0)
                if s == 1:
                    reduce(c_, 0.25)
            gain_low("ckv")
            for s in range(2):
                n = FIRST["ukv"] + s
                split(n + 1)
                if s == 0:
                    root("ckv")
                    link(nc.vector.reciprocal(kv_col[:, :], kv_col[:, :]))
                for i in range(12):
                    if i < 11:
                        dve.wait_ge(kv_tile, 11 * s + i + 1)
                    else:
                        dve.wait_ge(slab_half, 2 * n + 2)
                    b = bank[(TILE0["ukv"] + 12 * s + i) % 4]
                    if i < 8:
                        tt(lk[0:NOPE, 8 * s + i, :], b[0:NOPE, :], fb[1][0:NOPE, :], MUL).then_inc(tile_free, 1)
                    else:
                        ts(lv[:, i - 8, 512 * s:512 * s + 512], b[:, :], kv_col[:, i - 8:i - 7], None, MUL)\
                            .then_inc(tile_free, 1)
                if s:
                    continue
                gain_low("cq")
                swap = list(range(16, 32)) + list(range(16))
                dve.wait_ge(sin_done, 2)
                dve.wait_ge(tile_free, T0 + 6)
                k_ = kpe_raw[rr, :]
                link(ts(s_, s_, rope_c[rr, 1:2], None, MUL))
                link(nc.vector.stream_shuffle(t_, k_, swap))
                link(tt(t_, t_, s_, MUL))
                link(tt(k_, k_, c_, MUL))
                tt(k_, k_, t_, ADD).then_inc(k_rotated, 1)
            root("cq")
            split(FIRST["uq"] + 1)

            def queries(pair):
                n = FIRST["uq"] + pair
                for j in range(2):
                    h = 2 * pair + j
                    dve.wait_ge(slab_half, 2 * n + 1 + j)
                    wait(dve, ls_ready, 4 * (h - 3))
                    stt(lq[0:QKD, h % 4, :], bank[(TILE0["uq"] + h) % 4][0:QKD, :], MLA_SCALE, rstd[0:QKD, :], MUL, MUL)\
                        .then_inc(tile_free, 1)
                    dve.wait_ge(tile_free, TILE0["uq"] + h + 1)
                    wait(dve, q_ready, h - 1)
                    nc.vector.stream_shuffle(lsh[h % 2][rr, :], lq[rr, h % 4, :], swap).then_inc(q_base, 1)

            queries(0)
            for h in range(MH + 1):
                e = h - 1
                if h < MH:
                    for i in range(NB):
                        dve.wait_ge(ls_ready, 4 * h + i + 1)
                        nc.vector.tensor_reduce(nmax[:, h % 2, i:i + 1], bank[4 + LQ_AT[("S", h, i)] % 3][:, 0:(i + 1) * P],
                                                AX.X, MAX, negate=True).then_inc(lmax_done, 1)
                    dve.wait_ge(lexp_done, 4 * h + 4)
                    wait(dve, lp_ready, 4 * (h - 1))
                    nc.vector.reciprocal(rinv[:, h % 2, :], rsum[:, h % 2, :]).then_inc(rinv_ready, 1)
                    if h % 2 == 0 and h // 2 + 2 <= MH // 2:
                        split(FIRST["uq"] + h // 2 + 2)
                if h:
                    for j in range(NB):
                        dve.wait_ge(lt_ready, 4 * e + j + 1)
                        wait(dve, lo_ready, e)
                        n = (NB - j) * P
                        cp(lpT[:, KOFF[j]:KOFF[j] + n], bank[4 + LQ_AT[("T", e, j)] % 3][:, 0:n]).then_inc(lt_done, 1)
                    if e % 2:
                        dve.wait_ge(lo_hi, e // 2 + 1)
                        low(h_lo[:, e // 2, :], stat[:, :], h_hi[:, e // 2, :]).then_inc(lo_lo, 1)
                if h % 2 == 0 and h // 2 + 1 < MH // 2:
                    queries(h // 2 + 1)
            add_to_x("mla_o")
            cross(1)
            norm_in_place("final1")
            norm_apply("second")

            for s in range(13):
                n = FIRST["w_in"] + s
                split(n + 1)
                for j in range(2):
                    b = bank[(TILE0["w_in"] + 2 * s + j) % 4]
                    dve.wait_ge(slab_half, 2 * n + 1 + j)
                    i = 2 * s + j
                    if s < 2:
                        m = ts(sq_T[:, i, :], b[:, :], HSCALE, None, MUL)
                    elif s < 4:
                        m = cp(sk_T[:, i - 4, :], b[:, :])
                    elif s < 6:
                        m = cp(sv_N[:, 2 * j:2 * j + 2, (s - 4) * 256:(s - 3) * 256],
                               b[:, :].rearrange("p (a n) -> p a n", a=2))
                    elif s < 8:
                        m = cp(sg_T[:, i - 12, :], b[:, :])
                    elif s < 10:
                        m = ts(wq_T[:, i - 16, :], b[:, :], HSCALE, None, MUL)
                    elif i == 20:
                        cp(wk_T[0:HD, 0, :], b[0:HD, :])
                        m = cp(wk_T[HD:, 1, :], b[HD:, :])
                    elif i == 21:
                        m = cp(wv_N[:, :, :], b[:, :].rearrange("p (a n) -> p a n", a=NB))
                    else:
                        m = cp(wg_T[:, i - 22, :], b[:, :])
                    m.then_inc(tile_free, 1)

            dve.wait_ge(sb_masks, 5)
            dve.wait_ge(gate_act, 4)
            def softplus_of(h):
                for j in range(NB - 1, -1, -1):
                    v = softplus[h % 2][:, j, j * P:]
                    dve.wait_ge(ln_done, 4 * h + NB - j)
                    link(stt(v, bank[4 * (h % 2) + j][:, 0:(NB - j) * P], 0.0, v, MAX, ADD))
                    tt(v[:, 0:P], v[:, 0:P], before[:, :], MUL).then_inc(sp_ready, 1)

            softplus_of(0)
            for h in range(SBH):
                if h + 1 < SBH:
                    softplus_of(h + 1)
                r0 = (h % 2) * HD
                dve.wait_ge(so_ready, h + 1)
                o = fb[h % 2][r0:r0 + HD, :]
                tt(o, bank[4 * (h % 2) + 3][r0:r0 + HD, :], sg_T[r0:r0 + HD, h // 2, :], MUL).then_inc(so_scaled, 1)
                dve.wait_ge(so_hi, h + 1)
                low(h_lo[r0:r0 + HD, h // 2, :], o, h_hi[r0:r0 + HD, h // 2, :]).then_inc(so_lo, 1)

            for b in range(2):
                link(nc.vector.memset(wp[:, b, 0, 0:P], NEG))
            dve.wait_ge(gate_act, 8)
            for h in range(SWH + 2):
                if h < SWH:
                    slope = 2.0 ** (-8.0 * (h + 1) / SWH)
                    for q in range(NB):
                        c0 = P if q == 0 else 0
                        dve.wait_ge(ws_ready, 2 * h + q // 2 + 1)
                        wait(dve, wt_ready, 2 * (h - 1) if h >= 2 else 0)
                        b = bank[4 + SW_AT[("S", h, q // 2)] % 4]
                        stt(wp[:, h % 2, q, c0:], relm[:, c0:], -slope, b[:, (q % 2) * 2 * P + c0:(q % 2 + 1) * 2 * P],
                            MUL, ADD).then_inc(wl_done, 1)
                    dve.wait_ge(wl_done, 4 * h + 4)
                    link(nc.vector.tensor_reduce(nmax[:, h % 2, :], wp[:, h % 2, :, :], AX.X, MAX))
                    ts(nmax[:, h % 2, :], nmax[:, h % 2, :], sinks[:, h:h + 1], -1.0, MAX, MUL).then_inc(wmax_done, 1)
                if h >= 2:
                    e = h - 2
                    r0 = (e % 2) * HD
                    dve.wait_ge(wo_ready, e + 1)
                    o = fb[e % 2][r0:r0 + HD, :]
                    tt(o, bank[4 + SW_AT[("O", e, 0)] % 4][r0:r0 + HD, :], wg_T[r0:r0 + HD, e // 2, :], MUL)\
                        .then_inc(wo_scaled, 1)
                if 1 <= h <= SWH:
                    e = h - 1
                    flat = wpT[:, :, :].rearrange("p a n -> p (a n)")
                    for b in range(2):
                        dve.wait_ge(wt_ready, 2 * e + b + 1)
                        wait(dve, wo_ready, e)
                        n = 4 * P - b * P
                        cp(flat[:, b * 512:b * 512 + n], bank[4 + SW_AT[("T", e, b)] % 4][:, 0:n]).then_inc(wt_done, 1)
                if h < SWH:
                    dve.wait_ge(wexp_done, 5 * h + 5)
                    link(tt(rsum[:, h % 2, :], rsum[:, h % 2, :], esink[:, h % 2, :], ADD))
                    wait(dve, wp_ready, 4 * (h - 1) if h >= 2 else 0)
                    nc.vector.reciprocal(rinv[:, h % 2, :], rsum[:, h % 2, :]).then_inc(wrinv_ready, 1)
                if h >= 2:
                    e = h - 2
                    r0 = (e % 2) * HD
                    dve.wait_ge(wo_hi, e + 1)
                    low(h_lo[r0:r0 + HD, 4 + e // 2, :], fb[e % 2][r0:r0 + HD, :], h_hi[r0:r0 + HD, 4 + e // 2, :])\
                        .then_inc(wo_lo, 1)
            for s in range(4):
                n = FIRST["w_out"] + s
                split(n + 1)
                for j in range(2):
                    i = 2 * s + j
                    dve.wait_ge(slab_half, 2 * n + 1 + j)
                    stt(x[:, i, :], bank[(TILE0["w_out"] + i) % 4][:, :], mod[:, 16 + i:17 + i], x[:, i, :], MUL, ADD)\
                        .then_inc(tile_free, 1)
            norm_in_place("final2")
            for t in range(NB):
                dve.wait_ge(out_tr, 2 * t + 2)
                cp(x_nat[:, t, 512:], bank[2 * t + 1][:, :]).then_inc(out_copied, 1)


_INS = ["x", "mem", "positions", "norm_mix_g", "norm_xa_g", "norm_mem_g", "xa_wq", "xa_wkv", "xa_wo", "norm_ffn_g",
        "ffn_w_up", "ffn_conv_w", "ffn_conv_b", "ffn_w_down", "pc_w_in", "pool_w", "pool_scale", "conv_dw_w",
        "conv_dw_b", "conv_ln_g", "conv_ln_b", "pc_w_out", "mla_w_dq_dkv", "mla_q_norm_g", "mla_w_uq",
        "mla_kv_norm_g", "mla_w_ukv", "mla_w_o", "final_norm_g", "c_2", "w_ada_2", "b_ada_2", "norm_g_2", "w_in_2",
        "sinks_2", "w_out_2", "final_g_2"]


def kernel(**inputs):
    import numpy as _np
    import concourse.bacc as _bacc
    from concourse import mybir as _mybir
    from concourse.bass_utils import run_bass_kernel_spmd as _run

    nc = _bacc.Bacc("TRN2", target_bir_lowering=False, num_devices=1)
    arrays, args = {}, {}
    given = {name: _np.ascontiguousarray(inputs[name]) for name in _INS}
    half = ROPE // 2
    freq = 1.0 / 10000.0 ** (_np.arange(0, ROPE, 2, dtype=_np.float64) / ROPE)
    given["rope_const"] = _np.stack([_np.tile(freq, 2), _np.repeat([-1.0, 1.0], half)], 1).astype(_np.float32)
    for name, a in given.items():
        arrays[f"in_{name}_dram"] = a
        args[name] = nc.dram_tensor(f"in_{name}_dram", a.shape, _mybir.dt.from_np(a.dtype), kind="ExternalInput").ap()
    out = nc.dram_tensor("out_0_dram", (1, T, D), _mybir.dt.float32, kind="ExternalOutput").ap()
    build(nc, args, out)
    r = _run(nc, [arrays], core_ids=[0])
    return r.results[0]["out_0_dram"]
```

```python
import concourse.bass as bass
from concourse import mybir
from contextlib import ExitStack

P = 128
D = 1024
T = 512
DT = D // P
MEM = 256
XH = 4
XHD = D // XH
FF = 2816
FT = FF // P
CK = 31
MH = 16
NOPE, ROPE, VD = 64, 32, 64
QL, KVL = 384, 256
QKD = NOPE + ROPE
MLA_SCALE = QKD ** -0.5
SBH = SWH = 8
HD = 64
HSCALE = HD ** -0.5
WINDOWS = (2, 4, 8, 16)
EPS = 1e-6
NEG = -1e30
NB = T // P
SLAB = 2048

STAGES = [("pc_in", 6), ("kv0", 8), ("ada", 12), ("pc_out", 4), ("wq0", 4), ("wo0", 4), ("up0", 22),
          ("down0", 12), ("dq", 3), ("ukv", 2), ("uq", 8), ("mla_o", 4), ("wq1", 4), ("kv1", 8), ("wo1", 4),
          ("up1", 22), ("down1", 12), ("w_in", 13), ("w_out", 4)]
FIRST, COUNT = {}, {}
NSLAB = 0
for _name, _count in STAGES:
    FIRST[_name], COUNT[_name] = NSLAB, _count
    NSLAB += _count


def splits_before(n):
    return n - min(max(n - FIRST["ada"], 0), COUNT["ada"])


def slab_columns(n):
    if 0 <= n - FIRST["uq"] < COUNT["uq"]:
        return QL // P * 2 * QKD
    if n == FIRST["dq"] + 1:
        return DT * 160
    for down in ("down0", "down1"):
        if 0 <= n - FIRST[down] < COUNT[down] and (n - FIRST[down]) % 3 == 2:
            return (FT - 16) * 256
    return SLAB


DQ_SLABS = (1, 2, 0)
DQ_TILES = (2, 3, 4, 5, 0, 1)


def is_ada(n):
    return 0 <= n - FIRST["ada"] < COUNT["ada"]


POOL_AT = (2, 4, 6, 7)

TILES = {"ada": 0, "down0": 8, "down1": 8, "ukv": 24}
TILE0 = {}
_t = 0
for _name, _count in STAGES:
    TILE0[_name] = _t
    _t += TILES.get(_name, 2 * _count)

NORMS = [("mix0", 8), ("mem", 8), ("xa0", 8), ("ffn0", 8), ("mix1", 8), ("ckv", 2), ("cq", 3), ("xa1", 8), ("ffn1", 8)]
POOLED = ["mem", "xa0", "ffn0", "mix1", "ckv", "cq", "xa1", "ffn1"]
NORMI = {_name: _i for _i, (_name, _count) in enumerate(NORMS)}
NORMT = dict(NORMS)

PROW = {"norm_mix_g": (0, 0), "norm_xa_g": (0, 16), "norm_mem_g": (0, 32), "norm_ffn_g": (0, 48),
        "final_norm_g": (0, 64), "norm_g_2": (0, 72), "final_g_2": (0, 80), "pool_scale": (0, 88),
        "conv_dw_b": (0, 92), "conv_ln_g": (0, 96), "conv_ln_b": (0, 100), "mla_q_norm_g": (0, 104),
        "mla_kv_norm_g": (0, 107), "c_2": (0, 109), "b_ada_2": (1, 0), "ffn_conv_w1": (1, 24),
        "conv_dw_w": (2, 0), "ffn_conv_w0": (3, 0), "ffn_conv_b": (3, 66)}
PROWS = (117, 90, 124, 110)

TWO_PI = 6.283185307179586
PI2_A = 6.28125
PI2_B = 0.0019350051879882812
PI2_C = TWO_PI - PI2_A - PI2_B
ROUNDER = 12582912.0

SPLITS = ["mix0", "xa0", "ffn0", "mix1", "ckv", "cq", "xa1", "ffn1", "second"]
SPLIT0 = {}
_t = 0
for _name in SPLITS:
    SPLIT0[_name] = _t
    _t += NORMT.get(_name, DT)


def build(nc, ins, out):
    f32 = mybir.dt.float32
    f32r = mybir.dt.float32r
    i32 = mybir.dt.int32
    ALU = mybir.AluOpType
    ACT = mybir.ActivationFunctionType
    AX = mybir.AxisListType
    MUL, ADD, SUB, MAX = ALU.mult, ALU.add, ALU.subtract, ALU.max

    ctx = ExitStack()
    with ctx:
        top = [(nc.sbuf_base + 31) // 32 * 32]

        def at(name, shape, offset, dt=f32):
            return nc.alloc_sbuf_tensor_at(name, shape, dt, offset=offset)

        def size(shape):
            n = 4
            for s in shape[1:]:
                n *= s
            return (n + 31) // 32 * 32

        def sb(name, shape, dt=f32):
            here = top[0]
            top[0] += size(shape)
            return at(name, shape, here, dt)

        x = sb("x", [P, DT, T])
        h_hi = sb("h_hi", [P, DT, T], f32r)
        h_lo = sb("h_lo", [P, DT, T], f32r)
        raw = [sb(f"w_raw{i}", [P, SLAB]) for i in range(2)]
        w_hi = [sb(f"w_hi{i}", [P, SLAB], f32r) for i in range(2)]
        w_lo = [sb(f"w_lo{i}", [P, SLAB], f32r) for i in range(2)]
        memn = sb("memn", [P, DT, MEM])
        fb = [sb(f"fb{i}", [P, T]) for i in range(2)]
        sq = [sb(f"sq{i}", [P, T]) for i in range(2)]
        rstd = sb("rstd", [P, T])
        prm = sb("prm", [P, 4, P])
        ident = sb("ident", [P, P])
        ones = sb("ones", [P, P])
        relm = sb("relm", [P, 2 * P])
        c_silu = sb("c_silu", [P, DT])
        mod = sb("mod", [P, 24])
        gs2 = sb("gs2", [P, DT])
        gf_sq = sb("gf_sq", [P, DT])
        eps = sb("eps", [P, 1])
        inv16 = sb("inv16", [P, 16])
        sinks = sb("sinks", [P, SWH])
        rope_c = sb("rope_const", [P, 2])
        kv_col = sb("kv_col", [P, NB])
        ident_b = sb("ident_b", [P, P], mybir.dt.bfloat16)
        later_b = sb("later_b", [P, P], mybir.dt.bfloat16)
        nmax = sb("nmax", [P, 2, NB])
        rsum = sb("rsum", [P, 2, NB])
        rinv = sb("rinv", [P, 2, NB])
        esink = sb("esink", [P, 2, NB])
        arena = top[0]

        def area():
            here = [arena]

            def put(name, shape, dt=f32):
                o = here[0]
                here[0] += size(shape)
                return at(name, shape, o, dt)
            return put, here

        put, _ = area()
        x_nat = put("x_nat", [P, NB, D])
        mem_nat = put("mem_nat", [P, 2, D])
        prow = put("prow", [P, 4, P])
        iota_i = put("iota_i", [P, 2 * P], i32)
        later = put("later", [P, P])
        put, here = area()
        glu = put("glu", [P, 4, CK - 1 + T])
        cv = put("cv", [P, 4, T])
        u_pad = put("u_pad", [P, 4, 16 + T])
        pool_a = put("pool_a", [P, 16 + T])
        pool_b = put("pool_b", [P, 16 + T])
        pooled = put("pooled", [P, T])
        pooled_hi = put("pooled_hi", [P, 4, T], f32r)
        pooled_lo = put("pooled_lo", [P, 4, T], f32r)
        pw_raw = put("pw_raw", [P, 4, P])
        pw_hi = put("pw_hi", [P, 4, P], f32r)
        pw_lo = put("pw_lo", [P, 4, P], f32r)
        xa_at = here[0]
        m_hi = put("m_hi", [P, DT, MEM], f32r)
        m_lo = put("m_lo", [P, DT, MEM], f32r)
        kT = put("xa_kT", [P, DT, MEM])
        vN = put("xa_v", [P, 2, D])
        ends = [here[0]]
        put, here = area()
        qT = put("xa_qT", [P, DT, T])
        xp = put("xa_p", [P, 2, NB, MEM])
        xpT = put("xa_pT", [P, 2, 2, T])
        assert here[0] <= xa_at
        put, here = area()
        g_hi = put("g_hi", [P, FT, T], f32r)
        g_lo = put("g_lo", [P, FT, T], f32r)
        ends.append(here[0])
        put, here = area()
        lk = put("mla_k", [P, MH, T])
        lv = put("mla_v", [P, NB, MH * VD])
        lq = put("mla_q", [P, 4, T])
        cq_hi = put("cq_hi", [P, 3, T], f32r)
        cq_lo = put("cq_lo", [P, 3, T], f32r)
        lp_at = here[0]
        lp = put("mla_p", [P, 2, 10 * P])
        lpT = put("mla_pT", [P, 10 * P])
        r_cos = put("rope_cos", [P, T])
        r_sin = put("rope_sin", [P, T])
        ends.append(here[0])
        here[0] = lp_at
        cq_raw = put("cq_raw", [P, 3, T])
        ckv_raw = put("ckv_raw", [P, 2, T])
        kpe_raw = put("kpe_raw", [P, T])
        pos_i = put("pos_i", [P, T], i32)
        assert here[0] <= lp_at + 15 * P * 2 * 4
        here[0] = arena + size([P, MH, T]) + size([P, NB, MH * VD])
        ckv_hi = put("ckv_hi", [P, 2, T], f32r)
        ckv_lo = put("ckv_lo", [P, 2, T], f32r)
        lsh = sq
        put, here = area()
        sq_T = put("sb_q", [P, 4, T])
        sk_T = put("sb_k", [P, 4, T])
        sv_N = put("sb_v", [P, NB, 512])
        sg_T = put("sb_gate", [P, 4, T])
        wq_T = put("sw_q", [P, 4, T])
        wk_T = put("sw_k", [P, 2, T])
        wv_N = put("sw_v", [P, NB, P])
        wg_T = put("sw_gate", [P, 4, T])
        sp_T = put("softplus", [P, NB, T])
        sw_T = put("sb_w", [P, NB, T])
        sp_at = here[0]
        wp = put("sw_p", [P, 2, NB, 2 * P])
        wpT = put("sw_pT", [P, NB, 2 * P])
        minus = put("minus", [P, P])
        before = put("before", [P, P])
        not_before = put("not_before", [P, P], mybir.dt.bfloat16)
        from_here = put("from_here", [P, P])
        ends.append(here[0])
        here[0] = sp_at
        softplus = [sp_T, put("softplus_b", [P, NB, T])]
        here[0] = arena
        yT = put("y", [P, DT, T])
        out_nat = put("out_nat", [P, NB, D])
        assert max(ends) <= nc.sbuf_usable_end, (max(ends) - nc.sbuf_usable_end)

        bank = [ctx.enter_context(nc.psum_tensor(f"bank{i}", [P, T], f32)) for i in range(8)]
        stat = bank[7]

        def sem(name):
            return ctx.enter_context(nc.semaphore(name))

        masks_ready = sem("masks_ready")
        iota_ready = sem("iota_ready")
        x_loaded = [sem(f"x_loaded{i}") for i in range(2)]
        mem_loaded = sem("mem_loaded")
        rows_loaded = [sem(f"rows_loaded{i}") for i in range(2)]
        small_loaded = sem("small_loaded")
        poolw_loaded = sem("poolw_loaded")
        pre_ready = sem("pre_ready")
        pre_done = sem("pre_done")
        csilu_done = sem("csilu_done")
        ada_copied = sem("ada_copied")
        ada_cols = sem("ada_cols")
        mod_done = sem("mod_done")
        consts_done = sem("consts_done")
        raw_loaded = [sem(f"raw_loaded{i}") for i in range(2)]
        hi_done = sem("hi_done")
        lo_done = sem("lo_done")
        slab_half = sem("slab_half")
        tile_free = sem("tile_free")
        sq_done = sem("sq_done")
        mix_added = sem("mix_added")
        sum_done = sem("sum_done")
        squares_ready = sem("squares_ready")
        stat_done = sem("stat_done")
        sqrt_done = sem("sqrt_done")
        scaled = sem("scaled")
        split_hi = sem("split_hi")
        split_lo = sem("split_lo")
        memn_done = sem("memn_done")
        mem_hi = sem("mem_hi")
        mem_lo = sem("mem_lo")
        fin_done = sem("fin_done")
        fsq_done = sem("fsq_done")
        fsum_ready = sem("fsum_ready")
        stat2_done = sem("stat2_done")
        f_step = sem("f_step")
        v_ready = sem("v_ready")
        y_ready = sem("y_ready")
        col_sqrt = sem("col_sqrt")
        col_ready = sem("col_ready")
        dve_step = sem("dve_step")
        sig_done = sem("sig_done")
        pads_ready = sem("pads_ready")
        pool_step = sem("pool_step")
        pooled_ready = sem("pooled_ready")
        poolhi_done = sem("poolhi_done")
        poollo_done = sem("poollo_done")
        pwhi_done = sem("pwhi_done")
        pwlo_done = sem("pwlo_done")
        pool_out = sem("pool_out")
        ya_hi = sem("ya_hi")
        y_lo = sem("y_lo")
        cv_ready = sem("cv_ready")
        conv_step = sem("conv_step")
        cv_summed = sem("cv_summed")
        xc_ready = sem("xc_ready")
        xc_sq = sem("xc_sq")
        xc_summed = sem("xc_summed")
        ln_sqrt = sem("ln_sqrt")
        ln_norm = sem("ln_norm")
        ln_silu = sem("ln_silu")
        yb_hi = sem("yb_hi")
        xs_ready = sem("xs_ready")
        xmax_done = sem("xmax_done")
        xexp_done = sem("xexp_done")
        xrinv_ready = sem("xrinv_ready")
        xp_ready = sem("xp_ready")
        xt_ready = sem("xt_ready")
        xt_done = sem("xt_done")
        xo_ready = sem("xo_ready")
        xo_hi = sem("xo_hi")
        xo_lo = sem("xo_lo")
        tap2 = sem("tap2")
        tap1 = sem("tap1")
        taps_done = sem("taps_done")
        gate_silu = sem("gate_silu")
        silu_scaled = sem("silu_scaled")
        g_hi_done = sem("g_hi_done")
        g_lo_done = sem("g_lo_done")
        sin_done = sem("sin_done")
        pos_loaded = sem("pos_loaded")
        angle_ready = sem("angle_ready")
        k_rotated = sem("k_rotated")
        rope_ready = sem("rope_ready")
        kv_tile = sem("kv_tile")
        kv_cols = sem("kv_cols")
        kv_col_sqrt = sem("kv_col_sqrt")
        rinv_ready = sem("rinv_ready")
        q_base = sem("q_base")
        q_ready = sem("q_ready")
        ls_ready = sem("ls_ready")
        lmax_done = sem("lmax_done")
        lexp_done = sem("lexp_done")
        lp_ready = sem("lp_ready")
        lt_ready = sem("lt_ready")
        lt_done = sem("lt_done")
        lo_ready = sem("lo_ready")
        lo_hi = sem("lo_hi")
        lo_lo = sem("lo_lo")
        gate_act = sem("gate_act")
        k_shift = sem("k_shift")
        sb_masks = sem("sb_masks")
        z_ready = sem("z_ready")
        abs_done = sem("abs_done")
        exp_done = sem("exp_done")
        ln_done = sem("ln_done")
        sp_ready = sem("sp_ready")
        c_ready = sem("c_ready")
        w_ready = sem("w_ready")
        so_ready = sem("so_ready")
        so_scaled = sem("so_scaled")
        so_hi = sem("so_hi")
        so_lo = sem("so_lo")
        ws_ready = sem("ws_ready")
        wl_done = sem("wl_done")
        wmax_done = sem("wmax_done")
        wexp_done = sem("wexp_done")
        wrinv_ready = sem("wrinv_ready")
        wp_ready = sem("wp_ready")
        wt_ready = sem("wt_ready")
        wt_done = sem("wt_done")
        wo_ready = sem("wo_ready")
        wo_scaled = sem("wo_scaled")
        wo_hi = sem("wo_hi")
        wo_lo = sem("wo_lo")
        out_tr = sem("out_tr")
        out_copied = sem("out_copied")
        out_copied_a = sem("out_copied_a")
        out_stored = sem("out_stored")

        def wait(eng, s, value):
            if value > 0:
                eng.wait_ge(s, value)

        def hold(eng, s, value):
            if isinstance(value, int):
                wait(eng, s, value)
            else:
                eng.wait_ge(s, value)
                eng.nop(nofuse=True)

        def param(name, i=0):
            j, r = PROW[name]
            return prm[:, j, r + i:r + i + 1]

        def free_before(stage, tile):
            return TILE0[stage] + tile - 3

        def tap(layer, k, tile, moved):
            j, r = PROW[f"ffn_conv_w{layer}"]
            return prm[:, j, bass.ds(moved + (r + FT * k + tile), 1)]

        def conv_bias(layer, tile, moved):
            j, r = PROW["ffn_conv_b"]
            return prm[:, j, bass.ds(moved + (r + FT * layer + tile), 1)]

        LQ_SEQ = [("S", 0, i) for i in range(NB)]
        for _h in range(1, MH + 1):
            if _h < MH:
                LQ_SEQ += [("S", _h, i) for i in range(NB)]
            LQ_SEQ += [("T", _h - 1, j) for j in range(NB)]
        LQ_AT = {u: n for n, u in enumerate(LQ_SEQ)}
        QOFF = [0, P, 3 * P, 6 * P]
        KOFF = [0, 4 * P, 7 * P, 9 * P]
        XA_SEQ, SW_SEQ = [], []
        for _h in range(XH + 1):
            if _h < XH:
                XA_SEQ += [("S", _h, 0), ("S", _h, 1)]
            if _h:
                XA_SEQ += [("T", _h - 1, 0), ("T", _h - 1, 1), ("O", _h - 1, 0), ("O", _h - 1, 1)]
        for _h in range(SWH + 2):
            if _h < SWH:
                SW_SEQ += [("S", _h, 0), ("S", _h, 1)]
            if _h >= 2:
                SW_SEQ += [("O", _h - 2, 0)]
            if 1 <= _h <= SWH:
                SW_SEQ += [("T", _h - 1, 0), ("T", _h - 1, 1)]
        XA_AT = {u: n for n, u in enumerate(XA_SEQ)}
        SW_AT = {u: n for n, u in enumerate(SW_SEQ)}

        def norm_source(name, i):
            after = {"xa0": "pc_out", "ffn0": "wo0", "mix1": "down0", "xa1": "mla_o", "ffn1": "wo1"}
            if name in after:
                return tile_free, TILE0[after[name]] + i + 1
            if name == "mem":
                return pre_done, 4 + DT + i + 1
            if name == "mix0":
                return pre_done, i + 1
            return tile_free, TILE0["dq"] + DQ_TILES.index(i + 3 * (name == "ckv")) + 1

        NORM_SRC = {"mem": (lambda i: memn[:, i, :], MEM, D), "cq": (lambda i: cq_raw[:, i, :], T, QL),
                    "ckv": (lambda i: ckv_raw[:, i, :], T, KVL)}
        for _n in NORMT:
            NORM_SRC.setdefault(_n, (lambda i: x[:, i, :], T, D))
        NORM_DST = {"cq": (cq_hi, cq_lo), "ckv": (ckv_hi, ckv_lo)}
        NORM_GAIN = {"mix0": ("norm_mix_g", 0), "mix1": ("norm_mix_g", 8), "xa0": ("norm_xa_g", 0),
                     "xa1": ("norm_xa_g", 8), "ffn0": ("norm_ffn_g", 0), "ffn1": ("norm_ffn_g", 8),
                     "cq": ("mla_q_norm_g", 0), "ckv": ("mla_kv_norm_g", 0)}

        BEFORE = {"xa0": "pc_out", "ffn0": "wo0", "mix1": "up0", "xa1": "mla_o", "ffn1": "wo1"}
        RSTD_FREE = {"mem": (split_lo, 8), "xa0": (ln_norm, 4), "ffn0": (tile_free, TILE0["wq0"] + 8),
                     "mix1": (tile_free, TILE0["down0"] + 1), "ckv": (stat_done, POOLED.index("ckv") + 1),
                     "cq": (tile_free, TILE0["dq"] + 6), "xa1": (tile_free, TILE0["uq"] + MH),
                     "ffn1": (tile_free, TILE0["wq1"] + 8)}

        def acc_of(name):
            return {"mem": (pool_a, pool_b), "ckv": (fb[1], sq[1])}.get(name, (sq[0], sq[1]))

        def root_to(name):
            return fb[1] if name == "ckv" else rstd

        def slab_source(n):
            for stage, _ in STAGES:
                if FIRST[stage] <= n < FIRST[stage] + COUNT[stage]:
                    break
            s = n - FIRST[stage]

            def cols(w, start, width, rows=None):
                return w.rearrange("(k p) n -> p k n", p=P)[:, :, start:start + width], w.shape[0] // P, width
            if stage == "ada":
                return cols(ins["w_ada_2"][0], 256 * s, 256)
            if stage == "pc_in":
                return cols(ins["pc_w_in"][0], [1024, 512, 1280, 768, 0, 256][s], 256)
            if stage[:2] == "kv":
                return cols(ins["xa_wkv"][int(stage[2])], 256 * s, 256)
            if stage == "pc_out":
                return cols(ins["pc_w_out"][0], 256 * s, 256)
            if stage[:2] == "wq":
                return cols(ins["xa_wq"][int(stage[2])], 256 * s, 256)
            if stage[:2] == "wo":
                return cols(ins["xa_wo"][int(stage[2])], 256 * s, 256)
            if stage[:2] == "up":
                return cols(ins["ffn_w_up"][int(stage[2])], (s // 2) * 256 + (0 if s % 2 else FF), 256)
            if stage[:4] == "down":
                part = s % 3
                k0, k1 = 8 * part, min(8 * part + 8, FT)
                return cols(ins["ffn_w_down"][int(stage[4])][k0 * P:k1 * P, :], (s // 3) * 256, 256)
            if stage == "dq":
                return cols(ins["mla_w_dq_dkv"][0], 256 * DQ_SLABS[s], 160 if s == 1 else 256)
            if stage == "ukv":
                return cols(ins["mla_w_ukv"][0], 1024 * s, 1024)
            if stage == "uq":
                return cols(ins["mla_w_uq"][0], 192 * s, 192)
            if stage == "mla_o":
                return cols(ins["mla_w_o"][0], 256 * s, 256)
            if stage == "w_in":
                return cols(ins["w_in_2"][0], 256 * s, 256)
            return cols(ins["w_out_2"][0], 256 * s, 256)

        def view(buf, nk, width):
            return buf[:, 0:nk * width].rearrange("p (k n) -> p k n", k=nk)

        ROWS = list(PROW)

        def rows(eng, name, loaded):
            j, r = PROW[name]
            if name in ("ffn_conv_w0", "ffn_conv_w1"):
                v = ins["ffn_conv_w"][int(name[-1])].rearrange("k d -> (k d)")
            elif name == "conv_dw_w":
                v = ins[name][0].rearrange("k d -> (k d)")
            elif name in ("final_norm_g", "final_g_2"):
                v = ins[name]
            else:
                v = ins[name].rearrange("l d -> (l d)")
            v = v.rearrange("(r p) -> r p", p=P)
            eng.dma_start(prow[r:r + v.shape[0], j, :], v).then_inc(loaded, 16)

        block = ctx.enter_context(nc.Block())

        @block.sync
        def _(sp):
            for half in range(2):
                v = slice(half * 512, (half + 1) * 512)
                sp.dma_start(x_nat[:, :, v], ins["x"][0].rearrange("(t p) d -> p t d", p=P)[:, :, v]).then_inc(x_loaded[half], 16)

            for name in ROWS[::2]:
                rows(sp, name, rows_loaded[0])

            def load(n):
                src, nk, width = slab_source(n)
                if n >= 2 and is_ada(n - 2):
                    sp.wait_ge(slab_half, 2 * (n - 1))
                elif n >= 2:
                    sp.wait_ge(lo_done, splits_before(n - 2) + 1)
                sp.dma_start(view(raw[n % 2], nk, width), src).then_inc(raw_loaded[n % 2], 16)

            def load_up(layer):
                n0 = FIRST[f"up{layer}"]
                w = ins["ffn_w_up"][layer].rearrange("(k p) (a s n) -> p a s k n", p=P, a=2, n=256)
                with sp.Fori(0, COUNT[f"up{layer}"] // 2) as it:
                    for u in range(2):
                        hold(sp, lo_done, 2 * it + (splits_before(n0 + u - 2) + 1))
                        src = w[:, 1 - u, bass.ds(it, 1)].rearrange("p s k n -> p (s k) n")
                        sp.dma_start(view(raw[(n0 + u) % 2], 8, 256), src).then_inc(raw_loaded[(n0 + u) % 2], 16)

            n = 0
            while n < NSLAB:
                layer = {FIRST["up0"]: 0, FIRST["up1"]: 1}.get(n)
                if n == 2:
                    sp.dma_start(mem_nat[:, :, :], ins["mem"][0].rearrange("(t p) d -> p t d", p=P)).then_inc(mem_loaded, 16)
                if layer is None:
                    load(n)
                    n += 1
                else:
                    load_up(layer)
                    n += COUNT["up0"]
            for t in range(NB):
                sp.wait_ge(out_copied, t + 1)
                sp.wait_ge(out_copied_a, t + 1)
                sp.dma_start(out[0, t * P:(t + 1) * P, :], out_nat[:, t, :]).then_inc(out_stored, 16)
            sp.wait_ge(out_stored, 16 * NB)

        @block.gpsimd
        def _(pool):
            nc.gpsimd.memset(ident[:, :], 0.0).then_inc(iota_ready, 1)
            nc.gpsimd.memset(ones[:, :], 1.0).then_inc(masks_ready, 1)
            nc.gpsimd.memset(later[:, :], 0.0).then_inc(iota_ready, 1)
            nc.gpsimd.iota(iota_i[:, :], pattern=[[-1, 2 * P]], base=P, channel_multiplier=1).then_inc(iota_ready, 1)
            pool.wait_ge(iota_ready, 3)
            nc.gpsimd.affine_select(out=ident[:, :], in_=ident[:, :], compare_op=ALU.not_equal, fill=1.0, base=0,
                                    pattern=[[-1, P]], channel_multiplier=1).then_inc(masks_ready, 1)
            nc.gpsimd.affine_select(out=later[:, :], in_=later[:, :], compare_op=ALU.is_ge, fill=NEG, base=0,
                                    pattern=[[-1, P]], channel_multiplier=1).then_inc(masks_ready, 1)
            nc.gpsimd.tensor_copy(relm[:, :], iota_i[:, :]).then_inc(iota_ready, 1)
            pool.wait_ge(iota_ready, 4)
            nc.gpsimd.affine_select(out=relm[:, :], in_=relm[:, :], compare_op=ALU.is_ge, fill=-NEG, base=P,
                                    pattern=[[-1, 2 * P]], channel_multiplier=1).then_inc(iota_ready, 1)
            pool.wait_ge(iota_ready, 5)
            nc.gpsimd.affine_select(out=relm[:, :], in_=relm[:, :], compare_op=ALU.is_gt, fill=-NEG, base=0,
                                    pattern=[[1, 2 * P]], channel_multiplier=-1).then_inc(masks_ready, 1)
            pool.wait_ge(iota_ready, 5)
            nc.gpsimd.iota(iota_i[:, 0:16], pattern=[[1, 16]], base=1, channel_multiplier=0).then_inc(iota_ready, 1)
            pool.wait_ge(iota_ready, 6)
            nc.gpsimd.tensor_copy(inv16[:, :], iota_i[:, 0:16]).then_inc(masks_ready, 1)
            nc.gpsimd.memset(eps[:, :], EPS).then_inc(masks_ready, 1)

            pool.dma_start(sinks[:, :], ins["sinks_2"].broadcast_to([P, SWH])).then_inc(small_loaded, 16)
            pool.dma_start(rope_c[64:96, :], ins["rope_const"]).then_inc(small_loaded, 16)
            pool.dma_start(pw_raw[:, :, :], ins["pool_w"][0].rearrange("g c d -> c g d")).then_inc(poolw_loaded, 16)


            pool.wait_ge(pre_ready, 20)
            nc.gpsimd.memset(glu[:, :, 0:CK - 1], 0.0).then_inc(pads_ready, 1)
            nc.gpsimd.memset(u_pad[:, :, 0:16], 0.0).then_inc(pads_ready, 1)
            pool.wait_ge(pads_ready, 2)
            step = [0]

            def link(ins_):
                step[0] += 1
                ins_.then_inc(pool_step, 1)
                pool.wait_ge(pool_step, step[0])

            def squares(name):
                src, N, _ = NORM_SRC[name]
                acc, tmp = (b[:, 0:N] for b in acc_of(name))
                for i in range(NORMT[name]):
                    pool.wait_ge(*norm_source(name, i))
                    if i == 0:
                        wait(pool, stat_done, POOLED.index(name))
                        link(nc.gpsimd.tensor_tensor(acc, src(i), src(i), MUL))
                        continue
                    link(nc.gpsimd.tensor_tensor(tmp, src(i), src(i), MUL))
                    m = nc.gpsimd.tensor_tensor(acc, acc, tmp, ADD)
                    if i < NORMT[name] - 1:
                        link(m)
                m.then_inc(squares_ready, 1)

            squares("mem")
            pool.wait_ge(stat_done, 1)
            pool.wait_ge(consts_done, 1)
            for g, w in enumerate(WINDOWS):
                pool.wait_ge(tile_free, TILE0["pc_in"] + 8 + g + 1)
                wait(pool, pooled_ready, g)
                src, n = u_pad[:, g, :], 1
                bufs = [pool_a, pool_b]
                while n < w:
                    dst = bufs[0]
                    link(nc.gpsimd.tensor_tensor(dst[:, 2 * n - 1:], src[:, 2 * n - 1:], src[:, n - 1:16 + T - n], ADD))
                    src, n = dst, 2 * n
                    bufs.reverse()
                dst = bufs[0]
                link(nc.gpsimd.tensor_scalar(dst[:, 16:], src[:, 16:], 1.0 / w, 1.0, MUL, MUL))
                link(nc.gpsimd.tensor_tensor(dst[:, 16:16 + w], src[:, 16:16 + w], inv16[:, 0:w], MUL))
                wait(pool, poollo_done, g)
                nc.gpsimd.tensor_tensor(pooled[:, :], dst[:, 16:], u_pad[:, g, 16:], SUB).then_inc(pooled_ready, 1)

            squares("xa0")
            squares("ffn0")
            squares("mix1")
            squares("ckv")
            squares("cq")
            for h in range(MH):
                pool.wait_ge(q_base, h + 1)
                q = lq[64:96, h % 4, :]
                link(nc.gpsimd.tensor_tensor(lsh[h % 2][64:96, :], lsh[h % 2][64:96, :], r_sin[64:96, :], MUL))
                link(nc.gpsimd.tensor_tensor(q, q, r_cos[64:96, :], MUL))
                nc.gpsimd.tensor_tensor(q, q, lsh[h % 2][64:96, :], ADD).then_inc(q_ready, 1)

            squares("xa1")
            squares("ffn1")
            pool.wait_ge(tile_free, TILE0["down1"] + 8)
            nc.gpsimd.memset(minus[:, :], -1.0).then_inc(sb_masks, 1)
            nc.gpsimd.memset(not_before[:, :], NEG).then_inc(sb_masks, 1)
            pool.wait_ge(sb_masks, 2)
            nc.gpsimd.affine_select(out=before[:, :], in_=ones[:, :], compare_op=ALU.is_gt, fill=0.0, base=0,
                                    pattern=[[1, P]], channel_multiplier=-1).then_inc(sb_masks, 1)
            nc.gpsimd.affine_select(out=from_here[:, :], in_=minus[:, :], compare_op=ALU.is_ge, fill=0.0, base=0,
                                    pattern=[[-1, P]], channel_multiplier=1).then_inc(sb_masks, 1)
            nc.gpsimd.affine_select(out=not_before[:, :], in_=not_before[:, :], compare_op=ALU.is_ge, fill=0.0, base=0,
                                    pattern=[[1, P]], channel_multiplier=-1).then_inc(sb_masks, 1)
            pool.wait_ge(tile_free, TILE0["w_in"] + 21)
            pool.dma_start(wk_T[HD:, 0, :], wk_T[0:HD, 0, :]).then_inc(k_shift, 16)
            pool.dma_start(wk_T[0:HD, 1, :], wk_T[HD:, 1, :]).then_inc(k_shift, 16)

        @block.tensor
        def _(pe):
            def mm(o, w, v, start, stop, **kw):
                return nc.tensor.matmul(o, w, v, start=start, stop=stop, **kw)

            def slab_tile(stage, n, tile, o, nk, weights, operand, ready=None, first=True, last=True, k0=0, inc=1,
                          inc_sem=None, shift=0, free=True):
                if free:
                    value = free_before(stage, tile) + shift
                    if not isinstance(shift, int) or value > 0:
                        pe.wait_ge(tile_free, value)
                for k in range(nk):
                    if ready is not None:
                        pe.wait_ge(ready[0], ready[1] + ready[2] * max(k + 1 - ready[3], 0) if len(ready) > 2
                                   else ready[1] + k + 1)
                    wh, wl = weights(k)
                    vh, vl = operand(k0 + k)
                    mm(o, wh, vh, first and k == 0, False)
                    mm(o, wh, vl, False, False)
                    m = mm(o, wl, vh, False, last and k == nk - 1)
                m.then_inc(inc_sem or slab_half, inc)

            def slab(stage, n, tiles, nk, width, operand, N=T, ready=None, shift=0, step=0):
                pe.wait_ge(lo_done, splits_before(n) + 1 + step)
                wh, wl = view(w_hi[n % 2], nk, width), view(w_lo[n % 2], nk, width)
                for i, (tile, c0, cn) in enumerate(tiles):
                    o = bank[(TILE0[stage] + tile) % 4][0:cn, 0:N]
                    slab_tile(stage, n, tile, o, nk, lambda k: (wh[:, k, c0:c0 + cn], wl[:, k, c0:c0 + cn]), operand,
                              ready=ready if i == 0 else None, shift=shift)

            def h_operand(k):
                return h_hi[:, k, :], h_lo[:, k, :]

            def linear(stage, ready, after=lambda s: None):
                for s in range(COUNT[stage]):
                    slab(stage, FIRST[stage] + s, [(2 * s, 0, P), (2 * s + 1, P, P)], DT, 256, h_operand,
                         ready=ready if s == 0 else None)
                    after(s)

            def stat_sum(name):
                N = NORM_SRC[name][1]
                pe.wait_ge(squares_ready, POOLED.index(name) + 1)
                wait(pe, sqrt_done, NORMI[name])
                mm(stat[:, 0:N], ones[:, :], acc_of(name)[0][:, 0:N], True, True).then_inc(stat_done, 1)

            pe.wait_ge(masks_ready, 2)
            def turn_tiles(src, r0, nt):
                for r in range(r0, r0 + DT):
                    if r >= 4:
                        pe.wait_ge(pre_done, r - 3)
                    for t in range(nt):
                        m = nc.tensor.transpose(bank[4 + r % 4][:, t * P:(t + 1) * P],
                                                src[:, t, (r - r0) * P:(r - r0 + 1) * P], ident[:, :])
                    m.then_inc(pre_ready, 1)
                    if r == 3:
                        pe.wait_ge(x_loaded[1], 16)

            pe.wait_ge(x_loaded[0], 16)
            turn_tiles(x_nat, 0, NB)
            for half in range(2):
                pe.wait_ge(rows_loaded[half], 16 * len(ROWS[half::2]))
            for j, r in enumerate(PROWS):
                pe.wait_ge(pre_done, DT + j - 3)
                nc.tensor.transpose(bank[4 + j][:, 0:r], prow[0:r, j, :], ident[0:r, 0:r]).then_inc(pre_ready, 1)
            pe.wait_ge(pre_done, 4 + DT)
            pe.wait_ge(mix_added, DT - 1)
            mm(stat[:, :], ones[:, :], fb[0][:, :], True, True).then_inc(sum_done, 1)

            def mem_meanwhile(s):
                if s == 0:
                    pe.wait_ge(mem_loaded, 16)
                    pe.wait_ge(sqrt_done, 1)
                    turn_tiles(mem_nat, 4 + DT, 2)
                    pe.wait_ge(pre_done, 4 + 2 * DT)
                if s == 1:
                    stat_sum("mem")

            linear("pc_in", (split_lo, SPLIT0["mix0"]), mem_meanwhile)

            def memory(layer):
                stage = f"kv{layer}"

                def m_operand(k):
                    return m_hi[:, k, :], m_lo[:, k, :]
                for s in range(4):
                    slab(stage, FIRST[stage] + s, [(2 * s, 0, P), (2 * s + 1, P, P)], DT, 256, m_operand, N=MEM,
                         ready=(mem_lo, 8 * layer) if s == 0 else None)
                for s in range(4, 8):
                    n = FIRST[stage] + s
                    pe.wait_ge(lo_done, splits_before(n) + 1)
                    wh, wl = view(w_hi[n % 2], DT, 256), view(w_lo[n % 2], DT, 256)
                    for j in range(2):
                        o = bank[(TILE0[stage] + 2 * s + j) % 4][:, 0:256]
                        slab_tile(stage, n, 2 * s + j, o, DT,
                                  lambda k: (m_hi[:, k, j * P:(j + 1) * P], m_lo[:, k, j * P:(j + 1) * P]),
                                  lambda k: (wh[:, k, :], wl[:, k, :]))

            memory(0)
            pe.wait_ge(pwlo_done, 1)
            for g in range(4):
                pe.wait_ge(poollo_done, g + 1)
                wait(pe, y_lo, g - 1)
                o = bank[4 + g % 2][:, :]
                mm(o, pw_hi[:, g, :], pooled_hi[:, g, :], True, False)
                mm(o, pw_hi[:, g, :], pooled_lo[:, g, :], False, False)
                mm(o, pw_lo[:, g, :], pooled_hi[:, g, :], False, True).then_inc(pool_out, 1)
            pe.wait_ge(csilu_done, 1)
            pe.wait_ge(y_lo, 4)

            def ada_row(u, step=0):
                n = FIRST["ada"] + u
                pe.wait_ge(raw_loaded[n % 2], 8 * step + 16 * (n // 2 + 1))
                w = view(raw[n % 2], DT, 256)
                for k in range(DT):
                    m = mm(bank[4 + u % 2][0:1, 0:256], c_silu[:, k:k + 1], w[:, k, :], k == 0, k == DT - 1)
                m.then_inc(slab_half, 2)

            def ada_columns(u, step=0):
                pe.wait_ge(ada_copied, step + (u + 1))
                for j in range(2):
                    c = 2 * u + j
                    m = mm(bank[6][:, c:c + 1] if isinstance(step, int) else bank[6][:, bass.ds(2 * step + c, 1)],
                           sq[u % 2][0:1, j * P:(j + 1) * P], ones[0:1, 0:1], True, True)
                m.then_inc(ada_cols, 1)

            ada_row(0)
            with pe.Fori(0, COUNT["ada"] // 2 - 1) as it:
                for u in range(2):
                    ada_row(u + 1, 2 * it)
                    ada_columns(u, 2 * it)
            ada_row(COUNT["ada"] - 1)
            ada_columns(COUNT["ada"] - 2)
            ada_columns(COUNT["ada"] - 1)
            pe.wait_ge(mod_done, 1)
            for i in range(4):
                pe.wait_ge(cv_ready, i + 1)
                mm(bank[6][:, :], ones[:, :], cv[:, i, :], i == 0, i == 3).then_inc(cv_summed, 1)
            for i in range(4):
                pe.wait_ge(xc_sq, i + 1)
                mm(stat[:, :], ones[:, :], sq[i % 2][:, :], i == 0, i == 3).then_inc(xc_summed, 1)
            linear("pc_out", (y_lo, 0))

            def cross_attention(layer):
                base = layer

                def place(kind, h, j):
                    r = XA_AT[(kind, h, j)]
                    if r >= 4:
                        k, g, i = XA_SEQ[r - 4]
                        if k == "S":
                            pe.wait_ge(xexp_done, 16 * base + 4 * g + 2 * i + 2)
                        elif k == "T":
                            pe.wait_ge(xt_done, 8 * base + 2 * g + i + 1)
                        else:
                            pe.wait_ge(xo_lo, 8 * base + 2 * g + i + 1)
                    return bank[4 + r % 4]

                for h in range(XH + 1):
                    if h < XH:
                        for i in range(2):
                            o = place("S", h, i)
                            for b in range(2):
                                q0 = (2 * i + b) * P
                                for k in range(2):
                                    m = mm(o[:, b * MEM:(b + 1) * MEM], qT[:, 2 * h + k, q0:q0 + P],
                                           kT[:, 2 * h + k, :], k == 0, k == 1)
                            m.then_inc(xs_ready, 1)
                    if h:
                        g = h - 1
                        for j in range(2):
                            o = place("T", g, j)
                            for t in range(NB):
                                if j == 0:
                                    pe.wait_ge(xp_ready, 16 * base + 4 * g + t + 1)
                                m = nc.tensor.transpose(o[:, t * P:(t + 1) * P], xp[:, g % 2, t, j * P:(j + 1) * P],
                                                        ident[:, :])
                            m.then_inc(xt_ready, 1)
                        for d in range(2):
                            o = place("O", g, d)
                            for j in range(2):
                                pe.wait_ge(xt_done, 8 * base + 2 * g + j + 1)
                                c0 = g * XHD + d * P
                                m = mm(o[:, :], vN[:, j, c0:c0 + P], xpT[:, g % 2, j, :], j == 0, j == 1)
                            m.then_inc(xo_ready, 1)

            def ffn(layer):
                up, down = f"up{layer}", f"down{layer}"

                def up_step(it, first=False):
                    for u in range(2):
                        slab(up, FIRST[up] + u, [(2 * u, 0, P), (2 * u + 1, P, P)], DT, 256, h_operand,
                             ready=(split_lo, SPLIT0[f"ffn{layer}"]) if first and u == 0 else None,
                             shift=4 * it, step=2 * it)
                        if first and u == 0:
                            stat_sum(f"ffn{layer}")

                up_step(0, first=True)
                with pe.Fori(1, COUNT[up] // 2) as it:
                    up_step(it)
                with pe.Fori(0, 2) as it:
                    for s in range(6):
                        n = FIRST[down] + s
                        part, nk = s % 3, (8, 8, 6)[s % 3]
                        pe.wait_ge(lo_done, splits_before(n) + 1 + 6 * it)
                        wh, wl = view(w_hi[n % 2], nk, 256), view(w_lo[n % 2], nk, 256)
                        for j in range(2):
                            tile = 2 * (s // 3) + j
                            slab_tile(down, n, tile, bank[(TILE0[down] + tile) % 4][:, :], nk,
                                      lambda k: (wh[:, k, j * P:(j + 1) * P], wl[:, k, j * P:(j + 1) * P]),
                                      lambda k: (g_hi[:, k, :], g_lo[:, k, :]), k0=8 * part, first=part == 0,
                                      last=part == 2, free=part == 0, shift=4 * it,
                                      ready=(g_lo_done, FT * layer + 8 * part) if j == 0 else None)

            def cross(layer):
                linear(f"wq{layer}", (split_lo, SPLIT0[f"xa{layer}"]), lambda s: stat_sum(f"xa{layer}") if s == 0 else None)
                if layer:
                    memory(1)
                pe.wait_ge(tile_free, TILE0[f"wo{layer}"])
                cross_attention(layer)
                linear(f"wo{layer}", (xo_lo, 8 * layer))
                ffn(layer)

            cross(0)

            for s, tiles in enumerate(([(0, 0, P), (1, P, P)], [(2, 0, P), (3, 64, 96)], [(4, 0, P), (5, P, P)])):
                slab("dq", FIRST["dq"] + s, tiles, DT, 160 if s == 1 else 256, h_operand,
                     ready=(split_lo, SPLIT0["mix1"]) if s == 0 else None)
                if s == 0:
                    stat_sum("mix1")
            for s in range(2):
                if s:
                    stat_sum("cq")
                n = FIRST["ukv"] + s
                pe.wait_ge(lo_done, splits_before(n) + 1)
                wh, wl = view(w_hi[n % 2], 2, 1024), view(w_lo[n % 2], 2, 1024)
                for i in range(12):
                    tile = 12 * s + i
                    ready = (split_lo, SPLIT0["ckv"]) if tile == 0 else None
                    last = dict(inc=2) if i == 11 else dict(inc_sem=kv_tile)
                    b = bank[(TILE0["ukv"] + tile) % 4]
                    if i < 8:
                        c0 = i * P
                        slab_tile("ukv", n, tile, b[0:NOPE, :], 2,
                                  lambda k: (wh[:, k, c0:c0 + NOPE], wl[:, k, c0:c0 + NOPE]),
                                  lambda k: (ckv_hi[:, k, :], ckv_lo[:, k, :]), ready=ready, **last)
                        if tile == 1:
                            stat_sum("ckv")
                            for t in range(NB):
                                m = mm(bank[6][:, t:t + 1], fb[1][:, t * P:(t + 1) * P], ones[:, 0:1], True, True)
                            m.then_inc(kv_cols, 1)
                    else:
                        t = i - 8
                        vh, vl = (v.rearrange("p k (h c) -> p k h c", c=P)[:, :, :, NOPE:] for v in (wh, wl))
                        slab_tile("ukv", n, tile, b[:, :].rearrange("p (h c) -> p h c", c=VD), 2,
                                  lambda k: (ckv_hi[:, k, t * P:(t + 1) * P], ckv_lo[:, k, t * P:(t + 1) * P]),
                                  lambda k: (vh[:, k], vl[:, k]), **last)

            def queries(pair):
                n = FIRST["uq"] + pair
                pe.wait_ge(lo_done, splits_before(n) + 1)
                wh, wl = view(w_hi[n % 2], 3, 192), view(w_lo[n % 2], 3, 192)
                for j in range(2):
                    slab_tile("uq", n, 2 * pair + j, bank[(TILE0["uq"] + 2 * pair + j) % 4][0:QKD, :], 3,
                              lambda k: (wh[:, k, j * QKD:(j + 1) * QKD], wl[:, k, j * QKD:(j + 1) * QKD]),
                              lambda k: (cq_hi[:, k, :], cq_lo[:, k, :]),
                              ready=(split_lo, SPLIT0["cq"]) if pair + j == 0 else None)

            def lq_place(kind, h, j):
                r = LQ_AT[(kind, h, j)]
                if r >= 3:
                    k, g, i = LQ_SEQ[r - 3]
                    pe.wait_ge(lexp_done if k == "S" else lt_done, 4 * g + i + 1)
                return bank[4 + r % 3]

            def scores(h):
                pe.wait_ge(q_ready, h + 1)
                for i in range(NB):
                    o = lq_place("S", h, i)
                    n = (i + 1) * P
                    mm(o[:, 0:n], lq[0:QKD, h % 4, i * P:(i + 1) * P], lk[0:QKD, h, 0:n], True, False)
                    mm(o[:, i * P:n], ident_b[:, :], later_b[:, :], False, True).then_inc(ls_ready, 1)

            def turn(h):
                for j in range(NB):
                    o = lq_place("T", h, j)
                    for i in range(j, NB):
                        if j == 0:
                            pe.wait_ge(lp_ready, 4 * h + i + 1)
                        c0 = QOFF[i] + j * P
                        m = nc.tensor.transpose(o[:, (i - j) * P:(i - j + 1) * P], lp[:, h % 2, c0:c0 + P], ident[:, :])
                    m.then_inc(lt_ready, 1)

            def values(h):
                if h % 2 == 0:
                    wait(pe, lo_lo, h // 2)
                r0 = (h % 2) * VD
                for j in range(NB):
                    pe.wait_ge(lt_done, 4 * h + j + 1)
                    m = mm(stat[r0:r0 + VD, j * P:], lv[:, j, h * VD:(h + 1) * VD], lpT[:, KOFF[j]:KOFF[j] + (NB - j) * P],
                           j == 0, j == NB - 1, skip_group_check=True)
                m.then_inc(lo_ready, 1)

            queries(0)
            pe.wait_ge(tile_free, TILE0["uq"])
            pe.wait_ge(rope_ready, 1)
            for h in range(MH + 1):
                if h < MH:
                    scores(h)
                    if h % 2 == 0 and h // 2 + 1 < MH // 2:
                        queries(h // 2 + 1)
                if h:
                    turn(h - 1)
                    values(h - 1)
            linear("mla_o", (lo_lo, 0))
            cross(1)
            pe.wait_ge(fsq_done, 3 + 3 * DT)
            pe.wait_ge(sqrt_done, NORMI["ffn1"] + 1)
            mm(stat[:, :], ones[:, :], sq[0][:, :], True, True).then_inc(stat2_done, 1)
            mm(bank[6][:, :], ones[:, :], sq[1][:, :], True, True).then_inc(stat2_done, 1)

            for s in range(13):
                n = FIRST["w_in"] + s
                if s in (4, 5):
                    pe.wait_ge(lo_done, splits_before(n) + 1)
                    wh, wl = view(w_hi[n % 2], DT, 256), view(w_lo[n % 2], DT, 256)
                    for j in range(2):
                        tile = 2 * s + j
                        b = bank[(TILE0["w_in"] + tile) % 4]
                        wait(pe, tile_free, free_before("w_in", tile))
                        for half in range(2):
                            t = 2 * j + half
                            for k in range(DT):
                                o, hh, hl = b[:, half * 256:(half + 1) * 256], h_hi[:, k, t * P:(t + 1) * P], h_lo[:, k, t * P:(t + 1) * P]
                                mm(o, hh, wh[:, k, :], k == 0, False)
                                mm(o, hh, wl[:, k, :], False, False)
                                m = mm(o, hl, wh[:, k, :], False, k == DT - 1)
                        m.then_inc(slab_half, 1)
                elif s == 10:
                    pe.wait_ge(lo_done, splits_before(n) + 1)
                    wh, wl = view(w_hi[n % 2], DT, 256), view(w_lo[n % 2], DT, 256)
                    slab_tile("w_in", n, 20, bank[(TILE0["w_in"] + 20) % 4][:, :], DT,
                              lambda k: (wh[:, k, 0:P], wl[:, k, 0:P]), h_operand)
                    b = bank[(TILE0["w_in"] + 21) % 4]
                    wait(pe, tile_free, free_before("w_in", 21))
                    for t in range(NB):
                        for k in range(DT):
                            o, hh, hl = b[:, t * P:(t + 1) * P], h_hi[:, k, t * P:(t + 1) * P], h_lo[:, k, t * P:(t + 1) * P]
                            mm(o, hh, wh[:, k, P:], k == 0, False)
                            mm(o, hh, wl[:, k, P:], False, False)
                            m = mm(o, hl, wh[:, k, P:], False, k == DT - 1)
                    m.then_inc(slab_half, 1)
                else:
                    slab("w_in", n, [(2 * s, 0, P), (2 * s + 1, P, P)], DT, 256, h_operand,
                         ready=(split_lo, SPLIT0["second"]) if s == 0 else None)

            pe.wait_ge(tile_free, TILE0["w_out"])

            pe.wait_ge(sb_masks, 5)

            def logits(h):
                wait(pe, so_scaled, h - 1)
                r0, p = (h % 2) * HD, h // 2
                for j in range(NB - 1, -1, -1):
                    mm(bank[4 * (h % 2) + j][:, 0:(NB - j) * P], sk_T[r0:r0 + HD, p, j * P:(j + 1) * P],
                       sq_T[r0:r0 + HD, p, j * P:], True, True).then_inc(z_ready, 1)

            def sticks(h):
                for j in range(NB - 1, -1, -1):
                    pe.wait_ge(sp_ready, 4 * h + NB - j)
                    o = bank[4 * (h % 2) + j]
                    mm(o[:, 0:P], not_before[:, :], ident_b[:, :], False, False, skip_group_check=True)
                    for i in range(NB - 1, j, -1):
                        mm(o[:, (i - j) * P:(NB - j) * P], minus[:, :], softplus[h % 2][:, i, i * P:], False, False,
                           skip_group_check=True)
                    mm(o[:, 0:(NB - j) * P], from_here[:, :], softplus[h % 2][:, j, j * P:], False, True,
                       skip_group_check=True).then_inc(c_ready, 1)

            def stick_values(h):
                r0 = (h % 2) * HD
                o = bank[4 * (h % 2) + 3][r0:r0 + HD, :]
                pe.wait_ge(w_ready, 4 * h + NB)
                for j in range(NB):
                    m = mm(o[:, j * P:], sv_N[:, j, h * HD:(h + 1) * HD], sw_T[:, j, j * P:], j == 0, j == NB - 1)
                m.then_inc(so_ready, 1)

            logits(0)
            for h in range(SBH):
                if h + 1 < SBH:
                    logits(h + 1)
                sticks(h)
                stick_values(h)

            def w_place(kind, h, j):
                r = SW_AT[(kind, h, j)]
                if r >= 4:
                    k, g, i = SW_SEQ[r - 4]
                    if k == "O":
                        pe.wait_ge(wo_scaled, g + 1)
                    else:
                        pe.wait_ge(wl_done if k == "S" else wt_done, (4 if k == "S" else 2) * g + (2 * i + 2 if k == "S" else i + 1))
                return bank[4 + r % 4]

            pe.wait_ge(so_scaled, SBH)
            pe.wait_ge(k_shift, 32)
            for h in range(SWH + 2):
                if h < SWH:
                    r0, p, g = (h % 2) * HD, h // 2, h // 4
                    for i in range(2):
                        o = w_place("S", h, i)
                        for b in range(2):
                            q = 2 * i + b
                            c0 = P if q == 0 else 0
                            m = mm(o[:, b * 2 * P + c0:(b + 1) * 2 * P], wq_T[r0:r0 + HD, p, q * P:(q + 1) * P],
                                   wk_T[r0:r0 + HD, g, (q - 1) * P + c0:(q + 1) * P], True, True)
                        m.then_inc(ws_ready, 1)
                if h >= 2:
                    e = h - 2
                    r0, g = (e % 2) * HD, e // 4
                    o = w_place("O", e, 0)
                    pe.wait_ge(wt_done, 2 * e + 2)
                    for q in range(NB):
                        v = slice(g * HD, (g + 1) * HD)
                        m = mm(o[r0:r0 + HD, q * P:(q + 1) * P], wv_N[:, q, v], wpT[:, q, 0:P], True, q == 0)
                        if q:
                            m = mm(o[r0:r0 + HD, q * P:(q + 1) * P], wv_N[:, q - 1, v], wpT[:, q - 1, P:], False, True)
                    m.then_inc(wo_ready, 1)
                if 1 <= h <= SWH:
                    e = h - 1
                    for b in range(2):
                        o = w_place("T", e, b)
                        pe.wait_ge(wp_ready, 4 * e + 4)
                        for j in (2 * b, 2 * b + 1):
                            for q in (j, j + 1):
                                if q < NB:
                                    c0 = P if q == j else 0
                                    o0 = (j % 2) * 2 * P + (q - j) * P
                                    m = nc.tensor.transpose(o[:, o0:o0 + P], wp[:, e % 2, q, c0:c0 + P], ident[:, :])
                        m.then_inc(wt_ready, 1)
            pe.wait_ge(so_lo, SBH)
            for s in range(4):
                slab("w_out", FIRST["w_out"] + s, [(2 * s, 0, P), (2 * s + 1, P, P)], DT, 256, h_operand,
                     ready=(wo_lo, 2, 2, NB + 1) if s == 0 else None)
            pe.wait_ge(tile_free, TILE0["w_out"] + 8)
            for t in range(NB):
                for half in range(2):
                    for d in range(4):
                        if t == 0:
                            pe.wait_ge(y_ready, 4 * half + d + 1)
                        m = nc.tensor.transpose(bank[2 * t + half][:, d * P:(d + 1) * P],
                                                yT[:, 4 * half + d, t * P:(t + 1) * P], ident[:, :])
                    m.then_inc(out_tr, 1)
                if t == 0:
                    pe.wait_ge(fsum_ready, 1)
                    for b in range(NB):
                        m = mm(bank[7][:, b:b + 1], sq[0][:, b * P:(b + 1) * P], ones[:, 0:1], True, True)
                    m.then_inc(stat2_done, 1)
                if t == 2:
                    pe.wait_ge(col_sqrt, 1)

        @block.scalar
        def _(act):
            def a(o, i, f, **kw):
                return nc.scalar.activation(o, i, f, **kw)

            def split(n, step=0):
                if isinstance(step, int) and (n + step >= NSLAB or is_ada(n + step)):
                    return
                last = n - 2 - (COUNT["ada"] if is_ada(n - 2) else 0)
                hold(act, raw_loaded[n % 2], 16 * (n // 2 + 1) + 8 * step)
                hold(act, slab_half, 2 * (last + 1) + 2 * step)
                c = slab_columns(n)
                a(w_hi[n % 2][:, 0:c], raw[n % 2][:, 0:c], ACT.Copy).then_inc(hi_done, 1)

            def root_of(name):
                _, N, width = NORM_SRC[name]
                act.wait_ge(stat_done, POOLED.index(name) + 1)
                act.wait_ge(*RSTD_FREE[name])
                if name == "ckv":
                    act.wait_ge(kv_cols, 1)
                    a(kv_col[:, :], bank[6][:, 0:NB], ACT.Sqrt, scale=1.0 / width, bias=eps[:, :]).then_inc(kv_col_sqrt, 1)
                a(root_to(name)[:, 0:N], stat[:, 0:N], ACT.Sqrt, scale=1.0 / width, bias=eps[:, :]).then_inc(sqrt_done, 1)

            def gain_hi(name):
                if name in BEFORE:
                    act.wait_ge(slab_half, 2 * (FIRST[BEFORE[name]] + COUNT[BEFORE[name]]))
                g, o = NORM_GAIN[name]
                src, hi = NORM_SRC[name][0], NORM_DST.get(name, (h_hi, h_lo))[0]
                for i in range(NORMT[name]):
                    act.wait_ge(*norm_source(name, i))
                    a(hi[:, i, :], src(i), ACT.Copy, scale=param(g, o + i)).then_inc(split_hi, 1)

            def memory_hi(layer, tiles):
                act.wait_ge(memn_done, 8)
                for i in tiles:
                    a(m_hi[:, i, :], memn[:, i, :], ACT.Copy, scale=param("norm_mem_g", 8 * layer + i)).then_inc(mem_hi, 1)

            def splits(stage):
                for s in range(COUNT[stage]):
                    split(FIRST[stage] + s + 1)

            for name in ROWS[1::2]:
                rows(act, name, rows_loaded[1])
            for i in range(DT):
                act.wait_ge(*norm_source("mix0", i))
                wait(act, mix_added, i - 2)
                a((sq[i % 2] if i else fb[0])[:, :], x[:, i, :], ACT.Square).then_inc(sq_done, 1)
            act.wait_ge(sum_done, 1)
            act.wait_ge(masks_ready, 6)
            a(rstd[:, :], stat[:, :], ACT.Sqrt, scale=1.0 / D, bias=eps[:, :]).then_inc(sqrt_done, 1)
            split(0)
            for i in range(DT):
                act.wait_ge(scaled, i + 1)
                a(h_hi[:, i, :], fb[i % 2][:, :], ACT.Copy).then_inc(split_hi, 1)
            act.wait_ge(pre_done, DT + 1)
            c0 = PROW["c_2"][1]
            a(c_silu[:, :], prm[:, 0, c0:c0 + DT], ACT.Silu).then_inc(csilu_done, 1)
            for s in range(6):
                n = FIRST["pc_in"] + s
                split(n + 1)
                if s in (0, 2):
                    for j in range(2):
                        act.wait_ge(slab_half, 2 * n + 1 + j)
                        if s:
                            act.wait_ge(tile_free, TILE0["pc_in"] + 4)
                        b = bank[(TILE0["pc_in"] + 2 * s + j) % 4]
                        a(sq[j][:, :], b[:, :], ACT.Sigmoid).then_inc(sig_done, 1)
                if s == 2:
                    root_of("mem")
                    act.wait_ge(poolw_loaded, 16)
                    a(pw_hi[:, :, :], pw_raw[:, :, :], ACT.Copy).then_inc(pwhi_done, 1)
                if s in (4, 5):
                    memory_hi(0, range(4 * (s - 4), 4 * (s - 3)))
            for s in range(8):
                split(FIRST["kv0"] + s + 1)
                if s in POOL_AT:
                    g = POOL_AT.index(s)
                    act.wait_ge(pooled_ready, g + 1)
                    a(pooled_hi[:, g, :], pooled[:, :], ACT.Copy).then_inc(poolhi_done, 1)
            for g in range(4):
                act.wait_ge(pool_out, g + 1)
                a(h_hi[:, g, :], bank[4 + g % 2][:, :], ACT.Copy, scale=param("pool_scale", g)).then_inc(ya_hi, 1)
            act.wait_ge(tile_free, TILE0["pc_in"] + 8)
            with act.Fori(0, COUNT["ada"] // 2) as it:
                for u in range(2):
                    hold(act, slab_half, 4 * it + 2 * (FIRST["ada"] + u + 1))
                    a(sq[u][0:1, 0:256], bank[4 + u][0:1, 0:256], ACT.Copy).then_inc(ada_copied, 1)
            split(FIRST["pc_out"])
            for i in range(4):
                act.wait_ge(xc_ready, i + 1)
                wait(act, xc_summed, i - 1)
                a(sq[i % 2][:, :], cv[:, i, :], ACT.Square).then_inc(xc_sq, 1)
            act.wait_ge(xc_summed, 4)
            a(rstd[:, :], stat[:, :], ACT.Sqrt, scale=1.0 / (4 * P), bias=eps[:, :]).then_inc(ln_sqrt, 1)
            for i in range(4):
                act.wait_ge(ln_norm, i + 1)
                a(cv[:, i, :], cv[:, i, :], ACT.Silu, scale=param("conv_ln_g", i),
                  bias=param("conv_ln_b", i)).then_inc(ln_silu, 1)
                act.wait_ge(ln_silu, i + 1)
                a(h_hi[:, 4 + i, :], cv[:, i, :], ACT.Copy).then_inc(yb_hi, 1)
            splits("pc_out")

            def cross(layer):
                gain_hi(f"xa{layer}")
                for s in range(4):
                    split(FIRST[f"wq{layer}"] + s + 1)
                    if s == 0:
                        root_of(f"xa{layer}")
                    elif layer:
                        memory_hi(1, ((0, 1, 2), (3, 4, 5), (6, 7))[s - 1])
                if layer:
                    splits("kv1")
                for h in range(XH + 1):
                    if h < XH:
                        for t in range(NB):
                            act.wait_ge(xmax_done, 2 * XH * layer + 2 * h + t // 2 + 1)
                            if h >= 2:
                                act.wait_ge(xt_ready, 8 * layer + 2 * (h - 1))
                            b = bank[4 + XA_AT[("S", h, t // 2)] % 4]
                            a(xp[:, h % 2, t, :], b[:, (t % 2) * MEM:(t % 2 + 1) * MEM], ACT.Exp,
                              bias=nmax[:, h % 2, t:t + 1], accum_out=rsum[:, h % 2, t:t + 1]).then_inc(xexp_done, 1)
                        act.wait_ge(xrinv_ready, XH * layer + h + 1)
                        for t in range(NB):
                            v = xp[:, h % 2, t, :]
                            a(v, v, ACT.Copy, scale=rinv[:, h % 2, t:t + 1]).then_inc(xp_ready, 1)
                    if h:
                        for d in range(2):
                            act.wait_ge(xo_ready, 8 * layer + 2 * (h - 1) + d + 1)
                            b = bank[4 + XA_AT[("O", h - 1, d)] % 4]
                            a(h_hi[:, 2 * (h - 1) + d, :], b[:, :], ACT.Copy).then_inc(xo_hi, 1)
                splits(f"wo{layer}")
                gain_hi(f"ffn{layer}")
                up, down = f"up{layer}", f"down{layer}"
                n, tile = FIRST[up], TILE0[up]

                def up_step(it, first=False):
                    done = 2 * it + FT * layer
                    split(n + 1, 2 * it)
                    if first:
                        root_of(f"ffn{layer}")
                    for j in range(2):
                        hold(act, tile_free, 4 * it + (tile + j + 1))
                        hold(act, g_lo_done, done + (j - 1))
                        a(fb[j][:, :], sq[j][:, :], ACT.Identity, scale=tap(layer, 2, j, 2 * it),
                          bias=conv_bias(layer, j, 2 * it)).then_inc(tap2, 1)
                    for j in range(2):
                        hold(act, taps_done, done + (j + 1))
                        a(fb[j][:, :], fb[j][:, :], ACT.Silu).then_inc(gate_silu, 1)
                    split(n + 2, 2 * it)
                    for j in range(2):
                        hold(act, tile_free, 4 * it + (tile + 2 + j + 1))
                        a(g_hi[:, bass.ds(2 * it + j, 1), :].rearrange("p a t -> p (a t)"), fb[j][:, :],
                          ACT.Copy).then_inc(g_hi_done, 1)

                up_step(0, first=True)
                with act.Fori(1, COUNT[up] // 2) as it:
                    up_step(it)
                n = FIRST[down]
                with act.Fori(0, 2) as it:
                    for s in range(6):
                        split(n + s + 1, 6 * it)

            cross(0)
            gain_hi("mix1")
            act.dma_start(pos_i[64:96, :], ins["positions"].broadcast_to([32, T])).then_inc(pos_loaded, 16)
            for s in range(3):
                split(FIRST["dq"] + s + 1)
                if s == 0:
                    root_of("mix1")
            for i, (o, v) in enumerate(((r_sin, r_sin), (r_cos, r_cos))):
                act.wait_ge(angle_ready, i + 1)
                a(o[64:96, :], v[64:96, :], ACT.Sin).then_inc(sin_done, 1)
            gain_hi("ckv")
            split(FIRST["ukv"] + 1)
            root_of("ckv")
            gain_hi("cq")
            root_of("cq")
            split(FIRST["ukv"] + 2)
            act.wait_ge(k_rotated, 1)
            a(lk[64:96, :, :], kpe_raw[64:96, :].rearrange("p (a t) -> p a t", a=1).broadcast_to([32, MH, T]),
              ACT.Copy).then_inc(rope_ready, 1)
            split(FIRST["uq"] + 1)
            for h in range(MH + 1):
                if h < MH:
                    for i in range(NB):
                        act.wait_ge(lmax_done, 4 * h + i + 1)
                        if h >= 2:
                            act.wait_ge(lt_ready, 4 * (h - 1))
                        b = bank[4 + LQ_AT[("S", h, i)] % 3]
                        n = (i + 1) * P
                        a(lp[:, h % 2, QOFF[i]:QOFF[i] + n], b[:, 0:n], ACT.Exp, bias=nmax[:, h % 2, i:i + 1],
                          accum_out=rsum[:, h % 2, i:i + 1]).then_inc(lexp_done, 1)
                    if h % 2 == 0 and h // 2 + 2 <= MH // 2:
                        split(FIRST["uq"] + h // 2 + 2)
                    act.wait_ge(rinv_ready, h + 1)
                    for i in range(NB):
                        v = lp[:, h % 2, QOFF[i]:QOFF[i] + (i + 1) * P]
                        a(v, v, ACT.Copy, scale=rinv[:, h % 2, i:i + 1]).then_inc(lp_ready, 1)
                if h and h % 2 == 0:
                    act.wait_ge(lo_ready, h)
                    a(h_hi[:, h // 2 - 1, :], stat[:, :], ACT.Copy).then_inc(lo_hi, 1)
            splits("mla_o")
            cross(1)
            act.wait_ge(stat2_done, 1)
            a(fb[0][:, :], stat[:, :], ACT.Copy, scale=EPS / D, bias=EPS * EPS).then_inc(f_step, 1)
            act.wait_ge(v_ready, 1)
            a(rstd[:, :], fb[0][:, :], ACT.Sqrt).then_inc(f_step, 1)
            a(sq[0][:, :], stat[:, :], ACT.Sqrt, scale=1.0 / D, bias=eps[:, :]).then_inc(f_step, 1)
            for i in range(DT):
                act.wait_ge(scaled, DT + i + 1)
                a(h_hi[:, i, :], fb[i % 2][:, :], ACT.Identity, bias=mod[:, i:i + 1]).then_inc(split_hi, 1)
            for s in range(13):
                n = FIRST["w_in"] + s
                split(n + 1)
                if s in (6, 7, 11, 12):
                    for j in range(2):
                        act.wait_ge(tile_free, TILE0["w_in"] + 2 * s + j + 1)
                        g = (sg_T if s < 8 else wg_T)[:, 2 * ((s - 6) if s < 8 else (s - 11)) + j, :]
                        a(g, g, ACT.Silu).then_inc(gate_act, 1)
            chain = [0]
            def softplus_exp(h):
                for j in range(NB - 1, -1, -1):
                    act.wait_ge(abs_done, 4 * h + NB - j)
                    v = softplus[h % 2][:, j, j * P:]
                    a(v, v, ACT.Exp).then_inc(exp_done, 1)

            def softplus_log(h):
                for j in range(NB - 1, -1, -1):
                    act.wait_ge(exp_done, 4 * h + NB - j)
                    v = softplus[h % 2][:, j, j * P:]
                    a(v, v, ACT.Ln, bias=ones[:, 0:1]).then_inc(ln_done, 1)

            softplus_exp(0)
            softplus_log(0)
            for h in range(SBH):
                if h + 1 < SBH:
                    softplus_exp(h + 1)
                for j in range(NB - 1, -1, -1):
                    act.wait_ge(c_ready, 4 * h + NB - j)
                    wait(act, so_ready, h)
                    a(sw_T[:, j, j * P:], bank[4 * (h % 2) + j][:, 0:(NB - j) * P], ACT.Exp).then_inc(w_ready, 1)
                if h + 1 < SBH:
                    softplus_log(h + 1)
                act.wait_ge(so_scaled, h + 1)
                r0 = (h % 2) * HD
                a(h_hi[r0:r0 + HD, h // 2, :], fb[h % 2][r0:r0 + HD, :], ACT.Copy).then_inc(so_hi, 1)
            for h in range(SWH + 2):
                if h < SWH:
                    act.wait_ge(wmax_done, h + 1)
                    for q in range(NB):
                        c0 = P if q == 0 else 0
                        v = wp[:, h % 2, q, c0:]
                        a(v, v, ACT.Exp, bias=nmax[:, h % 2, q:q + 1],
                          accum_out=rsum[:, h % 2, q:q + 1]).then_inc(wexp_done, 1)
                    a(esink[:, h % 2, :], nmax[:, h % 2, :], ACT.Exp, bias=sinks[:, h:h + 1]).then_inc(wexp_done, 1)
                if h >= 2:
                    e = h - 2
                    r0 = (e % 2) * HD
                    act.wait_ge(wo_scaled, e + 1)
                    a(h_hi[r0:r0 + HD, 4 + e // 2, :], fb[e % 2][r0:r0 + HD, :], ACT.Copy).then_inc(wo_hi, 1)
                if h < SWH:
                    act.wait_ge(wrinv_ready, h + 1)
                    for q in range(NB):
                        v = wp[:, h % 2, q, P if q == 0 else 0:]
                        a(v, v, ACT.Copy, scale=rinv[:, h % 2, q:q + 1]).then_inc(wp_ready, 1)
            for s in range(4):
                split(FIRST["w_out"] + s + 1)
                for i in (2 * s - 2, 2 * s - 1) if s else ():
                    act.wait_ge(tile_free, TILE0["w_out"] + i + 1)
                    a(yT[:, i, :], x[:, i, :], ACT.Copy, scale=param("final_g_2", i)).then_inc(y_ready, 1)
            for i in (6, 7):
                act.wait_ge(tile_free, TILE0["w_out"] + i + 1)
                a(yT[:, i, :], x[:, i, :], ACT.Copy, scale=param("final_g_2", i)).then_inc(y_ready, 1)
            act.wait_ge(stat2_done, 3)
            a(kv_col[:, :], bank[7][:, 0:NB], ACT.Sqrt, scale=1.0 / D, bias=eps[:, :]).then_inc(col_sqrt, 1)
            act.wait_ge(col_ready, 1)
            for t in range(NB):
                act.wait_ge(out_tr, 2 * t + 1)
                a(out_nat[:, t, 0:512], bank[2 * t][:, :], ACT.Copy, scale=kv_col[:, t:t + 1]).then_inc(out_copied_a, 1)

        @block.vector
        def _(dve):
            tt, ts, stt, cp = nc.vector.tensor_tensor, nc.vector.tensor_scalar, nc.vector.scalar_tensor_tensor, \
                nc.vector.tensor_copy
            step = [0]

            def link(ins_):
                step[0] += 1
                ins_.then_inc(dve_step, 1)
                dve.wait_ge(dve_step, step[0])

            def low(lo_, v, hi):
                return tt(lo_, v, hi.bitcast(f32), SUB)

            def split(n, step_=0):
                if isinstance(step_, int) and (n + step_ >= NSLAB or is_ada(n + step_)):
                    return
                dve.wait_ge(hi_done, splits_before(n) + 1 + step_)
                c = slab_columns(n)
                low(w_lo[n % 2][:, 0:c], raw[n % 2][:, 0:c], w_hi[n % 2][:, 0:c]).then_inc(lo_done, 1)

            def splits(stage):
                for s in range(COUNT[stage]):
                    split(FIRST[stage] + s + 1)

            def root(name):
                dve.wait_ge(sqrt_done, NORMI[name] + 1)
                r = root_to(name)[:, 0:NORM_SRC[name][1]]
                link(nc.vector.reciprocal(r, r))

            def gain_low(name):
                g, o = NORM_GAIN[name]
                src, (hi, lo_) = NORM_SRC[name][0], NORM_DST.get(name, (h_hi, h_lo))
                for i in range(NORMT[name]):
                    dve.wait_ge(split_hi, SPLIT0[name] + i + 1)
                    stt(lo_[:, i, :], src(i), param(g, o + i), hi[:, i, :].bitcast(f32), MUL, SUB).then_inc(split_lo, 1)

            def memory_low(layer, tiles):
                for i in tiles:
                    dve.wait_ge(mem_hi, 8 * layer + i + 1)
                    stt(m_lo[:, i, :], memn[:, i, :], param("norm_mem_g", 8 * layer + i), m_hi[:, i, :].bitcast(f32),
                        MUL, SUB).then_inc(mem_lo, 1)

            def pre_copy(r):
                dve.wait_ge(pre_ready, r + 1)
                b = bank[4 + r % 4]
                if r < DT:
                    cp(x[:, r, :], b[:, :]).then_inc(pre_done, 1)
                elif r < 4 + DT:
                    cp(prm[:, r - DT, 0:PROWS[r - DT]], b[:, 0:PROWS[r - DT]]).then_inc(pre_done, 1)
                else:
                    cp(memn[:, r - 4 - DT, :], b[:, 0:MEM]).then_inc(pre_done, 1)

            for r in range(4 + DT):
                pre_copy(r)
                i = r - 3
                if 1 <= i < DT:
                    dve.wait_ge(sq_done, i + 1)
                    wait(dve, mix_added, i - 1)
                    tt(fb[0][:, :], fb[0][:, :], sq[i % 2][:, :], ADD).then_inc(mix_added, 1)
            dve.wait_ge(masks_ready, 5)
            cp(ident_b[:, :], ident[:, :])
            cp(later_b[:, :], later[:, :])
            root("mix0")
            split(0)
            for i in range(DT + 1):
                if i < DT:
                    wait(dve, split_lo, i - 1)
                    stt(fb[i % 2][:, :], x[:, i, :], param("norm_mix_g", i), rstd[:, :], MUL, MUL).then_inc(scaled, 1)
                if i:
                    dve.wait_ge(split_hi, i)
                    low(h_lo[:, i - 1, :], fb[(i - 1) % 2][:, :], h_hi[:, i - 1, :]).then_inc(split_lo, 1)

            CONV = [(k, i) for pair in ((0, 1), (2, 3)) for k in range(CK) for i in pair]
            conv_at, n_conv = {}, 0
            for k, i in CONV:
                if k < CK - 1:
                    n_conv += 1
                    conv_at[(k, i)] = n_conv
            todo = list(CONV)

            def conv(count):
                for _ in range(min(count, len(todo))):
                    k, i = todo.pop(0)
                    src, o, w = glu[:, i, k:k + T], cv[:, i, :], param("conv_dw_w", 4 * k + i)
                    if k == 0:
                        m = ts(o, src, w, param("conv_dw_b", i), MUL, ADD)
                    else:
                        dve.wait_ge(conv_step, conv_at[(k - 1, i)])
                        m = stt(o, src, w, o, MUL, ADD)
                    m.then_inc(cv_ready if k == CK - 1 else conv_step, 1)

            T0 = TILE0["pc_in"]
            for s in range(6):
                n = FIRST["pc_in"] + s
                split(n + 1)
                if s == 0:
                    for r in range(4 + DT, 4 + 2 * DT):
                        pre_copy(r)
                    dve.wait_ge(masks_ready, 5)
                    nc.vector.reciprocal(inv16[:, :], inv16[:, :]).then_inc(consts_done, 1)
                for j in range(2):
                    tile = 2 * s + j
                    b = bank[(T0 + tile) % 4]
                    if s in (1, 3):
                        dve.wait_ge(slab_half, 2 * n + 1 + j)
                        dve.wait_ge(sig_done, s + j)
                        if s == 1 and j == 0:
                            dve.wait_ge(pads_ready, 2)
                        tt(glu[:, s - 1 + j, CK - 1:], sq[j][:, :], b[:, :], MUL).then_inc(tile_free, 3 if j else 1)
                    elif s >= 4:
                        dve.wait_ge(slab_half, 2 * n + 1 + j)
                        cp(u_pad[:, 2 * (s - 4) + j, 16:], b[:, :]).then_inc(tile_free, 1)
                if s == 1:
                    dve.wait_ge(tile_free, T0 + 4)
                if s == 3:
                    dve.wait_ge(tile_free, T0 + 8)
                if s == 2:
                    root("mem")
                    for i in range(DT):
                        tt(memn[:, i, :], memn[:, i, :], rstd[:, 0:MEM], MUL).then_inc(memn_done, 1)
                    dve.wait_ge(pwhi_done, 1)
                    low(pw_lo[:, :, :], pw_raw[:, :, :], pw_hi[:, :, :]).then_inc(pwlo_done, 1)
                if s in (4, 5):
                    memory_low(0, range(4 * (s - 4), 4 * (s - 3)))
                conv([0, 0, 0, 9, 9, 8][s])

            def memory_out(layer, after=lambda s: None):
                stage = f"kv{layer}"
                for s in range(8):
                    n = FIRST[stage] + s
                    split(n + 1)
                    for j in range(2):
                        dve.wait_ge(slab_half, 2 * n + 1 + j)
                        b = bank[(TILE0[stage] + 2 * s + j) % 4][:, 0:256]
                        o = kT[:, 2 * s + j, :] if s < 4 else vN[:, j, (s - 4) * 256:(s - 3) * 256]
                        cp(o, b).then_inc(tile_free, 1)
                    after(s)

            def mixer_meanwhile(s):
                if s in POOL_AT:
                    g = POOL_AT.index(s)
                    dve.wait_ge(poolhi_done, g + 1)
                    low(pooled_lo[:, g, :], pooled[:, :], pooled_hi[:, g, :]).then_inc(poollo_done, 1)
                conv(3)

            memory_out(0, mixer_meanwhile)
            for g in range(4):
                dve.wait_ge(ya_hi, g + 1)
                stt(h_lo[:, g, :], bank[4 + g % 2][:, :], param("pool_scale", g), h_hi[:, g, :].bitcast(f32), MUL, SUB)\
                    .then_inc(y_lo, 1)
            conv(len(todo))
            dve.wait_ge(ada_cols, COUNT["ada"])
            tt(mod[:, :], bank[6][:, 0:24], prm[:, 1, 0:24], ADD).then_inc(mod_done, 1)
            dve.wait_ge(mod_done, 1)
            g0 = PROW["norm_g_2"][1]
            link(ts(gs2[:, :], mod[:, 8:16], 1.0, None, ADD))
            link(tt(gs2[:, :], gs2[:, :], prm[:, 0, g0:g0 + DT], MUL))
            g0 = PROW["final_norm_g"][1]
            link(tt(gs2[:, :], gs2[:, :], prm[:, 0, g0:g0 + DT], MUL))
            split(FIRST["pc_out"])
            dve.wait_ge(cv_summed, 4)
            for i in range(4):
                dve.wait_ge(cv_ready, i + 1)
                stt(cv[:, i, :], bank[6][:, :], -1.0 / (4 * P), cv[:, i, :], MUL, ADD).then_inc(xc_ready, 1)
            dve.wait_ge(ln_sqrt, 1)
            link(nc.vector.reciprocal(rstd[:, :], rstd[:, :]))
            for i in range(4):
                tt(cv[:, i, :], cv[:, i, :], rstd[:, :], MUL).then_inc(ln_norm, 1)
            for i in range(4):
                dve.wait_ge(yb_hi, i + 1)
                low(h_lo[:, 4 + i, :], cv[:, i, :], h_hi[:, 4 + i, :]).then_inc(y_lo, 1)

            def add_to_x(stage):
                for s in range(4):
                    n = FIRST[stage] + s
                    split(n + 1)
                    for j in range(2):
                        i = 2 * s + j
                        dve.wait_ge(slab_half, 2 * n + 1 + j)
                        tt(x[:, i, :], x[:, i, :], bank[(TILE0[stage] + i) % 4][:, :], ADD).then_inc(tile_free, 1)

            add_to_x("pc_out")

            def cross(layer):
                gain_low(f"xa{layer}")
                stage = f"wq{layer}"
                for s in range(4):
                    n = FIRST[stage] + s
                    split(n + 1)
                    if s == 0:
                        root(f"xa{layer}")
                    for j in range(2):
                        i = 2 * s + j
                        dve.wait_ge(slab_half, 2 * n + 1 + j)
                        stt(qT[:, i, :], bank[(TILE0[stage] + i) % 4][:, :], XHD ** -0.5, rstd[:, :], MUL, MUL)\
                            .then_inc(tile_free, 1)
                    if layer and s:
                        memory_low(1, ((0, 1, 2), (3, 4, 5), (6, 7))[s - 1])
                if layer:
                    memory_out(1)
                for h in range(XH + 1):
                    e = h - 1
                    if h < XH:
                        for i in range(2):
                            dve.wait_ge(xs_ready, 8 * layer + 2 * h + i + 1)
                            b = bank[4 + XA_AT[("S", h, i)] % 4]
                            nc.vector.tensor_reduce(nmax[:, h % 2, 2 * i:2 * i + 2],
                                                    b[:, :].rearrange("p (a m) -> p a m", a=2), AX.X, MAX,
                                                    negate=True).then_inc(xmax_done, 1)
                    if h:
                        for j in range(2):
                            dve.wait_ge(xt_ready, 8 * layer + 2 * e + j + 1)
                            wait(dve, xo_ready, 8 * layer + 2 * (e - 1) if e >= 2 else 0)
                            cp(xpT[:, e % 2, j, :], bank[4 + XA_AT[("T", e, j)] % 4][:, :]).then_inc(xt_done, 1)
                    if h < XH:
                        dve.wait_ge(xexp_done, 16 * layer + 4 * h + 4)
                        wait(dve, xp_ready, 16 * layer + 4 * (h - 1) if h >= 2 else 0)
                        nc.vector.reciprocal(rinv[:, h % 2, :], rsum[:, h % 2, :]).then_inc(xrinv_ready, 1)
                    if h:
                        for d in range(2):
                            i = 2 * e + d
                            dve.wait_ge(xo_hi, 8 * layer + i + 1)
                            low(h_lo[:, i, :], bank[4 + XA_AT[("O", e, d)] % 4][:, :], h_hi[:, i, :]).then_inc(xo_lo, 1)
                add_to_x(f"wo{layer}")
                gain_low(f"ffn{layer}")
                up, down = f"up{layer}", f"down{layer}"
                n, tile = FIRST[up], TILE0[up]

                def up_step(it, first=False):
                    done = 2 * it + FT * layer
                    split(n + 1, 2 * it)
                    if first:
                        root(f"ffn{layer}")
                    for j in range(2):
                        hold(dve, taps_done, done + (j - 1))
                        dve.wait_ge(slab_half, 4 * it + (2 * n + 1 + j))
                        tt(sq[j][:, :], bank[(tile + j) % 4][:, :], rstd[:, :], MUL).then_inc(tile_free, 1)
                    for j in range(2):
                        dve.wait_ge(tap2, done + (j + 1))
                        stt(fb[j][:, 1:], sq[j][:, :T - 1], tap(layer, 1, j, 2 * it), fb[j][:, 1:], MUL, ADD).then_inc(tap1, 1)
                        dve.wait_ge(tap1, done + (j + 1))
                        stt(fb[j][:, 2:], sq[j][:, :T - 2], tap(layer, 0, j, 2 * it), fb[j][:, 2:], MUL, ADD)\
                            .then_inc(taps_done, 1)
                    split(n + 2, 2 * it)
                    for j in range(2):
                        dve.wait_ge(gate_silu, done + (j + 1))
                        tt(fb[j][:, :], fb[j][:, :], rstd[:, :], MUL).then_inc(silu_scaled, 1)
                    for j in range(2):
                        hold(dve, silu_scaled, done + (j + 1))
                        dve.wait_ge(slab_half, 4 * it + (2 * n + 3 + j))
                        tt(fb[j][:, :], fb[j][:, :], bank[(tile + 2 + j) % 4][:, :], MUL).then_inc(tile_free, 1)
                    for j in range(2):
                        dve.wait_ge(g_hi_done, done + (j + 1))
                        i = bass.ds(2 * it + j, 1)
                        low(g_lo[:, i, :].rearrange("p a t -> p (a t)"), fb[j][:, :],
                            g_hi[:, i, :].rearrange("p a t -> p (a t)")).then_inc(g_lo_done, 1)

                up_step(0, first=True)
                with dve.Fori(1, COUNT[up] // 2) as it:
                    up_step(it)
                if layer:
                    dve.wait_ge(taps_done, 2 * FT)
                    dve.wait_ge(g_lo_done, 2 * FT)
                    nc.vector.memset(sq[0][:, :], 0.0).then_inc(fsq_done, 1)
                    nc.vector.memset(sq[1][:, :], 0.0).then_inc(fsq_done, 1)
                    g0 = PROW["final_norm_g"][1]
                    g = prm[:, 0, g0:g0 + DT]
                    tt(gf_sq[:, :], g, g, MUL).then_inc(fsq_done, 1)
                n, tile = FIRST[down], TILE0[down]
                with dve.Fori(0, 2) as it:
                    for s in range(6):
                        split(n + s + 1, 6 * it)
                        if s % 3 == 2:
                            for j in range(2):
                                i = 2 * (s // 3) + j
                                dve.wait_ge(slab_half, 12 * it + (2 * (n + s) + 1 + j))
                                v = x[:, bass.ds(4 * it + i, 1), :].rearrange("p a t -> p (a t)")
                                tt(v, v, bank[(tile + i) % 4][:, :], ADD).then_inc(tile_free, 1)
                                if layer == 0:
                                    continue
                                dve.wait_ge(tile_free, 4 * it + (tile + i + 1))
                                hold(dve, fsq_done, 12 * it + (3 * i + 3))
                                tt(fb[0][:, :], v, v, MUL).then_inc(fsq_done, 1)
                                hold(dve, fsq_done, 12 * it + (3 * i + 4))
                                tt(sq[0][:, :], sq[0][:, :], fb[0][:, :], ADD).then_inc(fsq_done, 1)
                                stt(sq[1][:, :], fb[0][:, :], gf_sq[:, bass.ds(4 * it + i, 1)], sq[1][:, :], MUL, ADD)\
                                    .then_inc(fsq_done, 1)

            cross(0)

            gain_low("mix1")
            rr = slice(64, 96)
            s_, c_, t_ = r_sin[rr, :], r_cos[rr, :], fb[0][rr, :]

            def angles():
                dve.wait_ge(pos_loaded, 16)
                dve.wait_ge(small_loaded, 32)
                link(cp(s_, pos_i[rr, :]))
                link(ts(c_, s_, rope_c[rr, 0:1], None, MUL))

            def reduce(o, shift):
                link(ts(t_, c_, 1.0 / TWO_PI, shift, MUL, ADD))
                link(ts(t_, t_, ROUNDER, None, ADD))
                link(ts(t_, t_, -ROUNDER, None, ADD))
                link(stt(o, t_, -PI2_A, c_, MUL, ADD))
                link(stt(o, t_, -PI2_B, o, MUL, ADD))
                link(stt(o, t_, -PI2_C, o, MUL, ADD))
                link(ts(o, o, shift * TWO_PI, 3.1415925, ADD, ALU.min))
                ts(o, o, -3.1415925, None, MAX).then_inc(angle_ready, 1)
                dve.wait_ge(angle_ready, 1 if shift == 0.0 else 2)

            T0 = TILE0["dq"]
            for s in range(3):
                n = FIRST["dq"] + s
                split(n + 1)
                if s == 0:
                    root("mix1")
                for j in range(2):
                    i = DQ_TILES[2 * s + j]
                    dve.wait_ge(slab_half, 2 * n + 1 + j)
                    b = bank[(T0 + 2 * s + j) % 4]
                    if i < 3:
                        tt(cq_raw[:, i, :], b[:, :], rstd[:, :], MUL).then_inc(tile_free, 1)
                    elif i < 5:
                        tt(ckv_raw[:, i - 3, :], b[:, :], rstd[:, :], MUL).then_inc(tile_free, 1)
                    else:
                        tt(kpe_raw[rr, :], b[rr, :], rstd[rr, :], MUL).then_inc(tile_free, 1)
                if s == 0:
                    angles()
                    reduce(s_, 0.0)
                if s == 1:
                    reduce(c_, 0.25)
            gain_low("ckv")
            def rotate_keys():
                dve.wait_ge(sin_done, 2)
                dve.wait_ge(tile_free, T0 + 6)
                k_ = kpe_raw[rr, :]
                link(ts(s_, s_, rope_c[rr, 1:2], None, MUL))
                link(nc.vector.stream_shuffle(t_, k_, swap))
                link(tt(t_, t_, s_, MUL))
                link(tt(k_, k_, c_, MUL))
                tt(k_, k_, t_, ADD).then_inc(k_rotated, 1)

            swap = list(range(16, 32)) + list(range(16))
            for s in range(2):
                n = FIRST["ukv"] + s
                split(n + 1)
                if s == 0:
                    root("ckv")
                    link(nc.vector.reciprocal(kv_col[:, :], kv_col[:, :]))
                for i in range(12):
                    if s and i == 4:
                        rotate_keys()
                    if s and i == 9:
                        root("cq")
                    if i < 11:
                        dve.wait_ge(kv_tile, 11 * s + i + 1)
                    else:
                        dve.wait_ge(slab_half, 2 * n + 2)
                    b = bank[(TILE0["ukv"] + 12 * s + i) % 4]
                    if i < 8:
                        tt(lk[0:NOPE, 8 * s + i, :], b[0:NOPE, :], fb[1][0:NOPE, :], MUL).then_inc(tile_free, 1)
                    else:
                        ts(lv[:, i - 8, 512 * s:512 * s + 512], b[:, :], kv_col[:, i - 8:i - 7], None, MUL)\
                            .then_inc(tile_free, 1)
                if s == 0:
                    gain_low("cq")
            split(FIRST["uq"] + 1)

            def queries(h):
                dve.wait_ge(slab_half, 2 * FIRST["uq"] + h + 1)
                wait(dve, ls_ready, 4 * (h - 3))
                stt(lq[0:QKD, h % 4, :], bank[(TILE0["uq"] + h) % 4][0:QKD, :], MLA_SCALE, rstd[0:QKD, :], MUL, MUL)\
                    .then_inc(tile_free, 1)
                dve.wait_ge(tile_free, TILE0["uq"] + h + 1)
                wait(dve, q_ready, h - 1)
                nc.vector.stream_shuffle(lsh[h % 2][rr, :], lq[rr, h % 4, :], swap).then_inc(q_base, 1)

            queries(0)
            queries(1)
            for h in range(MH + 1):
                e = h - 1
                if h < MH:
                    for i in range(NB):
                        dve.wait_ge(ls_ready, 4 * h + i + 1)
                        nc.vector.tensor_reduce(nmax[:, h % 2, i:i + 1], bank[4 + LQ_AT[("S", h, i)] % 3][:, 0:(i + 1) * P],
                                                AX.X, MAX, negate=True).then_inc(lmax_done, 1)
                    dve.wait_ge(lexp_done, 4 * h + 4)
                    wait(dve, lp_ready, 4 * (h - 1))
                    nc.vector.reciprocal(rinv[:, h % 2, :], rsum[:, h % 2, :]).then_inc(rinv_ready, 1)
                    if h % 2 == 0 and h // 2 + 2 <= MH // 2:
                        split(FIRST["uq"] + h // 2 + 2)
                    if h % 2 == 0 and h + 2 < MH:
                        queries(h + 2)
                if h:
                    for j in range(NB):
                        dve.wait_ge(lt_ready, 4 * e + j + 1)
                        wait(dve, lo_ready, e)
                        n = (NB - j) * P
                        cp(lpT[:, KOFF[j]:KOFF[j] + n], bank[4 + LQ_AT[("T", e, j)] % 3][:, 0:n]).then_inc(lt_done, 1)
                    if e % 2:
                        dve.wait_ge(lo_hi, e // 2 + 1)
                        low(h_lo[:, e // 2, :], stat[:, :], h_hi[:, e // 2, :]).then_inc(lo_lo, 1)
                if h % 2 and h + 2 < MH:
                    queries(h + 2)
            add_to_x("mla_o")
            cross(1)
            dve.wait_ge(stat2_done, 2)
            dve.wait_ge(f_step, 1)
            stt(fb[0][:, :], bank[6][:, :], 1.0 / D, fb[0][:, :], MUL, ADD).then_inc(v_ready, 1)
            dve.wait_ge(f_step, 2)
            link(nc.vector.reciprocal(rstd[:, :], rstd[:, :]))
            for i in range(DT + 1):
                if i < DT:
                    wait(dve, split_lo, SPLIT0["second"] + max(i - 1, 0))
                    stt(fb[i % 2][:, :], x[:, i, :], gs2[:, i:i + 1], rstd[:, :], MUL, MUL).then_inc(scaled, 1)
                if i:
                    dve.wait_ge(split_hi, SPLIT0["second"] + i)
                    stt(h_lo[:, i - 1, :], fb[(i - 1) % 2][:, :], mod[:, i - 1:i], h_hi[:, i - 1, :].bitcast(f32),
                        ADD, SUB).then_inc(split_lo, 1)
            split(FIRST["w_in"] + 1)
            dve.wait_ge(f_step, 3)
            link(nc.vector.reciprocal(sq[0][:, :], sq[0][:, :]))
            for i in range(DT):
                stt(x[:, i, :], x[:, i, :], param("final_norm_g", i), sq[0][:, :], MUL, MUL).then_inc(fin_done, 1)

            for s in range(13):
                n = FIRST["w_in"] + s
                if s:
                    split(n + 1)
                for j in range(2):
                    b = bank[(TILE0["w_in"] + 2 * s + j) % 4]
                    dve.wait_ge(slab_half, 2 * n + 1 + j)
                    i = 2 * s + j
                    if s < 2:
                        m = ts(sq_T[:, i, :], b[:, :], HSCALE, None, MUL)
                    elif s < 4:
                        m = cp(sk_T[:, i - 4, :], b[:, :])
                    elif s < 6:
                        m = cp(sv_N[:, 2 * j:2 * j + 2, (s - 4) * 256:(s - 3) * 256],
                               b[:, :].rearrange("p (a n) -> p a n", a=2))
                    elif s < 8:
                        m = cp(sg_T[:, i - 12, :], b[:, :])
                    elif s < 10:
                        m = ts(wq_T[:, i - 16, :], b[:, :], HSCALE, None, MUL)
                    elif i == 20:
                        cp(wk_T[0:HD, 0, :], b[0:HD, :])
                        m = cp(wk_T[HD:, 1, :], b[HD:, :])
                    elif i == 21:
                        m = cp(wv_N[:, :, :], b[:, :].rearrange("p (a n) -> p a n", a=NB))
                    else:
                        m = cp(wg_T[:, i - 22, :], b[:, :])
                    m.then_inc(tile_free, 1)

            dve.wait_ge(sb_masks, 5)
            dve.wait_ge(gate_act, 4)
            def negated_size(h):
                for j in range(NB - 1, -1, -1):
                    v, z = softplus[h % 2][:, j, j * P:], bank[4 * (h % 2) + j][:, 0:(NB - j) * P]
                    dve.wait_ge(z_ready, 4 * h + NB - j)
                    wait(dve, c_ready, 4 * (h - 1))
                    link(ts(v, z, -1.0, None, MUL))
                    tt(v, v, z, ALU.min).then_inc(abs_done, 1)

            def softplus_sum(h):
                for j in range(NB - 1, -1, -1):
                    v = softplus[h % 2][:, j, j * P:]
                    dve.wait_ge(ln_done, 4 * h + NB - j)
                    link(stt(v, bank[4 * (h % 2) + j][:, 0:(NB - j) * P], 0.0, v, MAX, ADD))
                    tt(v[:, 0:P], v[:, 0:P], before[:, :], MUL).then_inc(sp_ready, 1)

            negated_size(0)
            softplus_sum(0)
            for h in range(SBH):
                if h + 1 < SBH:
                    negated_size(h + 1)
                r0 = (h % 2) * HD
                dve.wait_ge(so_ready, h + 1)
                o = fb[h % 2][r0:r0 + HD, :]
                tt(o, bank[4 * (h % 2) + 3][r0:r0 + HD, :], sg_T[r0:r0 + HD, h // 2, :], MUL).then_inc(so_scaled, 1)
                if h + 1 < SBH:
                    softplus_sum(h + 1)
                dve.wait_ge(so_hi, h + 1)
                low(h_lo[r0:r0 + HD, h // 2, :], o, h_hi[r0:r0 + HD, h // 2, :]).then_inc(so_lo, 1)

            for b in range(2):
                link(nc.vector.memset(wp[:, b, 0, 0:P], NEG))
            dve.wait_ge(gate_act, 8)
            for h in range(SWH + 2):
                if h < SWH:
                    slope = 2.0 ** (-8.0 * (h + 1) / SWH)
                    for q in range(NB):
                        c0 = P if q == 0 else 0
                        dve.wait_ge(ws_ready, 2 * h + q // 2 + 1)
                        wait(dve, wt_ready, 2 * (h - 1) if h >= 2 else 0)
                        b = bank[4 + SW_AT[("S", h, q // 2)] % 4]
                        stt(wp[:, h % 2, q, c0:], relm[:, c0:], -slope, b[:, (q % 2) * 2 * P + c0:(q % 2 + 1) * 2 * P],
                            MUL, ADD).then_inc(wl_done, 1)
                    dve.wait_ge(wl_done, 4 * h + 4)
                    link(nc.vector.tensor_reduce(nmax[:, h % 2, :], wp[:, h % 2, :, :], AX.X, MAX))
                    ts(nmax[:, h % 2, :], nmax[:, h % 2, :], sinks[:, h:h + 1], -1.0, MAX, MUL).then_inc(wmax_done, 1)
                if h >= 2:
                    e = h - 2
                    r0 = (e % 2) * HD
                    dve.wait_ge(wo_ready, e + 1)
                    o = fb[e % 2][r0:r0 + HD, :]
                    tt(o, bank[4 + SW_AT[("O", e, 0)] % 4][r0:r0 + HD, :], wg_T[r0:r0 + HD, e // 2, :], MUL)\
                        .then_inc(wo_scaled, 1)
                if 1 <= h <= SWH:
                    e = h - 1
                    flat = wpT[:, :, :].rearrange("p a n -> p (a n)")
                    for b in range(2):
                        dve.wait_ge(wt_ready, 2 * e + b + 1)
                        wait(dve, wo_ready, e)
                        n = 4 * P - b * P
                        cp(flat[:, b * 512:b * 512 + n], bank[4 + SW_AT[("T", e, b)] % 4][:, 0:n]).then_inc(wt_done, 1)
                if h < SWH:
                    dve.wait_ge(wexp_done, 5 * h + 5)
                    link(tt(rsum[:, h % 2, :], rsum[:, h % 2, :], esink[:, h % 2, :], ADD))
                    wait(dve, wp_ready, 4 * (h - 1) if h >= 2 else 0)
                    nc.vector.reciprocal(rinv[:, h % 2, :], rsum[:, h % 2, :]).then_inc(wrinv_ready, 1)
                if h >= 2:
                    e = h - 2
                    r0 = (e % 2) * HD
                    dve.wait_ge(wo_hi, e + 1)
                    low(h_lo[r0:r0 + HD, 4 + e // 2, :], fb[e % 2][r0:r0 + HD, :], h_hi[r0:r0 + HD, 4 + e // 2, :])\
                        .then_inc(wo_lo, 1)
            for s in range(4):
                n = FIRST["w_out"] + s
                split(n + 1)
                for j in range(2):
                    i = 2 * s + j
                    dve.wait_ge(slab_half, 2 * n + 1 + j)
                    if i == 0:
                        dve.wait_ge(fin_done, DT)
                    stt(x[:, i, :], bank[(TILE0["w_out"] + i) % 4][:, :], mod[:, 16 + i:17 + i], x[:, i, :], MUL, ADD)\
                        .then_inc(tile_free, 1)
                    dve.wait_ge(tile_free, TILE0["w_out"] + i + 1)
                    if i == 0:
                        link(tt(sq[0][:, :], x[:, i, :], x[:, i, :], MUL))
                        continue
                    link(tt(sq[1][:, :], x[:, i, :], x[:, i, :], MUL))
                    m = tt(sq[0][:, :], sq[0][:, :], sq[1][:, :], ADD)
                    if i < DT - 1:
                        link(m)
                    else:
                        m.then_inc(fsum_ready, 1)
            dve.wait_ge(col_sqrt, 1)
            nc.vector.reciprocal(kv_col[:, :], kv_col[:, :]).then_inc(col_ready, 1)
            dve.wait_ge(col_ready, 1)
            for t in range(NB):
                dve.wait_ge(out_tr, 2 * t + 2)
                ts(out_nat[:, t, 512:], bank[2 * t + 1][:, :], kv_col[:, t:t + 1], None, MUL).then_inc(out_copied, 1)


_INS = ["x", "mem", "positions", "norm_mix_g", "norm_xa_g", "norm_mem_g", "xa_wq", "xa_wkv", "xa_wo", "norm_ffn_g",
        "ffn_w_up", "ffn_conv_w", "ffn_conv_b", "ffn_w_down", "pc_w_in", "pool_w", "pool_scale", "conv_dw_w",
        "conv_dw_b", "conv_ln_g", "conv_ln_b", "pc_w_out", "mla_w_dq_dkv", "mla_q_norm_g", "mla_w_uq",
        "mla_kv_norm_g", "mla_w_ukv", "mla_w_o", "final_norm_g", "c_2", "w_ada_2", "b_ada_2", "norm_g_2", "w_in_2",
        "sinks_2", "w_out_2", "final_g_2"]


def kernel(**inputs):
    import numpy as _np
    import concourse.bacc as _bacc
    from concourse import mybir as _mybir
    from concourse.bass_utils import run_bass_kernel_spmd as _run

    nc = _bacc.Bacc("TRN2", target_bir_lowering=False, num_devices=1)
    arrays, args = {}, {}
    given = {name: _np.ascontiguousarray(inputs[name]) for name in _INS}
    half = ROPE // 2
    freq = 1.0 / 10000.0 ** (_np.arange(0, ROPE, 2, dtype=_np.float64) / ROPE)
    given["rope_const"] = _np.stack([_np.tile(freq, 2), _np.repeat([-1.0, 1.0], half)], 1).astype(_np.float32)
    for name, a in given.items():
        arrays[f"in_{name}_dram"] = a
        args[name] = nc.dram_tensor(f"in_{name}_dram", a.shape, _mybir.dt.from_np(a.dtype), kind="ExternalInput").ap()
    out = nc.dram_tensor("out_0_dram", (1, T, D), _mybir.dt.float32, kind="ExternalOutput").ap()
    build(nc, args, out)
    r = _run(nc, [arrays], core_ids=[0])
    return r.results[0]["out_0_dram"]
```
